# Optimizing a Trainium2 kernel written in Bass

```python
import jax, jax.numpy as jnp
from jax import lax
import numpy as np

D_MODEL = 1024
BATCH = 1
SEQ = 1024
DEPTH = 1
DEC_BATCH = 8
DEC_SEQ = 4
PAST_LEN = 1024
PAGE_SIZE = 128

HEAD_DIM = 64
CONV_CH = D_MODEL // 4
CONV_WIDTH = 31
RWKV_HEADS = (3 * D_MODEL // 8) // HEAD_DIM
RWKV_DIM = RWKV_HEADS * HEAD_DIM
ATT_HEADS = (D_MODEL - CONV_CH - RWKV_DIM) // HEAD_DIM
ATT_DIM = ATT_HEADS * HEAD_DIM
MIX_DIM = CONV_CH + RWKV_DIM + ATT_DIM
DECAY_LORA = 64
AAA_LORA = 64
GATE_LORA = 128
CONV_COLS = 2 * CONV_CH
RWKV_COLS = 3 * RWKV_DIM + DECAY_LORA + AAA_LORA + GATE_LORA
ATT_COLS = 3 * ATT_DIM
IN_COLS = CONV_COLS + RWKV_COLS + ATT_COLS
ATT_BLOCK = 128
ATT_BIAS_INIT = -8.0
PEER_HEADS = 8
PEER_DK = 256
N_KEYS = 128
N_EXPERTS = N_KEYS * N_KEYS
PEER_TOPK = 16
PEER_BLOCK = 128
RMS_EPS = 1e-5
LN_EPS = 1e-5
GN_EPS = 64e-5

kernel_name = 'hymba_conv_rwkv7_stickbreak_peer_step'

def rmsnorm(x, g):
    xf = x.astype(jnp.float32)
    y = xf * lax.rsqrt(jnp.mean(xf * xf, axis=-1, keepdims=True) + RMS_EPS)
    return (y * g.astype(jnp.float32)).astype(x.dtype)

def layernorm_f32(x, g, b, eps):
    xf = x.astype(jnp.float32)
    mu = jnp.mean(xf, axis=-1, keepdims=True)
    var = jnp.mean(jnp.square(xf - mu), axis=-1, keepdims=True)
    return (xf - mu) * lax.rsqrt(var + eps) * g.astype(jnp.float32) + b.astype(jnp.float32)

def conv_mixer(p, buf, conv_w, conv_b, ln_g, ln_b):
    glu = p[..., :CONV_CH] * jax.nn.sigmoid(p[..., CONV_CH:])
    ext = jnp.concatenate([buf.astype(glu.dtype), glu], axis=1)
    y = lax.conv_general_dilated(ext, conv_w[:, None, :].astype(glu.dtype), window_strides=(1,),
                                 padding='VALID', dimension_numbers=('NWC', 'WIO', 'NWC'),
                                 feature_group_count=CONV_CH)
    y = layernorm_f32(y + conv_b, ln_g, ln_b, LN_EPS)
    y = y * jax.nn.sigmoid(y)
    return y.astype(p.dtype), ext[:, -(CONV_WIDTH - 1):]

def _wkv_step(S, inp):
    r, w, k, v, kk, b = inp
    sa = jnp.einsum('bhvk,bhk->bhv', S, kk)
    S = S * w[:, :, None, :] - sa[..., None] * b[:, :, None, :] + v[..., None] * k[:, :, None, :]
    return S, jnp.einsum('bhvk,bhk->bhv', S, r)

def rwkv_mixer(p, shift_prev, wkv0, mu, w0, w_up, a0, a_up, g_up, k_k, k_a, r_k, ln_g, ln_b):
    B, T, _ = p.shape
    f32 = jnp.float32
    pf = p.astype(f32)
    prev = jnp.concatenate([shift_prev.astype(f32)[:, None, :], pf[:, :-1]], axis=1)
    pm = pf + (prev - pf) * mu.astype(f32)
    o = [0, RWKV_DIM, 2 * RWKV_DIM, 3 * RWKV_DIM, 3 * RWKV_DIM + DECAY_LORA,
         3 * RWKV_DIM + DECAY_LORA + AAA_LORA, RWKV_COLS]
    r, k, v, xw, xa, xg = [pm[..., o[i]:o[i + 1]] for i in range(6)]
    w_log = -jax.nn.softplus(-(w0.astype(f32) + jnp.tanh(xw) @ w_up.astype(f32))) - 0.5
    decay = jnp.exp(-jnp.exp(w_log))
    a = jax.nn.sigmoid(a0.astype(f32) + xa @ a_up.astype(f32))
    g = jax.nn.sigmoid(xg) @ g_up.astype(f32)
    kk = k * k_k.astype(f32)
    k = k * (1.0 + (a - 1.0) * k_a.astype(f32))
    hs = lambda t: t.reshape(B, T, RWKV_HEADS, HEAD_DIM)
    r, k, v, decay, a, kk = hs(r), hs(k), hs(v), hs(decay), hs(a), hs(kk)
    kk = kk / jnp.maximum(jnp.sqrt(jnp.sum(kk * kk, axis=-1, keepdims=True)), 1e-12)
    xs = tuple(jnp.moveaxis(t, 1, 0) for t in (r, decay, k, v, kk, kk * a))
    S, ys = lax.scan(_wkv_step, wkv0.astype(f32), xs)
    y = jnp.moveaxis(ys, 0, 1)
    ym = jnp.mean(y, axis=-1, keepdims=True)
    yv = jnp.mean(jnp.square(y - ym), axis=-1, keepdims=True)
    yn = (y - ym) * lax.rsqrt(yv + GN_EPS)
    yn = yn * ln_g.astype(f32).reshape(RWKV_HEADS, HEAD_DIM) + ln_b.astype(f32).reshape(RWKV_HEADS, HEAD_DIM)
    bonus = jnp.sum(r * k * r_k.astype(f32), axis=-1, keepdims=True) * v
    out = (yn + bonus).reshape(B, T, RWKV_DIM) * g
    return out.astype(p.dtype), p[:, -1], S

def sb_block(q, k, v, q_pos, k_pos, bias):
    z = jnp.einsum('bqhd,bkhd->bhqk', q, k).astype(jnp.float32) * (HEAD_DIM ** -0.5)
    z = z + bias.astype(jnp.float32)[None, :, None, None]
    causal = k_pos[None, :] < q_pos[:, None]
    log_rest = jnp.where(causal, jax.nn.log_sigmoid(-z), 0.0)
    rest_after = lax.cumsum(log_rest, axis=3, reverse=True) - log_rest
    a = jnp.where(causal, jnp.exp(jax.nn.log_sigmoid(z) + rest_after), 0.0)
    return jnp.einsum('bhqk,bkhd->bqhd', a.astype(v.dtype), v)

def sb_attention(q, k, v, past_len, bias):
    B, T, H, Dh = q.shape
    k_pos = jnp.arange(k.shape[1])
    q_pos = past_len + jnp.arange(T)
    if T > ATT_BLOCK and T % ATT_BLOCK == 0:
        nb = T // ATT_BLOCK
        qb = jnp.moveaxis(q.reshape(B, nb, ATT_BLOCK, H, Dh), 1, 0)
        pb = q_pos.reshape(nb, ATT_BLOCK)
        ob = lax.map(lambda qp: sb_block(qp[0], k, v, qp[1], k_pos, bias), (qb, pb))
        return jnp.moveaxis(ob, 0, 1).reshape(B, T, H, Dh)
    return sb_block(q, k, v, q_pos, k_pos, bias)

def peer_block(xb, w_query, sub_keys, u_tab, v_tab):
    T = xb.shape[0]
    q = (xb @ w_query).reshape(T, PEER_HEADS, 2, PEER_DK // 2)
    s = jnp.einsum('thcd,hcnd->thcn', q, sub_keys).astype(jnp.float32)
    s1, i1 = lax.top_k(s[:, :, 0], PEER_TOPK)
    s2, i2 = lax.top_k(s[:, :, 1], PEER_TOPK)
    cand_s = (s1[..., :, None] + s2[..., None, :]).reshape(T, PEER_HEADS, PEER_TOPK * PEER_TOPK)
    cand_i = (i1[..., :, None] * N_KEYS + i2[..., None, :]).reshape(T, PEER_HEADS, PEER_TOPK * PEER_TOPK)
    top_s, pos = lax.top_k(cand_s, PEER_TOPK)
    e = jnp.take_along_axis(cand_i, pos, axis=-1)
    gate = jax.nn.softmax(top_s, axis=-1)
    act = jax.nn.gelu(jnp.einsum('thkd,td->thk', u_tab[e], xb).astype(jnp.float32))
    return jnp.einsum('thk,thkd->td', (gate * act).astype(xb.dtype), v_tab[e])

def peer(x, w_query, sub_keys, u_tab, v_tab):
    n, d = x.shape
    pad = (-n) % PEER_BLOCK
    xp = jnp.pad(x, ((0, pad), (0, 0))).reshape(-1, PEER_BLOCK, d)
    yb = lax.map(lambda xb: peer_block(xb, w_query, sub_keys, u_tab, v_tab), xp)
    return yb.reshape(-1, d)[:n]

def trunk_layer(x, conv_buf, shift_prev, wkv_state, k_past, v_past, past_len,
                norm1_g, w_in, conv_w, conv_b, conv_ln_g, conv_ln_b,
                rwkv_mu, rwkv_w0, rwkv_w_up, rwkv_a0, rwkv_a_up, rwkv_g_up,
                rwkv_k_k, rwkv_k_a, rwkv_r_k, rwkv_ln_g, rwkv_ln_b, att_bias,
                w_out, norm2_g, peer_w_query, peer_sub_keys, peer_u, peer_v):
    B, T, D = x.shape
    h = rmsnorm(x, norm1_g)
    p = h @ w_in
    p_conv = p[..., :CONV_COLS]
    p_rwkv = p[..., CONV_COLS:CONV_COLS + RWKV_COLS]
    p_att = p[..., CONV_COLS + RWKV_COLS:]
    y_conv, conv_new = conv_mixer(p_conv, conv_buf, conv_w, conv_b, conv_ln_g, conv_ln_b)
    y_rwkv, shift_new, wkv_new = rwkv_mixer(p_rwkv, shift_prev, wkv_state, rwkv_mu, rwkv_w0, rwkv_w_up,
                                            rwkv_a0, rwkv_a_up, rwkv_g_up, rwkv_k_k, rwkv_k_a,
                                            rwkv_r_k, rwkv_ln_g, rwkv_ln_b)
    q, k, v = [p_att[..., i * ATT_DIM:(i + 1) * ATT_DIM].reshape(B, T, ATT_HEADS, HEAD_DIM) for i in range(3)]
    if k_past is None:
        k_all, v_all = k, v
    else:
        k_all = jnp.concatenate([k_past.astype(k.dtype), k], axis=1)
        v_all = jnp.concatenate([v_past.astype(v.dtype), v], axis=1)
    y_att = sb_attention(q, k_all, v_all, past_len, att_bias).reshape(B, T, ATT_DIM)
    mix = jnp.concatenate([y_conv, y_rwkv, y_att], axis=-1)
    x = x + mix @ w_out
    h2 = rmsnorm(x, norm2_g)
    x = x + peer(h2.reshape(B * T, D), peer_w_query, peer_sub_keys, peer_u, peer_v).reshape(B, T, D)
    return x, (k, v, conv_new, shift_new, wkv_new.astype(x.dtype))

def setup_inputs(seed: int = 0) -> dict:
    key = jax.random.key(seed)
    ks = jax.random.split(key, 40)
    f32 = jnp.float32
    n_pages = PAST_LEN // PAGE_SIZE
    n_used = DEC_BATCH * n_pages
    n_pool = n_used + max(1, n_used // 4)

    def nrm(k, shape, scale):
        return jax.random.normal(k, shape, f32) * scale

    def gain(k, shape):
        return 1.0 + nrm(k, shape, 0.02)

    page_table = jax.random.permutation(ks[7], n_pool)[:n_used].reshape(DEC_BATCH, n_pages).astype(jnp.int32)
    return {
        'x_prompt': nrm(ks[0], (BATCH, SEQ, D_MODEL), 1.0),
        'x_sample': nrm(ks[1], (DEC_BATCH, DEC_SEQ, D_MODEL), 1.0),
        'cache_k': nrm(ks[2], (DEPTH, n_pool, PAGE_SIZE, ATT_HEADS, HEAD_DIM), 1.0),
        'cache_v': nrm(ks[3], (DEPTH, n_pool, PAGE_SIZE, ATT_HEADS, HEAD_DIM), 1.0),
        'state_conv': nrm(ks[4], (DEPTH, DEC_BATCH, CONV_WIDTH - 1, CONV_CH), 0.5),
        'state_shift': nrm(ks[5], (DEPTH, DEC_BATCH, RWKV_COLS), 1.0),
        'state_wkv': nrm(ks[6], (DEPTH, DEC_BATCH, RWKV_HEADS, HEAD_DIM, HEAD_DIM), 1.0),
        'page_table': page_table,
        'norm1_g': gain(ks[8], (DEPTH, D_MODEL)),
        'w_in': nrm(ks[9], (DEPTH, D_MODEL, IN_COLS), D_MODEL ** -0.5),
        'conv_w': nrm(ks[10], (DEPTH, CONV_WIDTH, CONV_CH), CONV_WIDTH ** -0.5),
        'conv_b': nrm(ks[11], (DEPTH, CONV_CH), 0.02),
        'conv_ln_g': gain(ks[12], (DEPTH, CONV_CH)),
        'conv_ln_b': nrm(ks[13], (DEPTH, CONV_CH), 0.02),
        'rwkv_mu': jax.random.uniform(ks[14], (DEPTH, RWKV_COLS), f32),
        'rwkv_w0': jax.random.uniform(ks[15], (DEPTH, RWKV_DIM), f32, -4.0, -1.0),
        'rwkv_w_up': nrm(ks[16], (DEPTH, DECAY_LORA, RWKV_DIM), 0.5 * DECAY_LORA ** -0.5),
        'rwkv_a0': nrm(ks[17], (DEPTH, RWKV_DIM), 0.1),
        'rwkv_a_up': nrm(ks[18], (DEPTH, AAA_LORA, RWKV_DIM), 0.5 * AAA_LORA ** -0.5),
        'rwkv_g_up': nrm(ks[19], (DEPTH, GATE_LORA, RWKV_DIM), GATE_LORA ** -0.5),
        'rwkv_k_k': 0.85 + nrm(ks[20], (DEPTH, RWKV_DIM), 0.02),
        'rwkv_k_a': gain(ks[21], (DEPTH, RWKV_DIM)),
        'rwkv_r_k': nrm(ks[22], (DEPTH, RWKV_HEADS, HEAD_DIM), 0.1),
        'rwkv_ln_g': gain(ks[23], (DEPTH, RWKV_DIM)),
        'rwkv_ln_b': nrm(ks[24], (DEPTH, RWKV_DIM), 0.02),
        'att_bias': ATT_BIAS_INIT + nrm(ks[32], (DEPTH, ATT_HEADS), 0.5),
        'w_out': nrm(ks[25], (DEPTH, MIX_DIM, D_MODEL), MIX_DIM ** -0.5),
        'norm2_g': gain(ks[26], (DEPTH, D_MODEL)),
        'peer_w_query': nrm(ks[27], (DEPTH, D_MODEL, PEER_HEADS * PEER_DK), D_MODEL ** -0.5),
        'peer_sub_keys': nrm(ks[28], (DEPTH, PEER_HEADS, 2, N_KEYS, PEER_DK // 2), (PEER_DK // 2) ** -0.5),
        'peer_u': nrm(ks[29], (DEPTH, N_EXPERTS, D_MODEL), D_MODEL ** -0.5),
        'peer_v': nrm(ks[30], (DEPTH, N_EXPERTS, D_MODEL), PEER_HEADS ** -0.5),
        'final_g': gain(ks[31], (D_MODEL,)),
    }

def reference(x_prompt, x_sample, cache_k, cache_v, state_conv, state_shift, state_wkv, page_table,
              norm1_g, w_in, conv_w, conv_b, conv_ln_g, conv_ln_b,
              rwkv_mu, rwkv_w0, rwkv_w_up, rwkv_a0, rwkv_a_up, rwkv_g_up,
              rwkv_k_k, rwkv_k_a, rwkv_r_k, rwkv_ln_g, rwkv_ln_b, att_bias,
              w_out, norm2_g, peer_w_query, peer_sub_keys, peer_u, peer_v, final_g):
    n_pages = PAST_LEN // PAGE_SIZE
    past_len = n_pages * PAGE_SIZE
    layer_params = (norm1_g, w_in, conv_w, conv_b, conv_ln_g, conv_ln_b,
                    rwkv_mu, rwkv_w0, rwkv_w_up, rwkv_a0, rwkv_a_up, rwkv_g_up,
                    rwkv_k_k, rwkv_k_a, rwkv_r_k, rwkv_ln_g, rwkv_ln_b, att_bias,
                    w_out, norm2_g, peer_w_query, peer_sub_keys, peer_u, peer_v)
    xp, xs = x_prompt, x_sample
    bp, bs = xp.shape[0], xs.shape[0]
    st_p = [[] for _ in range(5)]
    st_s = [[] for _ in range(5)]
    for li in range(DEPTH):
        lw = [a[li] for a in layer_params]
        xp, new_p = trunk_layer(xp, jnp.zeros((bp, CONV_WIDTH - 1, CONV_CH), xp.dtype),
                                jnp.zeros((bp, RWKV_COLS), xp.dtype),
                                jnp.zeros((bp, RWKV_HEADS, HEAD_DIM, HEAD_DIM), jnp.float32),
                                None, None, 0, *lw)
        k_past = cache_k[li][page_table].reshape(bs, past_len, ATT_HEADS, HEAD_DIM)
        v_past = cache_v[li][page_table].reshape(bs, past_len, ATT_HEADS, HEAD_DIM)
        xs, new_s = trunk_layer(xs, state_conv[li], state_shift[li], state_wkv[li],
                                k_past, v_past, past_len, *lw)
        for j in range(5):
            st_p[j].append(new_p[j])
            st_s[j].append(new_s[j])
    y_prompt = rmsnorm(xp, final_g)
    y_sample = rmsnorm(xs, final_g)
    k_p, v_p, conv_p, shift_p, wkv_p = [jnp.stack(s, axis=0) for s in st_p]
    k_s, v_s, conv_s, shift_s, wkv_s = [jnp.stack(s, axis=0) for s in st_s]
    return (y_prompt, y_sample, k_p, v_p, conv_p, shift_p, wkv_p, k_s, v_s, conv_s, shift_s, wkv_s)


_drawn_inputs = setup_inputs


def setup_inputs(seed=0):
    import zlib

    import numpy as np

    out = dict(_drawn_inputs(seed))
    spreads = {}
    factors = {'conv_b': 2.678,
     'conv_ln_g': 43.349,
     'conv_ln_b': 38.708,
     'rwkv_k_k': 194.052,
     'rwkv_k_a': 2.672,
     'rwkv_ln_g': 42.77,
     'rwkv_ln_b': 49.346,
     'att_bias': 3.924,
     'final_g': 24.304,
     'norm2_g': 15.726,
     'rwkv_r_k': 4.658}
    for name, (base, spread) in spreads.items():
        noise = np.random.default_rng([zlib.crc32(name.encode()), seed]).standard_normal(out[name].shape)
        drawn = base * np.exp(spread * noise) if base else spread * noise
        out[name] = __import__('jax').numpy.asarray(drawn.astype(out[name].dtype))
    for name, factor in factors.items():
        out[name] = (out[name] * factor).astype(out[name].dtype)
    return out
```

```python
import math
from contextlib import ExitStack

import numpy as np

import concourse.bass as bass
from concourse import mybir

F32 = mybir.dt.float32
U32 = mybir.dt.uint32
ALU = mybir.AluOpType
ACT = mybir.ActivationFunctionType
AX = mybir.AxisListType

P = 128
D = 1024
DC = D // P
SEQ = 1024
DB, DS = 8, 4
NS = DB * DS
T = SEQ + NS
NBLK = -(-T // P)
TP = NBLK * P
HD = 64
CC = 256
CT = CC // P
KW = 31
RH = 6
PR = RH // 2
AH = 6
PA = AH // 2
ATT = AH * HD
RC = 1408
RT = RC // P
NT = 2 * CT + RT
CH = 64
NCH = SEQ // CH
SW = DS + 1
SC = SEQ + CH
PW = SC + 1
PAGE = 128
NPG = 1024 // PAGE
POOLN = 80
KEYS = 128
PH = 8
TOPK = 16
RMS_EPS = 1e-5
LN_EPS = 1e-5
GN_EPS = 64e-5
NCHUNKS = [(0, 512), (512, 512), (1024, NS)]


class Steps:

    def __init__(self, sem, names):
        self.sem, self.names, self.next = sem, list(names), 0

    def did(self, ins, name):
        assert self.names[self.next % len(self.names)] == name, (self.names[self.next % len(self.names)], name)
        self.next += 1
        ins.then_inc(self.sem, 1)

    def at(self, name, turn=0):
        return turn * len(self.names) + self.names.index(name) + 1


class Chain:

    def __init__(self, eng, sem, base=0):
        self.eng, self.sem, self.base, self.n = eng, sem, base, 0

    def __call__(self, ins):
        self.n += 1
        ins.then_inc(self.sem, 1)
        self.eng.wait_ge(self.sem, self.base + self.n)


def project(nc, io, sb):
    with ExitStack() as ctx:
        h = sb.mix[:, :, 0:T]
        sq = sb.prc[:, 0:DC, 0:T]
        w = ctx.enter_context(nc.sbuf_tensor("w_in_tile", [P, 3, DC, P], F32))
        wv = ctx.enter_context(nc.sbuf_tensor("w_v", [P, DC, ATT], F32))
        g1 = ctx.enter_context(nc.sbuf_tensor("g1", [P, DC], F32))
        mean_of = ctx.enter_context(nc.sbuf_tensor("mean_of", [P, P], F32))
        rstd = ctx.enter_context(nc.sbuf_tensor("rstd", [P, T], F32))
        banks = [ctx.enter_context(nc.psum_tensor(f"proj{b}", [P, 512], F32)) for b in range(6)]
        tails = ctx.enter_context(nc.psum_tensor("proj_tails", [P, NS], F32))
        sem = lambda name: ctx.enter_context(nc.semaphore(name))
        x_in, small_in, wv_in = sem("x_in"), sem("small_in"), sem("wv_in")
        w_in = [sem(f"w_in{s}") for s in range(3)]
        ones_set, squared, mean_ready, root_ready = sem("ones_set"), sem("squared"), sem("mean_ready"), sem("root_ready")
        pads_set, h_ready, tile_done = sem("pads_set"), sem("h_ready"), sem("tile_done")
        act_free, dve_free = sem("act_free"), sem("dve_free")
        v_done, v_kept, kv_out = sem("v_done"), sem("v_kept"), sem("kv_out")
        dve_chain = sem("proj_dve")
        RCT, QKT = NT // 3, 2 * PA // 3
        block = ctx.enter_context(nc.Block())

        @block.sync
        def _(sp):
            for c in range(DC):
                sp.dma_start(h[:, c, :], io["xT"][:, c, :]).then_inc(x_in, 16)
            sp.dma_start(g1[:, :], io["norm1_g"]).then_inc(small_in, 16)
            for s in range(3):
                sp.dma_start(w[:, s, :, :], io["w_in"][s]).then_inc(w_in[s], 16)
            with sp.Fori(1, RCT + QKT) as i:
                for s in range(3):
                    sp.wait_ge(tile_done, 3 * (i - 1) + s + 1)
                    sp.dma_start(w[:, s, :, :], io["w_in"][bass.ds(3 * i + s, 1)].rearrange("o p c n -> p (o c) n"))\
                        .then_inc(w_in[s], 16)
            sp.dma_start(wv[:, :, :], io["w_v"]).then_inc(wv_in, 16)
            sp.wait_ge(act_free, 3 + NT + 2 * PA)
            sp.wait_ge(dve_free, 3 + NT + 2 * PA)
            sp.dma_start(io["k_new"], sb.qk[:, PA:2 * PA, :]).then_inc(kv_out, 16)
            sp.wait_ge(v_kept, NBLK)
            for b in range(NBLK):
                n = min(P, T - b * P)
                sp.dma_start(io["v_new"][b * P:b * P + n, :], sb.vtok[0:n, b, :]).then_inc(kv_out, 16)
            sp.wait_ge(kv_out, 16 * (1 + NBLK))

        @block.scalar
        def _(act):
            act.wait_ge(x_in, 16 * DC)
            for c in range(DC):
                nc.scalar.activation(sq[:, c, :], h[:, c, :], ACT.Square).then_inc(squared, 1)
            act.wait_ge(mean_ready, 1)
            act.wait_ge(ones_set, 2)
            for n, (lo, size) in enumerate(NCHUNKS):
                src = banks[n][:, 0:size]
                nc.scalar.activation(rstd[:, lo:lo + size], src, ACT.Sqrt, bias=sb.eps[:, 0:1]).then_inc(root_ready, 1)
            act.sem_inc(act_free, 3)
            act.wait_ge(h_ready, DC)

            def keep(i, dest, off, turn):
                for s in range(3):
                    act.wait_ge(tile_done, 3 * turn + s + 1)
                    nc.scalar.activation(dest[:, bass.ds(3 * i + s, 1), off:off + 512], banks[2 * s][:, :],
                                         ACT.Copy).then_inc(act_free, 1)

            with act.Fori(0, RCT) as i:
                keep(i, sb.prc, 1, i)
            with act.Fori(0, QKT) as i:
                keep(i, sb.qk, 0, i + RCT)
            for b in range(NBLK):
                n = min(P, T - b * P)
                act.wait_ge(v_done, b + 1)
                nc.scalar.activation(sb.vtok[0:n, b, :], banks[b % 6][0:n, 0:ATT], ACT.Copy).then_inc(v_kept, 1)

        @block.vector
        def _(dve):
            link = Chain(dve, dve_chain)
            nc.vector.memset(mean_of[:, :], 1.0 / D).then_inc(ones_set, 1)
            nc.vector.memset(sb.eps[:, 0:1], RMS_EPS).then_inc(ones_set, 1)
            dve.wait_ge(root_ready, len(NCHUNKS))
            link(nc.vector.reciprocal(rstd[:, :], rstd[:, :]))
            dve.wait_ge(small_in, 16)
            for c in range(DC):
                nc.vector.scalar_tensor_tensor(h[:, c, :], h[:, c, :], g1[:, c:c + 1], rstd[:, :],
                                               ALU.mult, ALU.mult).then_inc(h_ready, 1)
            dve.wait_ge(mean_ready, 1)
            nc.vector.memset(sb.prc[:, :, 0:1], 0.0).then_inc(pads_set, 1)
            nc.vector.memset(sb.prc[:, :, 1 + SEQ:PW], 0.0).then_inc(pads_set, 1)
            dve.wait_ge(pads_set, 2)
            nc.vector.sem_inc(dve_free, 3)

            def keep(i, dest, off, turn, spread):
                for s in range(3):
                    dve.wait_ge(tile_done, 3 * turn + s + 1)
                    nc.vector.tensor_copy(dest[:, bass.ds(3 * i + s, 1), off + 512:off + SEQ],
                                          banks[2 * s + 1][:, :])
                    if spread:
                        to = dest[:, bass.ds(3 * i + s, 1), 1 + SEQ:1 + SEQ + DB * SW]\
                            .rearrange("p o (b s) -> p (o b) s", s=SW)[:, :, 1:SW]
                        last = nc.vector.tensor_copy(to, tails[:, :].rearrange("p (b s) -> p b s", s=DS))
                    else:
                        last = nc.vector.tensor_copy(dest[:, bass.ds(3 * i + s, 1), SEQ:T], tails[:, :])
                    last.then_inc(dve_free, 1)

            with dve.Fori(0, RCT) as i:
                keep(i, sb.prc, 1, i, True)
            with dve.Fori(0, QKT) as i:
                keep(i, sb.qk, 0, i + RCT, False)

        @block.tensor
        def _(pe):
            pe.wait_ge(ones_set, 1)
            for n, (lo, size) in enumerate(NCHUNKS):
                for c in range(DC):
                    pe.wait_ge(squared, c + 1)
                    last = nc.tensor.matmul(banks[n][:, 0:size], mean_of[:, :], sq[:, c, lo:lo + size],
                                            start=c == 0, stop=c == DC - 1)
            last.then_inc(mean_ready, 1)
            pe.wait_ge(h_ready, DC)
            with pe.Fori(0, RCT + QKT) as i:
                for s in range(3):
                    pe.wait_ge(w_in[s], 16 * (i + 1))
                    pe.wait_ge(act_free, 3 * i + s + 1)
                    pe.wait_ge(dve_free, 3 * i + s + 1)
                    for n, (lo, size) in enumerate(NCHUNKS):
                        out = tails[:, :] if n == 2 else banks[2 * s + n][:, :]
                        if n == 2:
                            pe.wait_ge(dve_free, 3 * i + s + 3)
                        for c in range(DC):
                            last = nc.tensor.matmul(out, w[:, s, c, :], h[:, c, lo:lo + size],
                                                    start=c == 0, stop=c == DC - 1)
                    last.then_inc(tile_done, 1)
            pe.wait_ge(wv_in, 16)
            pe.wait_ge(act_free, 3 + NT + 2 * PA)
            pe.wait_ge(dve_free, 3 + NT + 2 * PA)
            for b in range(NBLK):
                n = min(P, T - b * P)
                if b >= 6:
                    pe.wait_ge(v_kept, b - 5)
                for c in range(DC):
                    last = nc.tensor.matmul(banks[b % 6][0:n, 0:ATT], h[:, c, b * P:b * P + n], wv[:, c, :],
                                            start=c == 0, stop=c == DC - 1)
                last.then_inc(v_done, 1)


def attend_prompt(nc, io, sb):
    QW = 512
    units = [(qc, kt, h) for qc in range(SEQ // QW) for kt in reversed(range((qc + 1) * QW // P)) for h in range(2)]
    U = len(units)
    R = 4
    with ExitStack() as ctx:
        t = lambda name, shape: ctx.enter_context(nc.sbuf_tensor(name, shape, F32))
        sem = lambda name: ctx.enter_context(nc.semaphore(name))
        q, k, v = t("q_pair", [P, SEQ]), t("k_pair", [P, SEQ]), t("v_pair", [P, SEQ // P, P])
        bias, bias2 = t("att_bias", [P, AH]), t("bias_pair", [P, 2])
        tri, rest = t("tri", [P, P]), t("rest", [P, P])
        seen, cap = t("seen", [P, QW // P, QW]), t("cap", [P, QW // P, QW])
        zb, w, a = t("logit", [P, R, QW]), t("soft", [P, R, QW]), t("weight", [P, R, QW])
        ps = lambda name: ctx.enter_context(nc.psum_tensor(name, [P, QW], F32))
        Z = [[ps(f"z{h}{n}") for n in range(2)] for h in range(2)]
        A = [ps(f"later{h}") for h in range(2)]
        O = ps("att_out")
        const_in = sem("att_const_in")
        q_staged, v_staged = sem("q_staged"), sem("v_staged")
        z_done, logit_done, min_done, exp_done, ln_done = sem("z_done"), sem("logit_done"), sem("min_done"), sem("exp_done"), sem("ln_done")
        soft_done, sum_done, diff_done, weight_done = sem("soft_done"), sem("sum_done"), sem("diff_done"), sem("weight_done")
        rest_done, pv_done, out_kept, masked = sem("rest_done"), sem("pv_done"), sem("out_kept"), sem("masked")
        block = ctx.enter_context(nc.Block())
        QCS = SEQ // QW
        last_of = {qc: max(n for n, x in enumerate(units) if x[0] == qc) for qc in range(QCS)}
        first = {(qc, h): min(n for n, x in enumerate(units) if x[0] == qc and x[2] == h) for qc in range(QCS) for h in range(2)}
        rests = [n for n, x in enumerate(units) if x[1] > 0]
        NM = 2 * sum(x[1] * P // QW == x[0] for x in units)

        @block.sync
        def _(sp):
            for dst, src in ((bias, "att_bias"), (tri, "tri"), (rest, "tri_rest")):
                sp.dma_start(dst[:, :], io[src]).then_inc(const_in, 16)
            for dst, src in ((seen, "att_seen"), (cap, "att_cap")):
                sp.dma_start(dst[:, :, :], io[src]).then_inc(const_in, 16)
            sp.wait_ge(const_in, 80)

        @block.vector
        def _(dve):
            def logit(i, n):
                qc, kt, h = units[n]
                dve.wait_ge(z_done, i * U + n + 1)
                if n >= R:
                    dve.wait_ge(diff_done, i * U + n - R + 1)
                nc.vector.tensor_scalar(zb[:, n % R, :], Z[h][n // 2 % 2][:, :], HD ** -0.5, bias2[:, h:h + 1],
                                        ALU.mult, ALU.add).then_inc(logit_done, 1)
                if n >= R:
                    if n - R in rests:
                        dve.wait_ge(rest_done, i * len(rests) + rests.index(n - R) + 1)
                    else:
                        dve.wait_ge(sum_done, i * U + n - R + 1)
                dve.wait_ge(logit_done, i * U + n + 1)
                nc.vector.tensor_scalar(w[:, n % R, :], zb[:, n % R, :], 40.0, None, ALU.min).then_inc(min_done, 1)

            masks = [0]

            def soft(i, n):
                qc, kt, h = units[n]
                dve.wait_ge(ln_done, i * U + n + 1)
                ins = nc.vector.tensor_tensor(w[:, n % R, :], w[:, n % R, :], zb[:, n % R, :], ALU.max)
                if kt * P // QW == qc:
                    masks[0] += 1
                    ins.then_inc(masked, 1)
                    dve.wait_ge(masked, i * NM + masks[0])
                    ins = nc.vector.tensor_tensor(w[:, n % R, :], w[:, n % R, :], seen[:, kt - qc * QW // P, :], ALU.mult)
                ins.then_inc(soft_done, 1)

            def diff(i, n):
                qc, kt, h = units[n]
                dve.wait_ge(sum_done, i * U + n + 1)
                if n >= R:
                    dve.wait_ge(pv_done, i * U + n - R + 1)
                ins = nc.vector.tensor_tensor(a[:, n % R, :], zb[:, n % R, :], A[h][:, :], ALU.subtract)
                if kt * P // QW == qc:
                    masks[0] += 1
                    ins.then_inc(masked, 1)
                    dve.wait_ge(masked, i * NM + masks[0])
                    ins = nc.vector.tensor_tensor(a[:, n % R, :], a[:, n % R, :], cap[:, kt - qc * QW // P, :], ALU.min)
                ins.then_inc(diff_done, 1)

            dve.wait_ge(const_in, 80)
            with dve.Fori(0, PA) as i:
                nc.vector.tensor_copy(q[:, :], sb.qk[:, bass.ds(i, 1), 0:SEQ]).then_inc(q_staged, 1)
                nc.vector.tensor_copy(k[:, :], sb.qk[:, bass.ds(i + PA, 1), 0:SEQ]).then_inc(q_staged, 1)
                nc.vector.tensor_copy(bias2[:, :], bias[:, bass.ds(2 * i, 2)]).then_inc(q_staged, 1)
                dve.wait_ge(q_staged, 3 * i + 3)
                masks[0] = 0
                for n in range(-3, U):
                    if n + 3 < U:
                        logit(i, n + 3)
                    if 0 <= n + 2 < U:
                        soft(i, n + 2)
                    if n >= 0:
                        diff(i, n)
                dve.wait_ge(pv_done, U * i + U)
                dve.wait_ge(weight_done, U * i + U)

        @block.scalar
        def _(act):
            with act.Fori(0, PA) as i:
                nc.scalar.activation(v[:, :, :], sb.vtok[:, 0:SEQ // P, bass.ds(i * P, P)], ACT.Copy).then_inc(v_staged, 1)
                for n in range(-2, U):
                    if n + 2 < U:
                        m = n + 2
                        act.wait_ge(min_done, i * U + m + 1)
                        nc.scalar.activation(w[:, m % R, :], w[:, m % R, :], ACT.Exp).then_inc(exp_done, 1)
                        act.wait_ge(exp_done, i * U + m + 1)
                        nc.scalar.activation(w[:, m % R, :], w[:, m % R, :], ACT.Ln, bias=1.0).then_inc(ln_done, 1)
                    if n >= 0:
                        act.wait_ge(diff_done, i * U + n + 1)
                        nc.scalar.activation(a[:, n % R, :], a[:, n % R, :], ACT.Exp).then_inc(weight_done, 1)
                    for qc in range(QCS):
                        if n == min(last_of[qc] + 2, U - 1):
                            act.wait_ge(pv_done, i * U + last_of[qc] + 1)
                            nc.scalar.activation(sb.mix[:, bass.ds(i + DC - PA, 1), qc * QW:(qc + 1) * QW], O[:, :],
                                                 ACT.Copy).then_inc(out_kept, 1)

        @block.tensor
        def _(pe):
            def score(i, n):
                qc, kt, h = units[n]
                if n >= 4:
                    pe.wait_ge(logit_done, i * U + n - 4 + 1)
                nc.tensor.matmul(Z[h][n // 2 % 2][:, :], k[h * HD:(h + 1) * HD, kt * P:(kt + 1) * P],
                                 q[h * HD:(h + 1) * HD, qc * QW:(qc + 1) * QW], start=True, stop=True).then_inc(z_done, 1)

            def later(i, n):
                qc, kt, h = units[n]
                pe.wait_ge(soft_done, i * U + n + 1)
                if n == first[qc, h] and qc:
                    pe.wait_ge(diff_done, i * U + last_of[qc - 1] + 1)
                nc.tensor.matmul(A[h][:, :], tri[:, :], w[:, n % R, :], start=n == first[qc, h], stop=True,
                                 skip_group_check=True).then_inc(sum_done, 1)

            def value(i, n):
                qc, kt, h = units[n]
                if n in rests:
                    pe.wait_ge(diff_done, i * U + n + 1)
                    nc.tensor.matmul(A[h][:, :], rest[:, :], w[:, n % R, :], start=False, stop=True,
                                     skip_group_check=True).then_inc(rest_done, 1)
                pe.wait_ge(weight_done, i * U + n + 1)
                if n == first[qc, 0] and qc:
                    pe.wait_ge(out_kept, i * QCS + qc)
                nc.tensor.matmul(O[h * HD:(h + 1) * HD, :], v[:, kt, h * HD:(h + 1) * HD], a[:, n % R, :],
                                 start=n == first[qc, h], stop=kt == 0, skip_group_check=True).then_inc(pv_done, 1)

            with pe.Fori(0, PA) as i:
                pe.wait_ge(q_staged, 3 * i + 3)
                pe.wait_ge(v_staged, i + 1)
                for n in range(-3, U + 1):
                    if n + 3 < U:
                        score(i, n + 3)
                    if 0 <= n < U:
                        later(i, n)
                    if n >= 1:
                        value(i, n - 1)
                pe.wait_ge(out_kept, i * QCS + QCS)


def convolve(nc, io, sb):
    HIST = KW - 1
    with ExitStack() as ctx:
        t = lambda name, shape: ctx.enter_context(nc.sbuf_tensor(name, shape, F32))
        sem = lambda name: ctx.enter_context(nc.semaphore(name))
        xp, xs = t("conv_rows", [P, CT, HIST + SEQ]), t("conv_rows_sample", [P, CT, DB, HIST + DS])
        gate = t("conv_gate", [P, CT, PW])
        y = sb.mix
        sq, rs = t("conv_sq", [P, CT, T]), t("conv_rstd", [P, T])
        cw, aff = t("conv_w", [P, CT, KW]), t("conv_affine", [P, CT, 3])
        mean_of = t("conv_mean_of", [P, P])
        mean = [ctx.enter_context(nc.psum_tensor(f"conv_mean{n}", [P, 512], F32)) for n in range(3)]
        var = [ctx.enter_context(nc.psum_tensor(f"conv_var{n}", [P, 512], F32)) for n in range(3)]
        params_in, state_in, gated, sig_done, glu_done = sem("conv_params"), sem("conv_state"), sem("conv_set"), sem("conv_sig"), sem("conv_glu")
        taps, conv_done, mean_done, centred = sem("conv_taps"), sem("conv_done"), sem("conv_mean_done"), sem("conv_centred")
        squared, var_done, root_done, rstd_done = sem("conv_squared"), sem("conv_var_done"), sem("conv_root"), sem("conv_rstd_done")
        normed, silu_done, mixed, out = sem("conv_normed"), sem("conv_silu"), sem("conv_mixed"), sem("conv_out")
        block = ctx.enter_context(nc.Block())

        @block.sync
        def _(sp):
            sp.dma_start(cw[:, :, :], io["conv_w"]).then_inc(params_in, 16)
            sp.dma_start(aff[:, :, :], io["conv_affine"]).then_inc(params_in, 16)
            for c in range(CT):
                sp.dma_start(xs[:, c, :, 0:HIST], io["state_conv"][c]).then_inc(state_in, 16)
            sp.wait_ge(glu_done, 2 * CT)
            sp.wait_ge(state_in, 16 * CT)
            sp.dma_start(io["conv_new_prompt"], xp[:, :, SEQ:]).then_inc(out, 16)
            for c in range(CT):
                sp.dma_start(io["conv_new_sample"][c], xs[:, c, :, DS:]).then_inc(out, 16)
            sp.wait_ge(out, 16 + 16 * CT)

        @block.scalar
        def _(act):
            for c in range(CT):
                nc.scalar.activation(gate[:, c, :], sb.prc[:, CT + c, :], ACT.Sigmoid).then_inc(sig_done, 1)
            for c in range(CT):
                act.wait_ge(centred, (c + 1) * len(NCHUNKS))
                nc.scalar.activation(sq[:, c, :], y[:, c, 0:T], ACT.Square).then_inc(squared, 1)
            act.wait_ge(var_done, 1)
            act.wait_ge(gated, 4)
            for n, (lo, size) in enumerate(NCHUNKS):
                nc.scalar.activation(rs[:, lo:lo + size], var[n][:, 0:size], ACT.Sqrt, bias=sb.eps[:, 1:2]).then_inc(root_done, 1)
            act.wait_ge(params_in, 32)
            for c in range(CT):
                act.wait_ge(normed, c + 1)
                nc.scalar.activation(sq[:, c, :], y[:, c, 0:T], ACT.Sigmoid, bias=aff[:, c, 2:3],
                                     scale=aff[:, c, 1:2]).then_inc(silu_done, 1)

        @block.vector
        def _(dve):
            nc.vector.memset(xp[:, :, 0:HIST], 0.0).then_inc(gated, 1)
            nc.vector.memset(mean_of[:, :], 1.0 / CC).then_inc(gated, 1)
            nc.vector.memset(sb.eps[:, 1:2], LN_EPS).then_inc(gated, 1)
            nc.vector.memset(sb.eps[:, 2:3], GN_EPS).then_inc(gated, 1)
            sample = lambda tile: tile[:, 1 + SEQ:1 + SEQ + DB * SW].rearrange("p (b s) -> p b s", s=SW)[:, :, 1:SW]
            for c in range(CT):
                dve.wait_ge(sig_done, c + 1)
                nc.vector.tensor_tensor(xp[:, c, HIST:], sb.prc[:, c, 1:1 + SEQ], gate[:, c, 1:1 + SEQ],
                                        ALU.mult).then_inc(glu_done, 1)
                nc.vector.tensor_tensor(xs[:, c, :, HIST:], sample(sb.prc[:, c, :]), sample(gate[:, c, :]),
                                        ALU.mult).then_inc(glu_done, 1)
            dve.wait_ge(params_in, 32)
            dve.wait_ge(state_in, 16 * CT)
            dve.wait_ge(gated, 4)
            dve.wait_ge(glu_done, 2 * CT)
            ys = lambda c: y[:, c, SEQ:T].rearrange("p (b s) -> p b s", s=DS)
            for j in range(KW):
                for c in range(CT):
                    if j:
                        dve.wait_ge(taps, 2 * (CT * (j - 1) + c + 1))
                    for to, rows in ((y[:, c, 0:SEQ], xp[:, c, j:j + SEQ]), (ys(c), xs[:, c, :, j:j + DS])):
                        if j == 0:
                            ins = nc.vector.tensor_scalar(to, rows, cw[:, c, 0:1], aff[:, c, 0:1], ALU.mult, ALU.add)
                        else:
                            ins = nc.vector.scalar_tensor_tensor(to, rows, cw[:, c, j:j + 1], to, ALU.mult, ALU.add)
                        ins.then_inc(taps, 1)
            dve.wait_ge(mean_done, 1)
            for c in range(CT):
                for n, (lo, size) in enumerate(NCHUNKS):
                    nc.vector.tensor_tensor(y[:, c, lo:lo + size], y[:, c, lo:lo + size], mean[n][:, 0:size],
                                            ALU.subtract).then_inc(centred, 1)
            dve.wait_ge(root_done, len(NCHUNKS))
            nc.vector.reciprocal(rs[:, :], rs[:, :]).then_inc(rstd_done, 1)
            dve.wait_ge(rstd_done, 1)
            dve.wait_ge(centred, CT * len(NCHUNKS))
            for c in range(CT):
                nc.vector.tensor_tensor(y[:, c, 0:T], y[:, c, 0:T], rs[:, :], ALU.mult).then_inc(normed, 1)
            for c in range(CT):
                dve.wait_ge(silu_done, c + 1)
                nc.vector.tensor_scalar(y[:, c, 0:T], y[:, c, 0:T], aff[:, c, 1:2], aff[:, c, 2:3],
                                        ALU.mult, ALU.add).then_inc(mixed, 1)
                dve.wait_ge(mixed, 2 * c + 1)
                nc.vector.tensor_tensor(y[:, c, 0:T], y[:, c, 0:T], sq[:, c, :], ALU.mult).then_inc(mixed, 1)

        @block.tensor
        def _(pe):
            pe.wait_ge(taps, 2 * CT * KW)
            for n, (lo, size) in enumerate(NCHUNKS):
                for c in range(CT):
                    last = nc.tensor.matmul(mean[n][:, 0:size], mean_of[:, :], y[:, c, lo:lo + size],
                                            start=c == 0, stop=c == CT - 1)
            last.then_inc(mean_done, 1)
            pe.wait_ge(squared, CT)
            for n, (lo, size) in enumerate(NCHUNKS):
                for c in range(CT):
                    last = nc.tensor.matmul(var[n][:, 0:size], mean_of[:, :], sq[:, c, lo:lo + size],
                                            start=c == 0, stop=c == CT - 1)
            last.then_inc(var_done, 1)


def prepare_rwkv(nc, io, sb):
    with ExitStack() as ctx:
        t = lambda name, shape: ctx.enter_context(nc.sbuf_tensor(name, shape, F32))
        sem = lambda name: ctx.enter_context(nc.semaphore(name))
        R0, K0, V0, LO, GA = 2 * CT, 2 * CT + PR, 2 * CT + 2 * PR, NT - 2, NT - 1
        tile = lambda j: sb.prc[:, j, 1:PW]
        mu, par = sb.mu, sb.rwkv_par
        wa_up, blk, fresh = t("wa_up", [P, RH * HD]), sb.head_sum, t("scan_keep", [P, SC])
        carried, shift = t("carried", [P, RT, DB]), t("shift_new", [P, RT, 1 + DB])
        step = t("shift_diff", [P, 2, SC])
        lw, aa, cs, before, sq, pw = (t(n, [P, SC]) for n in ("log_decay", "aaa", "log_product", "log_before", "k_sq", "product"))
        pieces = [(0, 512), (512, 512), (1024, SC - 1024)]
        bw = [ctx.enter_context(nc.psum_tensor(f"rw_w{n}", [P, 512], F32)) for n in range(3)]
        ba = [ctx.enter_context(nc.psum_tensor(f"rw_a{n}", [P, 512], F32)) for n in range(3)]
        const_in, carried_in, carried_set, shift_out = sem("rw_const"), sem("rw_carried"), sem("rw_carried_set"), sem("rw_shift_out")
        shifted, tanh_done = sem("rw_shifted"), sem("rw_tanh")
        V = Steps(sem("rw_dve"), ["scale", "scan", "before", "kraw", "root", "recip", "kk", "am", "knew", "b", "bon", "bonv",
                                  "rq", "kq", "kh", "bh", "ends", "ends_sample"])
        A = Steps(sem("rw_act"), ["decay", "aaa", "sq", "norm", "prod", "prod_before", "prod_inv"])
        E = Steps(sem("rw_pe"), ["up", "norm", "bonus"])
        block = ctx.enter_context(nc.Block())

        @block.sync
        def _(sp):
            sp.dma_start(carried[:, :, :], io["state_shift"]).then_inc(carried_in, 16)
            for dst, src in ((mu, "rwkv_mu"), (wa_up, "wa_up"), (blk, "head_sum"), (fresh, "scan_keep")):
                sp.dma_start(dst[:, :], io[src]).then_inc(const_in, 16)
            sp.dma_start(par[:, :, :], io["rwkv_par"]).then_inc(const_in, 16)
            sp.wait_ge(carried_set, 3)
            sp.dma_start(io["shift_new"], shift[:, :, :]).then_inc(shift_out, 16)
            sp.wait_ge(shift_out, 16)

        @block.vector
        def _(dve):
            rows = sb.prc[:, R0:NT, :]
            dve.wait_ge(carried_in, 16)
            nc.vector.tensor_copy(rows[:, :, 1 + SEQ:1 + SEQ + DB * SW].rearrange("p j (b s) -> p j b s", s=SW)[:, :, :, 0],
                                  carried[:, :, :]).then_inc(carried_set, 1)
            nc.vector.tensor_copy(shift[:, :, 0:1], rows[:, :, SEQ:SEQ + 1]).then_inc(carried_set, 1)
            nc.vector.tensor_copy(shift[:, :, 1:], rows[:, :, 1 + SEQ:1 + SEQ + DB * SW].rearrange("p j (b s) -> p j b s", s=SW)[:, :, :, SW - 1])\
                .then_inc(carried_set, 1)
            dve.wait_ge(carried_set, 3)
            dve.wait_ge(const_in, 80)
            for j in range(RT):
                j_ = R0 + j
                if j >= 2:
                    dve.wait_ge(shifted, 2 * (j - 1))
                nc.vector.tensor_tensor(step[:, j % 2, :], sb.prc[:, j_, 0:SC], tile(j_), ALU.subtract).then_inc(shifted, 1)
                dve.wait_ge(shifted, 2 * j + 1)
                nc.vector.scalar_tensor_tensor(tile(j_), step[:, j % 2, :], mu[:, j:j + 1], tile(j_), ALU.mult, ALU.add)\
                    .then_inc(shifted, 1)
            dve.wait_ge(shifted, 2 * RT)
            for i in range(PR):
                r, k, v = tile(R0 + i), tile(K0 + i), tile(V0 + i)
                kq, bh, bv = sb.kq[:, i, :], sb.bh[:, i, :], tile(i)
                p = lambda n: par[:, i, n:n + 1]
                own = lambda name: dve.wait_ge(V.sem, V.at(name, i))
                dve.wait_ge(A.sem, A.at("aaa", i))
                V.did(nc.vector.tensor_scalar(lw[:, :], lw[:, :], -math.exp(-0.5), None, ALU.mult), "scale")
                own("scale")
                V.did(nc.vector.tensor_tensor_scan(cs[:, :], fresh[:, :], lw[:, :], 0.0, ALU.mult, ALU.add), "scan")
                own("scan")
                V.did(nc.vector.tensor_tensor(before[:, :], cs[:, :], lw[:, :], ALU.subtract), "before")
                V.did(nc.vector.tensor_scalar(kq, k, p(2), None, ALU.mult), "kraw")
                dve.wait_ge(A.sem, A.at("norm", i))
                V.did(nc.vector.tensor_scalar(sq[:, :], sq[:, :], 1e-12, None, ALU.max), "root")
                own("root")
                V.did(nc.vector.reciprocal(sq[:, :], sq[:, :]), "recip")
                own("recip")
                V.did(nc.vector.tensor_tensor(kq, kq, sq[:, :], ALU.mult), "kk")
                own("kk")
                V.did(nc.vector.tensor_scalar(sq[:, :], aa[:, :], 1.0, p(3), ALU.subtract, ALU.mult), "am")
                own("am")
                V.did(nc.vector.scalar_tensor_tensor(k, sq[:, :], 1.0, k, ALU.add, ALU.mult), "knew")
                V.did(nc.vector.tensor_tensor(bh, kq, aa[:, :], ALU.mult), "b")
                own("knew")
                V.did(nc.vector.scalar_tensor_tensor(sq[:, :], r, p(4), k, ALU.mult, ALU.mult), "bon")
                dve.wait_ge(E.sem, E.at("bonus", i))
                for n, (lo, size) in enumerate(pieces):
                    last = nc.vector.tensor_tensor(bv[:, lo:lo + size], v[:, lo:lo + size], ba[n][:, 0:size], ALU.mult)
                V.did(last, "bonv")
                dve.wait_ge(A.sem, A.at("prod_inv", i))
                own("bonv")
                V.did(nc.vector.tensor_tensor(r, r, pw[:, :], ALU.mult), "rq")
                V.did(nc.vector.tensor_tensor(kq, kq, before[:, :], ALU.mult), "kq")
                V.did(nc.vector.tensor_tensor(k, k, cs[:, :], ALU.mult), "kh")
                V.did(nc.vector.tensor_tensor(bh, bh, cs[:, :], ALU.mult), "bh")
                V.did(nc.vector.tensor_copy(sb.ends[:, 0:NCH, i], pw[:, 0:SEQ].rearrange("p (n c) -> p n c", c=CH)[:, :, CH - 1]), "ends")
                V.did(nc.vector.tensor_copy(sb.ends[:, NCH:NCH + DB, i], pw[:, SEQ:SEQ + DB * SW].rearrange("p (n c) -> p n c", c=SW)[:, :, SW - 1]),
                      "ends_sample")

        @block.scalar
        def _(act):
            act.wait_ge(shifted, 2 * (LO - R0) + 2)
            nc.scalar.activation(sb.prc[0:HD, LO, 1:PW], sb.prc[0:HD, LO, 1:PW], ACT.Tanh).then_inc(tanh_done, 1)
            act.wait_ge(const_in, 80)
            for i in range(PR):
                p = lambda n: par[:, i, n:n + 1]
                if i:
                    act.wait_ge(V.sem, V.at("ends_sample", i - 1))
                act.wait_ge(E.sem, E.at("up", i))
                for what, bank, dst, n_ in (("decay", bw, lw, 0), ("aaa", ba, aa, 1)):
                    for n, (lo, size) in enumerate(pieces):
                        last = nc.scalar.activation(dst[:, lo:lo + size], bank[n][:, 0:size], ACT.Sigmoid, bias=p(n_))
                    A.did(last, what)
                act.wait_ge(V.sem, V.at("kraw", i))
                A.did(nc.scalar.activation(sq[:, :], sb.kq[:, i, :], ACT.Square), "sq")
                act.wait_ge(E.sem, E.at("norm", i))
                for n, (lo, size) in enumerate(pieces):
                    last = nc.scalar.activation(sq[:, lo:lo + size], bw[n][:, 0:size], ACT.Sqrt)
                A.did(last, "norm")
                A.did(nc.scalar.activation(pw[:, :], cs[:, :], ACT.Exp), "prod")
                A.did(nc.scalar.activation(before[:, :], before[:, :], ACT.Exp), "prod_before")
                A.did(nc.scalar.activation(cs[:, :], cs[:, :], ACT.Exp, scale=-1.0), "prod_inv")

        @block.tensor
        def _(pe):
            pe.wait_ge(tanh_done, 1)
            pe.wait_ge(shifted, 2 * RT)
            pe.wait_ge(const_in, 80)
            for i in range(PR):
                cols = slice(i * P, (i + 1) * P)
                if i:
                    pe.wait_ge(V.sem, V.at("bonv", i - 1))
                for bank, lo_p in ((bw, 0), (ba, HD)):
                    for n, (lo, size) in enumerate(pieces):
                        last = nc.tensor.matmul(bank[n][:, 0:size], wa_up[lo_p:lo_p + HD, cols],
                                                sb.prc[lo_p:lo_p + HD, LO, 1 + lo:1 + lo + size], start=True, stop=True)
                E.did(last, "up")
                pe.wait_ge(A.sem, A.at("sq", i))
                for n, (lo, size) in enumerate(pieces):
                    last = nc.tensor.matmul(bw[n][:, 0:size], blk[:, :], sq[:, lo:lo + size], start=True, stop=True)
                E.did(last, "norm")
                pe.wait_ge(V.sem, V.at("bon", i))
                for n, (lo, size) in enumerate(pieces):
                    last = nc.tensor.matmul(ba[n][:, 0:size], blk[:, :], sq[:, lo:lo + size], start=True, stop=True)
                E.did(last, "bonus")


def scan_rwkv(nc, io, sb):
    with ExitStack() as ctx:
        t = lambda name, shape: ctx.enter_context(nc.sbuf_tensor(name, shape, F32))
        sem = lambda name: ctx.enter_context(nc.semaphore(name))
        R0, K0, V0 = 2 * CT, 2 * CT + PR, 2 * CT + 2 * PR
        kr, kh, bh, vs = t("kq_rq", [P, PR, 2, CH]), t("kh_c", [P, PR, CH]), t("bh_c", [P, PR, CH]), t("v_c", [P, PR, CH])
        end, state, state2 = t("end_c", [P, PR]), t("state", [P, PR, HD]), t("state_kept", [P, PR, HD])
        eye = t("eye", [P, HD])
        masks = t("masks", [P, 2, 5, PR, CH])
        na, arb = t("na", [P, PR, 2, CH]), t("arb", [P, PR, CH])
        xd, xl, md = t("xd", [P, PR, CH]), t("xl", [P, PR, CH]), t("md", [P, PR, CH])
        vk, bt = t("v_kh_tok", [P, 2, PR, CH]), t("bh_tok", [P, PR, CH])
        p2, p4 = t("pow2", [P, 2, PR, CH]), t("pow4", [P, 2, PR, CH])
        r1, r2, r3, td, tdt, zt = (t(n, [P, PR, CH]) for n in ("r1", "r2", "r3", "td", "tdt", "zt"))
        q1, q2, tt, w, nu = (t(n, [P, PR, CH]) for n in ("q1", "q2", "tt", "w_rhs", "neg_u"))
        s0, tmask = t("state_sample", [P, PR, DB, HD]), t("seq_mask", [P, DB, HD])
        spread, w0, um, vm = t("spread", [P, DB, HD]), t("w_state", [P, PR, HD]), t("um", [P, DB, HD]), t("vm", [P, DB, HD])
        B = [ctx.enter_context(nc.psum_tensor(f"chunk{n}", [P, 512], F32)) for n in range(8)]
        pv = lambda b: B[b][:, 0:PR * CH].rearrange("p (i c) -> p i c", c=CH)
        pv2 = lambda b: B[b][:, PR * CH:2 * PR * CH].rearrange("p (i c) -> p i c", c=CH)
        const_in, state_set = sem("ch_const"), sem("ch_state_set")
        passed_pe, passed_act = sem("ch_passed_pe"), sem("ch_passed_act")
        V = Steps(sem("ch_dve"), ["stage_k", "stage_b", "keep_state", "na", "xd", "md", "xl", "arb", "r1", "r2", "r3", "td", "q1", "q2", "tt", "state"])
        A = Steps(sem("ch_act"), ["stage_kq", "stage_rq", "vk", "bt", "p2", "p4", "tdt", "zt", "w", "nu", "y"])
        G = Steps(sem("ch_pool"), ["stage_v", "stage_end"])
        E = Steps(sem("ch_pe"), ["kk", "bb", "tok", "p2", "p4", "p8", "r2", "r3", "td", "tdt", "zt", "q1", "q2", "tt", "w", "u", "y", "state"])
        AA, AB, S2, SO = sem("ch_sample_pe"), sem("ch_sample_dve"), sem("ch_sample_state"), sem("ch_out")
        block = ctx.enter_context(nc.Block())
        heads = [(i, slice(h * HD, (h + 1) * HD)) for i in range(PR) for h in range(2)]

        def col(i, c):
            return sb.prc[:, i, bass.ds(1 + c * CH, CH)]

        @block.sync
        def _(sp):
            sp.dma_start(eye[:, :], io["eye2"]).then_inc(const_in, 16)
            sp.dma_start(masks[:, :, :, :, :], io["chunk_masks"]).then_inc(const_in, 16)
            sp.dma_start(s0[:, :, :, :], io["state_wkv"]).then_inc(const_in, 16)
            sp.dma_start(tmask[:, :, :], io["seq_mask"]).then_inc(const_in, 16)
            sp.wait_ge(V.sem, V.at("state", NCH - 1))
            sp.dma_start(io["wkv_new_prompt"], state[:, :, :]).then_inc(SO, 16)
            sp.wait_ge(S2, 2 * PR)
            sp.dma_start(io["wkv_new_sample"], s0[:, :, :, :]).then_inc(SO, 16)
            sp.wait_ge(SO, 32)

        @block.gpsimd
        def _(pool):
            def stage(c, first):
                if not first:
                    pool.wait_ge(E.sem, E.at("tok", c - 1))
                    pool.wait_ge(V.sem, V.at("keep_state", c - 1))
                    pool.wait_ge(V.sem, V.at("state", c - 1))
                G.did(nc.gpsimd.tensor_copy(vs[:, :, :], sb.prc[:, V0:V0 + PR, bass.ds(1 + c * CH, CH)]), "stage_v")
                G.did(nc.gpsimd.tensor_copy(end[:, :], sb.ends[:, bass.ds(c, 1), :].rearrange("p o i -> p (o i)")), "stage_end")
            stage(0, True)
            with pool.Fori(1, NCH + 1) as c:
                stage(c, False)

        @block.scalar
        def _(act):
            def chunk(c, first=False, sample=False):
                at = lambda s, name: act.wait_ge(s.sem, s.at(name, c))
                if not first:
                    act.wait_ge(E.sem, E.at("y", c - 1))
                    act.wait_ge(E.sem, E.at("state", c - 1))
                    act.sem_inc(passed_act, 1)
                A.did(nc.scalar.activation(kr[:, :, 0, :], sb.kq[:, :, bass.ds(c * CH, CH)], ACT.Copy), "stage_kq")
                A.did(nc.scalar.activation(kr[:, :, 1, :], sb.prc[:, R0:R0 + PR, bass.ds(1 + c * CH, CH)], ACT.Copy), "stage_rq")
                at(E, "tok")
                A.did(nc.scalar.activation(vk[:, :, :, :], B[2][:, 0:2 * PR * CH], ACT.Copy), "vk")
                at(V, "md")
                A.did(nc.scalar.activation(bt[:, :, :], pv(3), ACT.Copy), "bt")
                at(E, "p2")
                A.did(nc.scalar.activation(p2[:, :, :, :], B[4][:, 0:2 * PR * CH], ACT.Copy), "p2")
                at(E, "p4")
                A.did(nc.scalar.activation(p4[:, :, :, :], B[5][:, 0:2 * PR * CH], ACT.Copy), "p4")
                at(E, "tdt")
                A.did(nc.scalar.activation(tdt[:, :, :], pv(4), ACT.Copy), "tdt")
                at(E, "zt")
                A.did(nc.scalar.activation(zt[:, :, :], pv(5), ACT.Copy), "zt")
                at(E, "w")
                if sample:
                    act.wait_ge(AB, 2 * PR + 1)
                    A.did(nc.scalar.activation(w[:, :, :], w0[:, :, :], ACT.Copy), "w")
                else:
                    A.did(nc.scalar.activation(w[:, :, :], pv(5), ACT.Copy), "w")
                at(E, "u")
                A.did(nc.scalar.activation(nu[:, :, :], pv(4), ACT.Copy, scale=-1.0), "nu")
                at(E, "y")
                act.sem_inc(passed_act, 1)
                A.did(nc.scalar.activation(sb.prc[:, R0:R0 + PR, bass.ds(1 + c * CH, CH)], pv(6), ACT.Copy), "y")
            chunk(0, first=True)
            with act.Fori(1, NCH) as c:
                chunk(c)
            chunk(NCH, sample=True)

        @block.vector
        def _(dve):
            def chunk(c, first=False, sample=False):
                at = lambda s, name: dve.wait_ge(s.sem, s.at(name, c))
                m = masks[:, int(sample), :, :, :]
                if not first:
                    dve.wait_ge(E.sem, E.at("tok", c - 1))
                V.did(nc.vector.tensor_copy(kh[:, :, :], sb.prc[:, K0:K0 + PR, bass.ds(1 + c * CH, CH)]), "stage_k")
                V.did(nc.vector.tensor_copy(bh[:, :, :], sb.bh[:, :, bass.ds(c * CH, CH)]), "stage_b")
                at(G, "stage_end")
                if not first:
                    dve.wait_ge(V.sem, V.at("state", c - 1))
                for i in range(PR):
                    last = nc.vector.tensor_scalar(state2[:, i, :], state[:, i, :], end[:, i:i + 1], None, ALU.mult)
                V.did(last, "keep_state")
                at(E, "kk")
                nc.vector.tensor_tensor(na[:, :, 0, :], B[0][:, 0:2 * PR * CH].rearrange("p (i a c) -> p i a c", a=2, c=CH)[:, :, 0, :],
                                        m[:, 0, :, :], ALU.mult)
                V.did(nc.vector.tensor_tensor(na[:, :, 1, :], B[0][:, 0:2 * PR * CH].rearrange("p (i a c) -> p i a c", a=2, c=CH)[:, :, 1, :],
                                              m[:, 1, :, :], ALU.mult), "na")
                bx = B[1][:, 0:2 * PR * CH].rearrange("p (i a c) -> p i a c", a=2, c=CH)
                at(E, "tok")
                V.did(nc.vector.tensor_tensor(xd[:, :, :], bx[:, :, 0, :], m[:, 2, :, :], ALU.mult), "xd")
                V.did(nc.vector.tensor_tensor(md[:, :, :], pv2(3), m[:, 4, :, :], ALU.mult), "md")
                V.did(nc.vector.tensor_tensor(xl[:, :, :], bx[:, :, 0, :], m[:, 3, :, :], ALU.mult), "xl")
                V.did(nc.vector.tensor_tensor(arb[:, :, :], bx[:, :, 1, :], m[:, 1, :, :], ALU.mult), "arb")
                at(E, "p8")
                for i in range(PR):
                    last = nc.vector.tensor_tensor(r1[:, i, :], pv(4)[:, i, :], eye[:, :], ALU.add)
                V.did(last, "r1")
                for name, bank, dst, base, op in (("r2", 5, r2, r1, ALU.add), ("r3", 4, r3, r2, ALU.add), ("td", 5, td, r3, ALU.subtract),
                                                  ("q1", 4, q1, td, ALU.subtract), ("q2", 5, q2, td, ALU.subtract), ("tt", 4, tt, td, ALU.subtract)):
                    at(E, name)
                    dve.wait_ge(V.sem, V.at("td" if name in ("q1", "q2", "tt") else {"r2": "r1", "r3": "r2", "td": "r3"}[name], c))
                    V.did(nc.vector.tensor_tensor(dst[:, :, :], base[:, :, :], pv(bank), op), name)
                if sample:
                    for i in range(PR):
                        dve.wait_ge(AA, i + 1)
                        nc.vector.tensor_tensor(spread[:, :, :], B[(6, 7, 0)[i]][:, :].rearrange("p (b v) -> p b v", v=HD), tmask[:, :, :],
                                                ALU.mult).then_inc(AB, 1)
                        dve.wait_ge(AB, 2 * i + 1)
                        nc.vector.tensor_reduce(w0[:, i, :], spread[:, :, :].rearrange("p b v -> p v b"), AX.X, ALU.add).then_inc(AB, 1)
                        dve.wait_ge(AB, 2 * i + 2)
                    at(E, "w")
                    nc.vector.tensor_tensor(w0[:, :, :], w0[:, :, :], pv(5), ALU.add).then_inc(AB, 1)
                    at(A, "nu")
                    at(A, "vk")
                    for i in range(PR):
                        if i:
                            dve.wait_ge(AA, PR + i)
                        for src, dst in ((vk[:, 0, i, :], vm), (nu[:, i, :], um)):
                            nc.vector.tensor_tensor(dst[:, :, :], src.unsqueeze(1).to_broadcast([P, DB, HD]), tmask[:, :, :],
                                                    ALU.mult).then_inc(AB, 1)
                        dve.wait_ge(AA, PR + i + 1)
                        nc.vector.tensor_tensor(s0[:, i, :, :], s0[:, i, :, :], B[(7, 0, 1)[i]][:, :].rearrange("p (b v) -> p b v", v=HD),
                                                ALU.add).then_inc(S2, 1)
                        dve.wait_ge(S2, 2 * i + 1)
                        nc.vector.tensor_tensor(s0[:, i, :, :], s0[:, i, :, :],
                                                sb.ends[:, NCH:NCH + DB, i].unsqueeze(2).to_broadcast([P, DB, HD]), ALU.mult).then_inc(S2, 1)
                    return
                at(E, "state")
                for i in range(PR):
                    last = nc.vector.scalar_tensor_tensor(state[:, i, :], pv(7)[:, i, :], end[:, i:i + 1], state2[:, i, :], ALU.mult, ALU.add)
                V.did(last, "state")
            nc.vector.memset(state[:, :, :], 0.0).then_inc(state_set, 1)
            dve.wait_ge(const_in, 64)
            dve.wait_ge(state_set, 1)
            chunk(0, first=True)
            with dve.Fori(1, NCH) as c:
                chunk(c)
            chunk(NCH, sample=True)

        @block.tensor
        def _(pe):
            def mm(out, lhs, rhs, **kw):
                kw = dict(start=True, stop=True) | kw
                return nc.tensor.matmul(out, lhs, rhs, **kw)

            def each(name, f):
                for i, r in heads:
                    last = f(i, r)
                E.did(last, name)

            def chunk(c, first=False, sample=False):
                def at(s, name):
                    pe.wait_ge(s.sem, s.at(name, c))
                    pe.sem_inc(passed_pe, 1)
                at(A, "stage_rq")
                at(V, "stage_b")
                b2 = lambda b, i, r: B[b][r, i * 2 * CH:(i + 1) * 2 * CH]
                each("kk", lambda i, r: mm(b2(0, i, r), kh[r, i, :], kr[r, i, :, :]))
                each("bb", lambda i, r: mm(b2(1, i, r), bh[r, i, :], kr[r, i, :, :]))
                at(G, "stage_v")
                for i, r in heads:
                    mm(pv(2)[r, i, :], vs[r, i, :], eye[r, :])
                    mm(pv2(2)[r, i, :], kh[r, i, :], eye[r, :])
                    mm(pv(3)[r, i, :], bh[r, i, :], eye[r, :])
                    last = mm(pv2(3)[r, i, :], kr[r, i, 0, :], bh[r, i, :])
                E.did(last, "tok")
                at(V, "md")
                for i, r in heads:
                    mm(pv(4)[r, i, :], md[r, i, :], xd[r, i, :])
                    last = mm(pv2(4)[r, i, :], xd[r, i, :], md[r, i, :])
                E.did(last, "p2")
                at(A, "p2")
                for i, r in heads:
                    mm(pv(5)[r, i, :], p2[r, 1, i, :], p2[r, 0, i, :])
                    last = mm(pv2(5)[r, i, :], p2[r, 0, i, :], p2[r, 1, i, :])
                E.did(last, "p4")
                at(A, "p4")
                each("p8", lambda i, r: mm(pv(4)[r, i, :], p4[r, 1, i, :], p4[r, 0, i, :]))
                at(V, "r1")
                each("r2", lambda i, r: mm(pv(5)[r, i, :], p4[r, 1, i, :], r1[r, i, :]))
                at(V, "r2")
                each("r3", lambda i, r: mm(pv(4)[r, i, :], p2[r, 1, i, :], r2[r, i, :]))
                at(V, "r3")
                each("td", lambda i, r: mm(pv(5)[r, i, :], md[r, i, :], r3[r, i, :]))
                at(V, "td")
                each("tdt", lambda i, r: mm(pv(4)[r, i, :], td[r, i, :], eye[r, :]))
                at(A, "tdt")
                each("zt", lambda i, r: mm(pv(5)[r, i, :], xl[r, i, :], tdt[r, i, :]))
                at(A, "zt")
                each("q1", lambda i, r: mm(pv(4)[r, i, :], zt[r, i, :], td[r, i, :]))
                at(V, "q1")
                each("q2", lambda i, r: mm(pv(5)[r, i, :], zt[r, i, :], q1[r, i, :]))
                at(V, "q2")
                each("tt", lambda i, r: mm(pv(4)[r, i, :], zt[r, i, :], q2[r, i, :]))
                at(V, "keep_state")
                if sample:
                    pe.wait_ge(A.sem, A.at("y", c - 1))
                    for i in range(PR):
                        for h in range(2):
                            r = slice(h * HD, (h + 1) * HD)
                            last = mm(B[(6, 7, 0)[i]][r, :], kr[r, i, 0, :], s0[r, i, :, :])
                        last.then_inc(AA, 1)
                    each("w", lambda i, r: mm(pv(5)[r, i, :], na[r, i, 0, :], vk[r, 0, i, :]))
                else:
                    for i, r in heads:
                        mm(pv(5)[r, i, :], kr[r, i, 0, :], state[r, i, :], stop=False)
                        last = mm(pv(5)[r, i, :], na[r, i, 0, :], vk[r, 0, i, :], start=False)
                    E.did(last, "w")
                at(V, "tt")
                at(A, "w")
                each("u", lambda i, r: mm(pv(4)[r, i, :], tt[r, i, :], w[r, i, :]))
                at(A, "nu")
                if sample:
                    pe.wait_ge(AB, 2 * PR)
                for i, r in heads:
                    mm(pv(6)[r, i, :], vk[r, 0, i, :], na[r, i, 1, :], stop=False, skip_group_check=sample)
                    last = mm(pv(6)[r, i, :], nu[r, i, :], arb[r, i, :], start=False, stop=sample, skip_group_check=sample)
                    if sample:
                        for b in range(DB):
                            s = slice(b * SW + 1, (b + 1) * SW)
                            last = mm(pv(6)[r, i, s], s0[r, i, b, :], kr[r, i, 1, s], start=False, skip_group_check=True)
                    else:
                        last = mm(pv(6)[r, i, :], state[r, i, :], kr[r, i, 1, :], start=False)
                E.did(last, "y")
                if sample:
                    for i in range(PR):
                        pe.wait_ge(AB, 2 * PR + 1 + 2 * (i + 1))
                        for h in range(2):
                            r = slice(h * HD, (h + 1) * HD)
                            mm(B[(7, 0, 1)[i]][r, :], vk[r, 1, i, :], vm[r, :, :], stop=False)
                            last = mm(B[(7, 0, 1)[i]][r, :], bt[r, i, :], um[r, :, :], start=False)
                        last.then_inc(AA, 1)
                    return
                for i, r in heads:
                    mm(pv(7)[r, i, :], vk[r, 1, i, :], vk[r, 0, i, :], stop=False)
                    last = mm(pv(7)[r, i, :], bt[r, i, :], nu[r, i, :], start=False)
                E.did(last, "state")
            pe.wait_ge(const_in, 64)
            chunk(0, first=True)
            with pe.Fori(1, NCH) as c:
                chunk(c)
            chunk(NCH, sample=True)


def finish_rwkv(nc, io, sb):
    with ExitStack() as ctx:
        t = lambda name, shape: ctx.enter_context(nc.sbuf_tensor(name, shape, F32))
        sem = lambda name: ctx.enter_context(nc.semaphore(name))
        R0, GA = 2 * CT, NT - 1
        pieces = [(0, 512), (512, 512), (1024, SC - 1024)]
        par = sb.rwkv_par
        g_up, rs, sq = t("g_up", [P, RH * HD]), t("gn_rstd", [P, SC]), t("gn_sq", [P, SC])
        m, g = t("head_mean", [P, P]), t("gate", [P, SC])
        b1 = [ctx.enter_context(nc.psum_tensor(f"gn_a{n}", [P, 512], F32)) for n in range(3)]
        b2 = [ctx.enter_context(nc.psum_tensor(f"gn_b{n}", [P, 512], F32)) for n in range(3)]
        const_in, sig, mset = sem("gn_const"), sem("gn_sig"), sem("gn_mset")
        V = Steps(sem("gn_dve"), ["centre", "recip", "norm", "affine", "bonus", "gated"])
        A = Steps(sem("gn_act"), ["gate", "sq", "root"])
        E = Steps(sem("gn_pe"), ["mean", "gate", "var"])
        block = ctx.enter_context(nc.Block())

        @block.sync
        def _(sp):
            sp.dma_start(g_up[:, :], io["g_up"]).then_inc(const_in, 16)
            sp.wait_ge(const_in, 16)

        @block.vector
        def _(dve):
            nc.vector.tensor_scalar(m[:, :], sb.head_sum[:, :], 1.0 / HD, None, ALU.mult).then_inc(mset, 1)
            for i in range(PR):
                y, bv = sb.prc[:, R0 + i, 1:PW], sb.prc[:, i, 1:PW]
                own = lambda name: dve.wait_ge(V.sem, V.at(name, i))
                dve.wait_ge(E.sem, E.at("mean", i))
                for n, (lo, size) in enumerate(pieces):
                    last = nc.vector.tensor_tensor(y[:, lo:lo + size], y[:, lo:lo + size], b1[n][:, 0:size], ALU.subtract)
                V.did(last, "centre")
                dve.wait_ge(A.sem, A.at("root", i))
                V.did(nc.vector.reciprocal(rs[:, :], rs[:, :]), "recip")
                own("recip")
                V.did(nc.vector.tensor_tensor(y, y, rs[:, :], ALU.mult), "norm")
                own("norm")
                V.did(nc.vector.tensor_scalar(y, y, par[:, i, 5:6], par[:, i, 6:7], ALU.mult, ALU.add), "affine")
                own("affine")
                V.did(nc.vector.tensor_tensor(y, y, bv, ALU.add), "bonus")
                own("bonus")
                nc.vector.tensor_tensor(sb.mix[:, CT + i, 0:SEQ], y[:, 0:SEQ], g[:, 0:SEQ], ALU.mult)
                seq = lambda x: x[:, SEQ:SEQ + DB * SW].rearrange("p (b s) -> p b s", s=SW)[:, :, 1:SW]
                V.did(nc.vector.tensor_tensor(sb.mix[:, CT + i, SEQ:T].rearrange("p (b s) -> p b s", s=DS), seq(y), seq(g),
                                              ALU.mult), "gated")

        @block.scalar
        def _(act):
            nc.scalar.activation(sb.prc[:, GA, 1:PW], sb.prc[:, GA, 1:PW], ACT.Sigmoid).then_inc(sig, 1)
            for i in range(PR):
                if i:
                    act.wait_ge(V.sem, V.at("gated", i - 1))
                act.wait_ge(E.sem, E.at("gate", i))
                for n, (lo, size) in enumerate(pieces):
                    last = nc.scalar.activation(g[:, lo:lo + size], b2[n][:, 0:size], ACT.Copy)
                A.did(last, "gate")
                act.wait_ge(V.sem, V.at("centre", i))
                A.did(nc.scalar.activation(sq[:, :], sb.prc[:, R0 + i, 1:PW], ACT.Square), "sq")
                act.wait_ge(E.sem, E.at("var", i))
                for n, (lo, size) in enumerate(pieces):
                    last = nc.scalar.activation(rs[:, lo:lo + size], b1[n][:, 0:size], ACT.Sqrt, bias=sb.eps[:, 2:3])
                A.did(last, "root")

        @block.tensor
        def _(pe):
            pe.wait_ge(mset, 1)
            for i in range(PR):
                y = sb.prc[:, R0 + i, 1:PW]
                if i:
                    pe.wait_ge(A.sem, A.at("root", i - 1))
                for n, (lo, size) in enumerate(pieces):
                    last = nc.tensor.matmul(b1[n][:, 0:size], m[:, :], y[:, lo:lo + size], start=True, stop=True)
                E.did(last, "mean")
                pe.wait_ge(const_in, 16)
                pe.wait_ge(sig, 1)
                for n, (lo, size) in enumerate(pieces):
                    last = nc.tensor.matmul(b2[n][:, 0:size], g_up[:, i * P:(i + 1) * P], sb.prc[:, GA, 1 + lo:1 + lo + size],
                                            start=True, stop=True)
                E.did(last, "gate")
                pe.wait_ge(A.sem, A.at("sq", i))
                for n, (lo, size) in enumerate(pieces):
                    last = nc.tensor.matmul(b1[n][:, 0:size], m[:, :], sq[:, lo:lo + size], start=True, stop=True)
                E.did(last, "var")


def attend_sample(nc, io, sb):
    NK = NPG + 1
    HQ = AH * DS
    with ExitStack() as ctx:
        t = lambda name, shape, dt=F32: ctx.enter_context(nc.sbuf_tensor(name, shape, dt))
        sem = lambda name: ctx.enter_context(nc.semaphore(name))
        kp, vp = t("k_pages", [P, 2, NPG, ATT]), t("v_pages", [P, 2, NPG, ATT])
        pages, row, rows = t("pages", [P, DB * NPG], mybir.dt.int32), t("row", [P, 1]), t("page_rows", [P, 2, NPG], U32)
        kn, vn = t("k_own", [P, PA, P]), t("v_own", [P, ATT])
        kt, qd = t("k_turned", [P, 3, ATT]), t("q_diag", [P, 2, PA, 2, DS])
        bias, seen, cap = t("s_bias", [P, NK * HQ]), t("s_seen", [P, DB, HQ]), t("s_cap", [P, DB, HQ])
        tri, ones, ident = t("s_tri", [P, P]), t("s_ones", [P, P]), t("s_ident", [P, P])
        zb, w, suf, a = t("s_logit", [P, NK * HQ]), t("s_soft", [P, NK * HQ]), t("s_suffix", [P, NPG * HQ]), t("s_weight", [P, NK * HQ])
        turn = [ctx.enter_context(nc.psum_tensor(f"s_turn{n}", [P, 512], F32)) for n in range(3)]
        zp = [ctx.enter_context(nc.psum_tensor(f"s_z{n}", [P, 512], F32)) for n in range(2)]
        rp, op = (ctx.enter_context(nc.psum_tensor(n, [P, 512], F32)) for n in ("s_later", "s_out"))
        const_in, own_set, gathered = sem("s_const"), sem("s_own"), [sem(f"s_gathered{n}") for n in range(2)]
        turned, kept, z_done = sem("s_turned"), sem("s_kept"), sem("s_z_done")
        V = Steps(sem("s_dve"), ["rows", "q", "logit", "min", "soft", "seen", "suf"] + [f"suf{n}" for n in range(NPG - 1)]
                  + ["diff", "cap"])
        A = Steps(sem("s_act"), ["exp", "ln", "weight", "out"])
        E = Steps(sem("s_pe"), ["later", "out"])
        passed, passed_pool = sem("s_passed"), sem("s_passed_pool")
        block = ctx.enter_context(nc.Block())

        @block.sync
        def _(sp):
            for dst, src in ((pages, "pages"), (row, "row"), (bias, "sample_bias"), (tri, "tri"), (ones, "ones"), (ident, "ident")):
                sp.dma_start(dst[:, :], io[src]).then_inc(const_in, 16)
            for dst, src in ((seen, "sample_seen"), (cap, "sample_cap")):
                sp.dma_start(dst[:, :, :], io[src]).then_inc(const_in, 16)
            sp.wait_ge(const_in, 128)

        @block.gpsimd
        def _(pool):
            with pool.Fori(0, DB // 2) as i:
                for s in range(2):
                    b = 2 * i + s
                    pool.wait_ge(V.sem, V.at("rows", b))
                    pool.wait_ge(passed, b + 1)
                    pool.sem_inc(passed_pool, 1)
                    for dst, src in ((kp, "cache_k"), (vp, "cache_v")):
                        for g in range(NPG):
                            pool.indirect_dma_start(out=dst[:, s, g, :], out_offset=None, in_=io[src],
                                                    in_offset=bass.IndirectOffsetOnAxis(ap=rows[:, s, g:g + 1], axis=0))\
                                .then_inc(gathered[s], 16)

        @block.vector
        def _(dve):
            nc.vector.memset(kn[:, :, :], 0.0).then_inc(own_set, 1)
            nc.vector.memset(vn[:, :], 0.0).then_inc(own_set, 1)
            nc.vector.memset(qd[:, :, :, :, :], 0.0).then_inc(own_set, 1)
            dve.wait_ge(own_set, 3)
            nc.vector.tensor_copy(kn[:, :, 0:NS], sb.qk[:, PA:2 * PA, SEQ:T]).then_inc(own_set, 1)
            nc.vector.tensor_copy(vn[0:NS, :], sb.vtok[0:NS, NBLK - 1, :]).then_inc(own_set, 1)
            dve.wait_ge(const_in, 128)

            def prepare(b, s):
                V.did(nc.vector.tensor_scalar(rows[:, s, :], pages[:, bass.ds(b * NPG, NPG)], float(PAGE), row[:, 0:1],
                                              ALU.mult, ALU.add), "rows")
                for h in range(2):
                    r = slice(h * HD, (h + 1) * HD)
                    last = nc.vector.tensor_copy(qd[r, s, :, h, :], sb.qk[r, 0:PA, bass.ds(SEQ + b * DS, DS)])
                V.did(last, "q")

            with dve.Fori(0, DB // 2) as i:
                for s in range(2):
                    b = 2 * i + s
                    own = lambda name: dve.wait_ge(V.sem, V.at(name, b))
                    dve.wait_ge(passed, b + 1)
                    prepare(b, s)
                    for g in range(NPG):
                        dve.wait_ge(turned, b * NPG + g + 1)
                        nc.vector.tensor_copy(kt[:, g % 3, :], turn[g % 3][:, 0:ATT]).then_inc(kept, 1)
                    dve.wait_ge(z_done, b + 1)
                    V.did(nc.vector.scalar_tensor_tensor(zb[:, :], zp[s][:, 0:NK * HQ], HD ** -0.5, bias[:, :], ALU.mult, ALU.add), "logit")
                    own("logit")
                    V.did(nc.vector.tensor_scalar(w[:, :], zb[:, :], 40.0, None, ALU.min), "min")
                    dve.wait_ge(A.sem, A.at("ln", b))
                    V.did(nc.vector.tensor_tensor(w[:, :], w[:, :], zb[:, :], ALU.max), "soft")
                    own("soft")
                    last_page = slice(NPG * HQ, NK * HQ)
                    V.did(nc.vector.tensor_tensor(w[:, last_page], w[:, last_page], seen[:, bass.ds(b, 1), :].rearrange("p o q -> p (o q)"),
                                                  ALU.mult), "seen")
                    own("seen")
                    V.did(nc.vector.tensor_copy(suf[:, (NPG - 1) * HQ:], w[:, last_page]), "suf")
                    own("suf")
                    for n in range(NPG - 1):
                        g = NPG - 2 - n
                        V.did(nc.vector.tensor_tensor(suf[:, g * HQ:(g + 1) * HQ], suf[:, (g + 1) * HQ:(g + 2) * HQ],
                                                      w[:, (g + 1) * HQ:(g + 2) * HQ], ALU.add), f"suf{n}")
                        own(f"suf{n}")
                    dve.wait_ge(E.sem, E.at("later", b))
                    V.did(nc.vector.tensor_tensor(a[:, :], zb[:, :], rp[:, 0:NK * HQ], ALU.subtract), "diff")
                    own("diff")
                    V.did(nc.vector.tensor_tensor(a[:, last_page], a[:, last_page], cap[:, bass.ds(b, 1), :].rearrange("p o q -> p (o q)"),
                                                  ALU.min), "cap")

        @block.scalar
        def _(act):
            with act.Fori(0, DB // 2) as i:
                for s in range(2):
                    b = 2 * i + s
                    act.wait_ge(V.sem, V.at("min", b))
                    A.did(nc.scalar.activation(w[:, :], w[:, :], ACT.Exp), "exp")
                    act.wait_ge(A.sem, A.at("exp", b))
                    A.did(nc.scalar.activation(w[:, :], w[:, :], ACT.Ln, bias=1.0), "ln")
                    act.wait_ge(V.sem, V.at("cap", b))
                    A.did(nc.scalar.activation(a[:, :], a[:, :], ACT.Exp), "weight")
                    act.wait_ge(E.sem, E.at("out", b))
                    act.sem_inc(own_set, 1)
                    for h in range(2):
                        r = slice(h * HD, (h + 1) * HD)
                        last = nc.scalar.activation(sb.mix[r, DC - PA:DC, bass.ds(SEQ + b * DS, DS)],
                                                    op[r, 0:HQ].rearrange("p (i h q) -> p i h q", h=2, q=DS)[:, :, h, :], ACT.Copy)
                    A.did(last, "out")

        @block.tensor
        def _(pe):
            pe.sem_inc(passed, 2)
            pe.wait_ge(const_in, 128)
            pe.wait_ge(own_set, 5)
            with pe.Fori(0, DB // 2) as i:
                for s in range(2):
                    b = 2 * i + s
                    pe.wait_ge(gathered[s], 16 * 2 * NPG * (i + 1))
                    pe.wait_ge(V.sem, V.at("q", b))
                    for g in range(NK):
                        if g < NPG:
                            if g >= 3:
                                pe.wait_ge(kept, b * NPG + g - 3 + 1)
                            for j in range(PA):
                                last = nc.tensor.transpose(turn[g % 3][:, j * P:(j + 1) * P], kp[:, s, g, j * P:(j + 1) * P], ident[:, :])
                            last.then_inc(turned, 1)
                        if g:
                            pe.wait_ge(kept, b * NPG + g)
                            for j in range(PA):
                                nc.tensor.matmul(zp[s][:, (g - 1) * HQ + j * 2 * DS:(g - 1) * HQ + (j + 1) * 2 * DS],
                                                 kt[:, (g - 1) % 3, j * P:(j + 1) * P], qd[:, s, j, :, :], start=True, stop=True)
                    for j in range(PA):
                        last = nc.tensor.matmul(zp[s][:, NPG * HQ + j * 2 * DS:NPG * HQ + (j + 1) * 2 * DS],
                                                kn[:, j, :], qd[:, s, j, :, :], start=True, stop=True)
                    last.then_inc(z_done, 1)
                    pe.wait_ge(V.sem, V.at(f"suf{NPG - 2}", b))
                    nc.tensor.matmul(rp[:, 0:NK * HQ], tri[:, :], w[:, :], start=True, stop=False, skip_group_check=True)
                    E.did(nc.tensor.matmul(rp[:, 0:NPG * HQ], ones[:, :], suf[:, :], start=False, stop=True, skip_group_check=True), "later")
                    pe.wait_ge(A.sem, A.at("weight", b))
                    for j in range(PA):
                        for g in range(NK):
                            lhs = vn[:, j * P:(j + 1) * P] if g == NPG else vp[:, s, g, j * P:(j + 1) * P]
                            last = nc.tensor.matmul(op[:, j * 2 * DS:(j + 1) * 2 * DS], lhs,
                                                    a[:, g * HQ + j * 2 * DS:g * HQ + (j + 1) * 2 * DS], start=g == 0, stop=g == NK - 1)
                    E.did(last, "out")
                    pe.wait_ge(A.sem, A.at("out", b))
                    pe.sem_inc(passed, 1)


def close_mixer(nc, io, sb):
    with ExitStack() as ctx:
        t = lambda name, shape: ctx.enter_context(nc.sbuf_tensor(name, shape, F32))
        sem = lambda name: ctx.enter_context(nc.semaphore(name))
        wo, x, h2, h2t = t("w_out", [P, DC, D]), t("x_rows", [P, 2, D]), t("h2_rows", [P, 2, D]), t("h2_turned", [P, 2, DC, P])
        g2, junk, ident = t("g2", [P, D]), t("close_junk", [P, D]), t("close_ident", [P, P])
        ssq, rstd = t("ssq", [P, 2]), t("close_rstd", [P, 2])
        Y = [[ctx.enter_context(nc.psum_tensor(f"close_y{s}{n}", [P, 512], F32)) for n in range(2)] for s in range(2)]
        TR = [[ctx.enter_context(nc.psum_tensor(f"close_t{s}{n}", [P, 512], F32)) for n in range(2)] for s in range(2)]
        const_in, pad_set = sem("cl_const"), sem("cl_pad")
        x_in = [sem(f"cl_x_in{s}") for s in range(2)]
        x_out = [sem(f"cl_out{s}") for s in range(2)]
        V = Steps(sem("cl_dve"), ["x0", "x1", "recip", "h2"])
        A = Steps(sem("cl_act"), ["ssq", "root", "t0", "t1"])
        E = Steps(sem("cl_pe"), ["y", "turn"])
        block = ctx.enter_context(nc.Block())

        @block.sync
        def _(sp):
            for c in range(DC):
                sp.dma_start(wo[:, c, :], io["w_out"][:, c, :]).then_inc(const_in, 16)
            sp.dma_start(g2[:, :], io["norm2_g"]).then_inc(const_in, 16)
            sp.dma_start(ident[:, :], io["ident"]).then_inc(const_in, 16)
            for b in range(NBLK + 1):
                if b < NBLK:
                    s = b % 2
                    if b >= 2:
                        sp.wait_ge(x_out[s], 48 * (b // 2))
                    sp.dma_start(x[:, s, :], io["x_rows"][b]).then_inc(x_in[s], 16)
                if b:
                    s = (b - 1) % 2
                    sp.wait_ge(V.sem, V.at("h2", b - 1))
                    sp.dma_start(io["x1"][b - 1], x[:, s, :]).then_inc(x_out[s], 16)
                    sp.dma_start(io["h2"][b - 1], h2[:, s, :]).then_inc(x_out[s], 16)
                    sp.wait_ge(A.sem, A.at("t1", b - 1))
                    sp.dma_start(io["h2t"][b - 1], h2t[:, s, :, :]).then_inc(x_out[s], 16)
            sp.wait_ge(x_out[0], 48 * ((NBLK + 1) // 2))
            sp.wait_ge(x_out[1], 48 * (NBLK // 2))

        @block.vector
        def _(dve):
            nc.vector.memset(sb.mix[:, :, T:], 0.0).then_inc(pad_set, 1)
            dve.wait_ge(const_in, 16 * (DC + 2))
            for b in range(NBLK):
                s = b % 2
                dve.wait_ge(x_in[s], 16 * (b // 2 + 1))
                dve.wait_ge(E.sem, E.at("y", b))
                for n in range(2):
                    V.did(nc.vector.tensor_tensor(x[:, s, n * 512:(n + 1) * 512], x[:, s, n * 512:(n + 1) * 512], Y[s][n][:, :], ALU.add), f"x{n}")
                dve.wait_ge(A.sem, A.at("root", b))
                V.did(nc.vector.reciprocal(rstd[:, s:s + 1], rstd[:, s:s + 1]), "recip")
                dve.wait_ge(V.sem, V.at("recip", b))
                if b >= 2:
                    dve.wait_ge(x_out[s], 48 * (b // 2))
                V.did(nc.vector.scalar_tensor_tensor(h2[:, s, :], x[:, s, :], rstd[:, s:s + 1], g2[:, :], ALU.mult, ALU.mult), "h2")

        @block.scalar
        def _(act):
            for b in range(NBLK):
                s = b % 2
                act.wait_ge(V.sem, V.at("x1", b))
                A.did(nc.scalar.activation(junk[:, :], x[:, s, :], ACT.Square, accum_out=ssq[:, s:s + 1]), "ssq")
                act.wait_ge(A.sem, A.at("ssq", b))
                A.did(nc.scalar.activation(rstd[:, s:s + 1], ssq[:, s:s + 1], ACT.Sqrt, bias=sb.eps[:, 0:1], scale=1.0 / D), "root")
                act.wait_ge(E.sem, E.at("turn", b))
                for n in range(2):
                    A.did(nc.scalar.activation(h2t[:, s, 4 * n:4 * n + 4, :], TR[s][n][:, :], ACT.Copy), f"t{n}")

        @block.tensor
        def _(pe):
            pe.wait_ge(const_in, 16 * (DC + 2))
            pe.wait_ge(pad_set, 1)

            def turn(b):
                s = b % 2
                pe.wait_ge(V.sem, V.at("h2", b))
                if b >= 2:
                    pe.wait_ge(A.sem, A.at("t1", b - 2))
                    pe.wait_ge(x_out[s], 48 * (b // 2))
                for c in range(DC):
                    last = nc.tensor.transpose(TR[s][c // 4][:, c % 4 * P:(c % 4 + 1) * P], h2[:, s, c * P:(c + 1) * P], ident[:, :])
                E.did(last, "turn")

            for b in range(NBLK):
                s = b % 2
                if b >= 2:
                    pe.wait_ge(V.sem, V.at("x1", b - 2))
                for n in range(2):
                    for c in range(DC):
                        last = nc.tensor.matmul(Y[s][n][:, :], sb.mix[:, c, b * P:(b + 1) * P], wo[:, c, n * 512:(n + 1) * 512],
                                                start=c == 0, stop=c == DC - 1)
                E.did(last, "y")
                turn(b)


def peer(nc, io, sb):
    RING = 8
    BH = PH * TOPK
    HN = 2 * KEYS
    LOW = -3.0e38
    with ExitStack() as ctx:
        t = lambda name, shape, dt=F32: ctx.enter_context(nc.sbuf_tensor(name, shape, dt))
        sem = lambda name: ctx.enter_context(nc.semaphore(name))
        wk = t("wk", [P, DC, PH * HN])
        u, v = t("u_rows", [P, RING, D]), t("v_rows", [P, RING, D])
        h2, h2t, x1 = t("p_h2", [P, 2, D]), t("p_h2t", [P, 2, DC, P]), t("p_x1", [P, 2, D])
        gf, ident, iota = t("final_g", [P, D]), t("p_ident", [P, P]), t("iota", [P, TOPK])
        sc, work = t("scores", [P, 2, 2, KEYS]), t("scores_left", [P, KEYS])
        best, where, wheref = t("best", [P, 2, TOPK]), t("where", [P, 2, TOPK], U32), t("where_f", [P, 2, TOPK])
        cand, left = t("cand", [P, TOPK, TOPK]), t("cand_left", [P, TOPK * TOPK])
        top, pos = t("top", [P, TOPK]), t("pos", [P, TOPK], U32)
        part, partf = t("pos_part", [P, 2, TOPK], U32), t("pos_part_f", [P, 2, TOPK])
        same, pick = t("same", [P, TOPK, TOPK]), t("pick", [P, 2, TOPK])
        expert, gate = t("expert", [P, 2, PH, TOPK], U32), t("p_gate", [P, 2, PH, TOPK])
        neg, expo, esum = t("neg_max", [P, 1]), t("exp_top", [P, TOPK]), t("exp_sum", [P, 1])
        hid, gel, wgt = t("hidden", [P, 2, TOPK]), t("gelu", [P, 2, TOPK]), t("weights", [P, 2, TOPK])
        diag = t("diag", [P, RING, P])
        passed, passed_dve, eps_set = sem("p_passed"), sem("p_passed_dve"), sem("p_eps_set")
        act_junk, small = t("p_act_junk", [P, D]), sem("p_small")
        ssq, rstd = t("p_ssq", [P, 1]), t("p_rstd", [P, 1])
        ps = lambda name: ctx.enter_context(nc.psum_tensor(name, [P, 512], F32))
        Y = [[ps(f"peer_y{s}{n}") for n in range(2)] for s in range(2)]
        S = [ps(f"peer_s{n}") for n in range(2)]
        K = [ps(f"peer_k{n}") for n in range(2)]
        const_in, key_in, wq_in = sem("p_const"), sem("p_key_in"), [sem(f"p_wq_in{n}") for n in range(2)]
        wk_done, wk_kept = sem("wk_done"), sem("wk_kept")
        u_in, v_in = [sem(f"u_in{n}") for n in range(RING)], [sem(f"v_in{n}") for n in range(RING)]
        u_free, v_free = sem("u_free"), sem("v_free")
        h2_in, h2t_in, x1_in = ([sem(f"{n}_{s}") for s in range(2)] for n in ("p_h2_in", "p_h2t_in", "p_x1_in"))
        gelu_done, weights_done, diag_done = sem("gelu_done"), sem("weights_done"), sem("diag_done")
        score_done, score_kept, exps_done = sem("score_done"), sem("score_kept"), sem("exps_done")
        values_done, summed, y_ready, y_out = sem("values_done"), sem("p_summed"), sem("y_ready"), sem("y_out")
        C = Steps(sem("choice"), [n + str(side) for side in range(2) for n in ("max_a", "at_a", "left", "max_b", "at_b")]
                  + ["where_f", "cand", "top_a", "neg", "pos_a", "cand_left", "top_b", "pos_b", "first", "second", "parts_f"]
                  + [n + str(side) for side in range(2) for n in ("same", "marked", "pick")] + ["expert"])
        G = Steps(sem("gates"), ["recip", "gate"])
        F = Steps(sem("final_act"), ["ssq", "root"])
        R = Steps(sem("final_dve"), ["recip"])

        def blocks(eng, body):
            body(0, 0, 0, P)
            with eng.Fori(0, (NBLK - 3) // 2) as i:
                body(2 * i + 1, i, 1, P)
                body(2 * i + 2, i + 1, 0, P)
            body(NBLK - 2, (NBLK - 2) // 2, 1, P)
            body(NBLK - 1, (NBLK - 1) // 2, 0, NS)

        first = lambda b: isinstance(b, int) and b == 0
        last = lambda b: isinstance(b, int) and b == NBLK - 1
        pair = lambda ap: ap.rearrange("p a n -> p (a n)")
        block = ctx.enter_context(nc.Block())
        wq = [pair(u[:, n:n + 1, :]) for n in range(2)]
        keys = pair(v[:, 0:2, :]).rearrange("p (h n) -> p h n", n=KEYS)

        @block.sync
        def _(sp):
            sp.dma_start(keys, io["sub_keys"]).then_inc(key_in, 16)
            for hc in range(2 * PH):
                if hc >= 2:
                    sp.wait_ge(wk_done, 2 * (hc - 1))
                sp.dma_start(wq[hc % 2], io["w_query"][hc]).then_inc(wq_in[hc % 2], 16)
            sp.dma_start(gf[:, :], io["final_g"]).then_inc(const_in, 16)
            sp.dma_start(ident[:, :], io["ident"]).then_inc(const_in, 16)
            sp.dma_start(iota[:, :], io["iota"]).then_inc(const_in, 16)
            sp.dma_start(h2t[:, 0, :, :], io["h2t"][0]).then_inc(h2t_in[0], 16)
            sp.dma_start(h2[:, 0, :], io["h2"][0]).then_inc(h2_in[0], 16)
            sp.dma_start(x1[:, 0, :], io["x1"][0]).then_inc(x1_in[0], 16)

            def body(b, half, s, n):
                o = 1 - s
                row = lambda name, x: io[name][bass.ds(x, 1)]
                if not last(b):
                    if not first(b):
                        sp.wait_ge(score_done, PH * b)
                    sp.dma_start(h2t[:, o, :, :], row("h2t", b + 1).rearrange("o p c n -> p (o c) n")).then_inc(h2t_in[o], 16)
                    if not first(b):
                        sp.wait_ge(u_free, RING + BH * b)
                    sp.dma_start(h2[:, o, :], row("h2", b + 1).rearrange("o p n -> p (o n)")).then_inc(h2_in[o], 16)
                if not first(b):
                    sp.wait_ge(y_ready, b)
                    sp.dma_start(row("y", b - 1).rearrange("o p n -> p (o n)"), x1[:, o, :]).then_inc(y_out, 16)
                    sp.wait_ge(y_out, 16 * b)
                if not last(b):
                    sp.dma_start(x1[:, o, :], row("x1", b + 1).rearrange("o p n -> p (o n)")).then_inc(x1_in[o], 16)
            blocks(sp, body)
            sp.wait_ge(y_ready, NBLK)
            sp.dma_start(io["y"][NBLK - 1, 0:NS, :], x1[0:NS, 0, :]).then_inc(y_out, 16)
            sp.wait_ge(y_out, 16 * NBLK)

        @block.gpsimd
        def _(pool):
            def body(b, half, s, n):
                for h in range(PH):
                    pool.wait_ge(C.sem, C.at("expert", b * PH + h))
                    for rows, table, free, arrived in ((u, "peer_u", u_free, u_in), (v, "peer_v", v_free, v_in)):
                        for m in range(h * TOPK, (h + 1) * TOPK):
                            pool.wait_ge(free, b * BH + m + 1)
                            pool.sem_inc(passed, 1)
                            pool.indirect_dma_start(out=rows[0:n, m % RING, :], out_offset=None, in_=io[table],
                                                    in_offset=bass.IndirectOffsetOnAxis(ap=expert[0:n, s, h, m % TOPK:m % TOPK + 1], axis=0))\
                                .then_inc(arrived[m % RING], 16)
            blocks(pool, body)

        @block.vector
        def _(dve):
            def choose(b, s, h):
                turn = b * PH + h

                def step(name, ins):
                    C.did(ins, name)
                    dve.wait_ge(C.sem, C.at(name, turn))
                    dve.sem_inc(passed_dve, 1)
                dve.wait_ge(score_kept, turn + 1)
                dve.sem_inc(passed_dve, 1)
                lo, hi = slice(0, 8), slice(8, TOPK)
                for side in range(2):
                    x, n = sc[:, h % 2, side, :], str(side)
                    step("max_a" + n, nc.vector.max(best[:, side, lo], x))
                    step("at_a" + n, nc.vector.max_index(where[:, side, lo], best[:, side, lo], x))
                    step("left" + n, nc.vector.match_replace(work[:, :], best[:, side, lo], x, LOW))
                    step("max_b" + n, nc.vector.max(best[:, side, hi], work[:, :]))
                    step("at_b" + n, nc.vector.max_index(where[:, side, hi], best[:, side, hi], work[:, :]))
                step("where_f", nc.vector.tensor_copy(wheref[:, :, :], where[:, :, :]))
                grid = [P, TOPK, TOPK]
                step("cand", nc.vector.tensor_tensor(cand[:, :, :], best[:, 0, :].unsqueeze(2).to_broadcast(grid),
                                                     best[:, 1, :].unsqueeze(1).to_broadcast(grid), ALU.add))
                flat = pair(cand[:, :, :])
                step("top_a", nc.vector.max(top[:, lo], flat))
                step("neg", nc.vector.tensor_scalar(neg[:, :], top[:, 0:1], -1.0, None, ALU.mult))
                step("pos_a", nc.vector.max_index(pos[:, lo], top[:, lo], flat))
                step("cand_left", nc.vector.match_replace(left[:, :], top[:, lo], flat, LOW))
                step("top_b", nc.vector.max(top[:, hi], left[:, :]))
                step("pos_b", nc.vector.max_index(pos[:, hi], top[:, hi], left[:, :]))
                step("first", nc.vector.tensor_scalar(part[:, 0, :], pos[:, :], int(math.log2(TOPK)), None, ALU.logical_shift_right))
                step("second", nc.vector.tensor_scalar(part[:, 1, :], pos[:, :], TOPK - 1, None, ALU.bitwise_and))
                step("parts_f", nc.vector.tensor_copy(partf[:, :, :], part[:, :, :]))
                for side in range(2):
                    n = str(side)
                    step("same" + n, nc.vector.tensor_tensor(same[:, :, :], partf[:, side, :].unsqueeze(2).to_broadcast(grid),
                                                             iota[:, :].unsqueeze(1).to_broadcast(grid), ALU.is_equal))
                    step("marked" + n, nc.vector.tensor_tensor(same[:, :, :], same[:, :, :],
                                                               wheref[:, side, :].unsqueeze(1).to_broadcast(grid), ALU.mult))
                    step("pick" + n, nc.vector.tensor_reduce(pick[:, side, :], same[:, :, :], AX.X, ALU.add))
                step("expert", nc.vector.scalar_tensor_tensor(expert[:, s, h, :], pick[:, 0, :], float(KEYS), pick[:, 1, :],
                                                              ALU.mult, ALU.add))

            def gates(b, s, h):
                turn = b * PH + h
                dve.wait_ge(exps_done, turn + 1)
                G.did(nc.vector.reciprocal(esum[:, :], esum[:, :]), "recip")
                dve.wait_ge(G.sem, G.at("recip", turn))
                G.did(nc.vector.tensor_scalar(gate[:, s, h, :], expo[:, :], esum[:, 0:1], None, ALU.mult), "gate")

            def finish(b, half, s, n):
                dve.wait_ge(values_done, b + 1)
                dve.wait_ge(x1_in[s], 16 * (half + 1))
                for k in range(2):
                    ins = nc.vector.tensor_tensor(x1[0:n, s, k * 512:(k + 1) * 512], x1[0:n, s, k * 512:(k + 1) * 512],
                                                  Y[s][k][0:n, :], ALU.add)
                ins.then_inc(summed, 1)
                dve.wait_ge(F.sem, F.at("root", b))
                R.did(nc.vector.reciprocal(rstd[0:n, :], rstd[0:n, :]), "recip")
                dve.wait_ge(R.sem, R.at("recip", b))
                nc.vector.scalar_tensor_tensor(x1[0:n, s, :], x1[0:n, s, :], rstd[0:n, 0:1], gf[0:n, :], ALU.mult, ALU.mult)\
                    .then_inc(y_ready, 1)

            def body(b, half, s, n):
                o = 1 - s
                dve.wait_ge(h2_in[s], 16 * (half + 1))
                for h in range(PH):
                    turn = b * PH + h
                    if h >= 2 or not first(b):
                        dve.wait_ge(gelu_done, turn - 1)
                    for k in range(TOPK):
                        m = h * TOPK + k
                        dve.wait_ge(u_in[m % RING], 16 * (b * (BH // RING) + m // RING + 1))
                        nc.vector.tensor_tensor_reduce(out=u[0:n, m % RING, :], in0=u[0:n, m % RING, :], in1=h2[0:n, s, :], scale=1.0, scalar=0.0,
                                                       op0=ALU.mult, op1=ALU.add, accum_out=hid[0:n, h % 2, k:k + 1]).then_inc(u_free, 1)
                    if h:
                        if not last(b):
                            gates(b + 1, o, h - 1)
                    elif not first(b):
                        gates(b, s, PH - 1)
                    dve.wait_ge(gelu_done, turn + 1)
                    if h >= 2 or not first(b):
                        dve.wait_ge(diag_done, TOPK * (turn - 1))
                    dve.wait_ge(G.sem, G.at("gate", b * PH + h))
                    nc.vector.tensor_tensor(wgt[0:n, h % 2, :], gel[0:n, h % 2, :], gate[0:n, s, h, :], ALU.mult).then_inc(weights_done, 1)
                    if not last(b):
                        if h == 0 and not first(b):
                            dve.wait_ge(v_free, RING + BH * b)
                        choose(b + 1, o, h)
                    if h == 1 and not first(b):
                        finish(b - 1, half - 1 + s, o, P)

            nc.vector.memset(sb.eps[:, 0:1], RMS_EPS).then_inc(eps_set, 1)
            nc.vector.sem_inc(u_free, RING)
            nc.vector.sem_inc(summed, 2)
            dve.wait_ge(const_in, 48)
            for h in range(PH):
                choose(0, 0, h)
                gates(0, 0, h)
            blocks(dve, body)
            finish(NBLK - 1, (NBLK - 1) // 2, 0, NS)

        @block.scalar
        def _(act):
            def keep(b, h):
                turn = b * PH + h
                act.wait_ge(score_done, turn + 1)
                if not (first(b) and h < 2):
                    act.wait_ge(C.sem, C.at("at_b1", turn - 2))
                nc.scalar.activation(sc[:, h % 2, :, :], S[h % 2][:, 0:HN], ACT.Copy).then_inc(score_kept, 1)

            def exps(b, h):
                turn = b * PH + h
                act.wait_ge(C.sem, C.at("top_b", turn))
                nc.scalar.activation(expo[:, :], top[:, :], ACT.Exp, bias=neg[:, 0:1], accum_out=esum[:, 0:1]).then_inc(exps_done, 1)

            def norm(b, s, n):
                act.wait_ge(summed, b + 3)
                F.did(nc.scalar.activation(act_junk[0:n, :], x1[0:n, s, :], ACT.Square, accum_out=ssq[0:n, 0:1]), "ssq")
                act.wait_ge(F.sem, F.at("ssq", b))
                F.did(nc.scalar.activation(rstd[0:n, :], ssq[0:n, :], ACT.Sqrt, bias=sb.eps[0:n, 0:1], scale=1.0 / D), "root")

            def body(b, half, s, n):
                for h in range(PH):
                    turn = b * PH + h
                    if not last(b):
                        keep(b + 1, h)
                    act.wait_ge(u_free, RING + b * BH + (h + 1) * TOPK)
                    if h >= 2 or not first(b):
                        act.wait_ge(weights_done, turn - 1)
                    nc.scalar.activation(gel[0:n, h % 2, :], hid[0:n, h % 2, :], ACT.Gelu_apprx_tanh).then_inc(gelu_done, 1)
                    act.wait_ge(weights_done, turn + 1)
                    for k in range(TOPK):
                        m = h * TOPK + k
                        act.wait_ge(v_free, b * BH + m + 1)
                        nc.scalar.activation(diag[0:n, m % RING, 0:n], ident[0:n, 0:n], ACT.Copy, scale=wgt[0:n, h % 2, k:k + 1])\
                            .then_inc(diag_done, 1)
                    if not last(b):
                        exps(b + 1, h)
                    if h == 1 and not first(b):
                        norm(b - 1, 1 - s, P)

            for hc in range(2 * PH):
                for j in range(2):
                    act.wait_ge(wk_done, 2 * hc + j + 1)
                    nc.scalar.activation(wk[:, 4 * j:4 * j + 4, hc * P:(hc + 1) * P], K[j][:, :], ACT.Copy).then_inc(wk_kept, 1)
            act.wait_ge(const_in, 48)
            act.wait_ge(eps_set, 1)
            for h in range(PH):
                keep(0, h)
                exps(0, h)
            blocks(act, body)
            norm(NBLK - 1, 0, NS)

        @block.tensor
        def _(pe):
            def score(b, s, h):
                turn = b * PH + h
                if not (first(b) and h < 2):
                    pe.wait_ge(score_kept, turn - 1)
                for c in range(DC):
                    ins = nc.tensor.matmul(S[h % 2][:, 0:HN], h2t[:, s, c, :], wk[:, c, h * HN:(h + 1) * HN], start=c == 0, stop=c == DC - 1)
                ins.then_inc(score_done, 1)

            def body(b, half, s, n):
                o = 1 - s
                pe.wait_ge(summed, b + 1)
                for h in range(PH):
                    if not last(b):
                        if h == 0:
                            pe.wait_ge(h2t_in[o], 16 * (half + 1 + s))
                        score(b + 1, o, h)
                    for k in range(TOPK):
                        m = h * TOPK + k
                        pe.wait_ge(diag_done, b * BH + m + 1)
                        pe.wait_ge(v_in[m % RING], 16 * (b * (BH // RING) + m // RING + 1))
                        if n < P:
                            pe.sem_inc(small, 1)
                        for j in range(2):
                            ins = nc.tensor.matmul(Y[s][j][0:n, :], diag[0:n, m % RING, 0:n], v[0:n, m % RING, j * 512:(j + 1) * 512],
                                                   start=m == 0, stop=m == BH - 1)
                        ins.then_inc(v_free, 1)
                pe.wait_ge(v_free, RING + BH * (b + 1))
                pe.sem_inc(values_done, 1)

            pe.wait_ge(key_in, 16)
            for hc in range(2 * PH):
                pe.wait_ge(wq_in[hc % 2], 16 * (hc // 2 + 1))
                for j in range(2):
                    if hc:
                        pe.wait_ge(wk_kept, 2 * hc + j - 1)
                    for c in range(4):
                        ins = nc.tensor.matmul(K[j][:, c * P:(c + 1) * P], wq[hc % 2][:, (4 * j + c) * P:(4 * j + c + 1) * P],
                                               keys[:, hc, :], start=True, stop=True)
                    ins.then_inc(wk_done, 1)
            pe.wait_ge(wk_kept, 4 * PH)
            pe.sem_inc(v_free, RING)
            pe.wait_ge(h2t_in[0], 16)
            for h in range(PH):
                score(0, 0, h)
            blocks(pe, body)


class Resident:
    pass


def build(nc, io):
    with ExitStack() as ctx:
        sb = Resident()
        sb.mix = ctx.enter_context(nc.sbuf_tensor("mix", [P, DC, TP], F32))
        sb.eps = ctx.enter_context(nc.sbuf_tensor("eps", [P, 4], F32))
        with ExitStack() as mixer:
            sb.prc = mixer.enter_context(nc.sbuf_tensor("prc", [P, NT, PW], F32))
            with ExitStack() as att:
                sb.qk = att.enter_context(nc.sbuf_tensor("qk", [P, 2 * PA, T], F32))
                sb.vtok = att.enter_context(nc.sbuf_tensor("vtok", [P, NBLK, ATT], F32))
                project(nc, io, sb)
                attend_prompt(nc, io, sb)
                attend_sample(nc, io, sb)
            convolve(nc, io, sb)
            with ExitStack() as rwkv:
                t = lambda name, shape: rwkv.enter_context(nc.sbuf_tensor(name, shape, F32))
                sb.kq, sb.bh = t("kq", [P, PR, SC]), t("bh", [P, PR, SC])
                sb.ends, sb.rwkv_par, sb.mu = t("ends", [P, NCH + DB, PR]), t("rwkv_par", [P, PR, 7]), t("mu", [P, RT])
                sb.head_sum = t("head_sum", [P, P])
                prepare_rwkv(nc, io, sb)
                scan_rwkv(nc, io, sb)
                finish_rwkv(nc, io, sb)
        close_mixer(nc, io, sb)
    with ExitStack() as ctx:
        sb.eps = ctx.enter_context(nc.sbuf_tensor("eps_peer", [P, 4], F32))
        peer(nc, io, sb)


def layout(given):
    dense = np.ascontiguousarray
    f4 = np.float32
    a = lambda name: np.asarray(given[name])
    chans = lambda arr, n: arr.reshape(n, P)
    everywhere = lambda arr: dense(np.broadcast_to(arr, (P,) + arr.shape))
    x = np.concatenate([a("x_prompt").reshape(SEQ, D), a("x_sample").reshape(NS, D)], 0)
    w_in = a("w_in")[0].reshape(DC, P, NT + 3 * PA, P)
    VT = NT + 2 * PA
    part = np.arange(P)
    out = {
        "xT": dense(x.T.reshape(DC, P, T).transpose(1, 0, 2)),
        "x_rows": np.concatenate([x, np.zeros((TP - T, D), f4)]).reshape(NBLK, P, D),
        "w_in": dense(w_in[:, :, :VT].transpose(2, 1, 0, 3)),
        "w_v": dense(a("w_in")[0][:, VT * P:].reshape(DC, P, ATT).transpose(1, 0, 2)),
        "norm1_g": dense(chans(a("norm1_g")[0], DC).T),
        "norm2_g": everywhere(a("norm2_g")[0]),
        "final_g": everywhere(a("final_g")),
        "w_out": dense(a("w_out")[0].reshape(DC, P, D).transpose(1, 0, 2)),
        "ones": np.ones((P, P), f4),
        "ident": np.eye(P, dtype=f4),
    }

    bias = a("att_bias")[0]
    later = part[:, None] >= part[None, :]
    query = np.arange(512)
    seen = np.arange(4)[None, :, None] * P + part[:, None, None] < query[None, None, :]
    key_seq, key_at = part // DS, part % DS
    seen_new = (key_seq[:, None, None] == np.arange(DB)[None, :, None]) & \
        (key_at[:, None, None] < np.tile(np.arange(DS), AH)[None, None, :])
    out.update({
        "att_bias": everywhere(bias),
        "tri": later.astype(f4), "tri_rest": (~later).astype(f4),
        "att_seen": seen.astype(f4), "att_cap": np.where(seen, 0, -1e30).astype(f4),
        "sample_bias": everywhere(np.tile(np.repeat(bias, DS), NPG + 1)),
        "sample_seen": seen_new.astype(f4), "sample_cap": np.where(seen_new, 0, -1e30).astype(f4),
        "pages": everywhere(a("page_table").reshape(DB * NPG)),
        "row": np.arange(P, dtype=f4)[:, None].copy(),
        "cache_k": a("cache_k")[0].reshape(-1, ATT), "cache_v": a("cache_v")[0].reshape(-1, ATT),
    })

    conv = lambda name: chans(a(name)[0], CT)
    out.update({
        "conv_w": dense(a("conv_w")[0].T.reshape(CT, P, KW).transpose(1, 0, 2)),
        "conv_affine": dense(np.stack([conv("conv_b"), conv("conv_ln_g"), conv("conv_ln_b")], -1).transpose(1, 0, 2)),
        "state_conv": dense(a("state_conv")[0].transpose(2, 0, 1).reshape(CT, P, DB, KW - 1)),
    })

    par = [a("rwkv_" + name)[0].reshape(PR, P) for name in ("w0", "a0", "k_k", "k_a", "r_k", "ln_g", "ln_b")]
    keep = np.ones(SC, f4)
    keep[0:SEQ:CH] = 0
    keep[SEQ:SEQ + DB * SW:SW] = 0
    keep[SEQ + 1:SEQ + DB * SW:SW] = 0
    keep[SEQ + DB * SW] = 0
    s, t = np.arange(CH)[:, None], np.arange(CH)[None, :]
    near = s // 16 == t // 16
    real = lambda col: (col < DB * SW) & (col % SW != 0)
    same = (s // SW == t // SW) & real(s) & real(t)
    prompt = [s < t, s <= t, (s < t) & near, (s < t) & ~near, (s > t) & near]
    sample = [(s < t) & same, (s <= t) & same, (s < t) & same, np.zeros_like(same), (s > t) & same]
    masks = np.stack([np.stack(prompt), np.stack(sample)]).astype(f4)
    masks = np.tile(masks.transpose(2, 0, 1, 3), (2, 1, 1, 1))
    step = np.arange(CH)
    of_seq = ((step[:, None] // SW == np.arange(DB)[None, :]) & real(step)[:, None]).astype(f4)
    out.update({
        "rwkv_mu": dense(chans(a("rwkv_mu")[0], RT).T),
        "wa_up": dense(np.concatenate([a("rwkv_w_up")[0], a("rwkv_a_up")[0]], 0)),
        "g_up": dense(a("rwkv_g_up")[0]),
        "rwkv_par": dense(np.stack(par, -1).transpose(1, 0, 2)),
        "head_sum": (part[:, None] // HD == part[None, :] // HD).astype(f4),
        "scan_keep": everywhere(keep),
        "eye2": np.tile(np.eye(CH, dtype=f4), (2, 1)),
        "chunk_masks": dense(np.repeat(masks[:, :, :, None, :], PR, axis=3)),
        "seq_mask": dense(np.repeat(np.tile(of_seq, (2, 1))[:, :, None], HD, axis=2)),
        "state_shift": dense(a("state_shift")[0].T.reshape(RT, P, DB).transpose(1, 0, 2)),
        "state_wkv": dense(a("state_wkv")[0].transpose(1, 3, 0, 2).reshape(PR, P, DB, HD).transpose(1, 0, 2, 3)),
    })

    out.update({
        "sub_keys": dense(a("peer_sub_keys")[0].transpose(3, 0, 1, 2).reshape(P, 2 * PH, KEYS)),
        "w_query": dense(a("peer_w_query")[0].T.reshape(2 * PH, P, D)),
        "iota": everywhere(np.arange(TOPK, dtype=f4)),
        "peer_u": a("peer_u")[0], "peer_v": a("peer_v")[0],
    })
    return out


OUTPUTS = {
    "y": (NBLK, P, D), "k_new": (P, PA, T), "v_new": (T, ATT),
    "conv_new_prompt": (P, CT, KW - 1), "conv_new_sample": (CT, P, DB, KW - 1), "shift_new": (P, RT, 1 + DB),
    "wkv_new_prompt": (P, PR, HD), "wkv_new_sample": (P, PR, DB, HD),
}
SCRATCH = {"x1": (NBLK, P, D), "h2": (NBLK, P, D), "h2t": (NBLK, P, DC, P)}


def kernel(**inputs):
    import concourse.bacc as bacc
    from concourse.bass_utils import run_bass_kernel_spmd

    nc = bacc.Bacc("TRN2", target_bir_lowering=False, num_devices=1)
    arrays, io = {}, {}
    for name, arr in layout(inputs).items():
        arrays["in_" + name] = np.ascontiguousarray(arr)
        io[name] = nc.dram_tensor("in_" + name, arr.shape, mybir.dt.from_np(arr.dtype), kind="ExternalInput").ap()
    for name, shape in OUTPUTS.items():
        io[name] = nc.dram_tensor("out_" + name, shape, F32, kind="ExternalOutput").ap()
    for name, shape in SCRATCH.items():
        io[name] = nc.dram_tensor("scratch_" + name, shape, F32).ap()
    build(nc, io)
    got = run_bass_kernel_spmd(nc, [arrays], core_ids=[0]).results[0]

    out = lambda name: np.asarray(got["out_" + name])
    y = out("y").reshape(TP, D)
    k = out("k_new").transpose(1, 0, 2).reshape(ATT, T).T
    v = out("v_new")
    conv_p = out("conv_new_prompt").transpose(2, 1, 0).reshape(1, 1, KW - 1, CC)
    conv_s = out("conv_new_sample").transpose(2, 3, 0, 1).reshape(1, DB, KW - 1, CC)
    shift = out("shift_new").transpose(2, 1, 0).reshape(1, 1 + DB, RC)
    wkv_p = out("wkv_new_prompt").reshape(2, HD, PR, HD).transpose(2, 0, 3, 1).reshape(1, 1, RH, HD, HD)
    wkv_s = out("wkv_new_sample").reshape(2, HD, PR, DB, HD).transpose(3, 2, 0, 4, 1).reshape(1, DB, RH, HD, HD)
    prompt = lambda arr: arr[:SEQ].reshape(1, 1, SEQ, AH, HD)
    sample = lambda arr: arr[SEQ:T].reshape(1, DB, DS, AH, HD)
    return (y[:SEQ].reshape(1, SEQ, D), y[SEQ:T].reshape(DB, DS, D),
            prompt(k), prompt(v), conv_p, shift[:, :1], wkv_p,
            sample(k), sample(v), conv_s, shift[:, 1:], wkv_s)
```

```python
import math
from contextlib import ExitStack

import numpy as np

import concourse.bass as bass
from concourse import mybir

F32 = mybir.dt.float32
U32 = mybir.dt.uint32
ALU = mybir.AluOpType
ACT = mybir.ActivationFunctionType
AX = mybir.AxisListType

P = 128
D = 1024
DC = D // P
SEQ = 1024
DB, DS = 8, 4
NS = DB * DS
T = SEQ + NS
NBLK = -(-T // P)
TP = NBLK * P
HD = 64
CC = 256
CT = CC // P
KW = 31
RH = 6
PR = RH // 2
AH = 6
PA = AH // 2
ATT = AH * HD
RC = 1408
RT = RC // P
NT = 2 * CT + RT
CH = 64
NCH = SEQ // CH
SW = DS + 1
SC = SEQ + CH
PW = SC + 1
PAGE = 128
NPG = 1024 // PAGE
POOLN = 80
KEYS = 128
PH = 8
TOPK = 16
RMS_EPS = 1e-5
LN_EPS = 1e-5
GN_EPS = 64e-5
NCHUNKS = [(0, 512), (512, 512), (1024, NS)]


class Steps:

    def __init__(self, sem, names):
        self.sem, self.names, self.next = sem, list(names), 0

    def did(self, ins, name):
        assert self.names[self.next % len(self.names)] == name, (self.names[self.next % len(self.names)], name)
        self.next += 1
        ins.then_inc(self.sem, 1)

    def at(self, name, turn=0):
        return turn * len(self.names) + self.names.index(name) + 1


class Chain:

    def __init__(self, eng, sem, base=0):
        self.eng, self.sem, self.base, self.n = eng, sem, base, 0

    def __call__(self, ins):
        self.n += 1
        ins.then_inc(self.sem, 1)
        self.eng.wait_ge(self.sem, self.base + self.n)


def project(nc, io, sb):
    with ExitStack() as ctx:
        h = sb.mix[:, :, 0:T]
        sq = sb.prc[:, 0:DC, 0:T]
        w = ctx.enter_context(nc.sbuf_tensor("w_in_tile", [P, 3, DC, P], F32))
        wv = ctx.enter_context(nc.sbuf_tensor("w_v", [P, DC, ATT], F32))
        g1 = ctx.enter_context(nc.sbuf_tensor("g1", [P, DC], F32))
        mean_of = ctx.enter_context(nc.sbuf_tensor("mean_of", [P, P], F32))
        rstd = ctx.enter_context(nc.sbuf_tensor("rstd", [P, T], F32))
        banks = [ctx.enter_context(nc.psum_tensor(f"proj{b}", [P, 512], F32)) for b in range(6)]
        tails = ctx.enter_context(nc.psum_tensor("proj_tails", [P, NS], F32))
        sem = lambda name: ctx.enter_context(nc.semaphore(name))
        x_in, small_in, wv_in = sem("x_in"), sem("small_in"), sem("wv_in")
        w_in = [sem(f"w_in{s}") for s in range(3)]
        ones_set, squared, mean_ready, root_ready = sem("ones_set"), sem("squared"), sem("mean_ready"), sem("root_ready")
        pads_set, h_ready, tile_done = sem("pads_set"), sem("h_ready"), sem("tile_done")
        act_free, dve_free = sem("act_free"), sem("dve_free")
        v_done, v_kept, kv_out = sem("v_done"), sem("v_kept"), sem("kv_out")
        dve_chain = sem("proj_dve")
        RCT, QKT = NT // 3, 2 * PA // 3
        block = ctx.enter_context(nc.Block())

        @block.sync
        def _(sp):
            for c in range(DC):
                sp.dma_start(h[:, c, :], io["xT"][:, c, :]).then_inc(x_in, 16)
            sp.dma_start(g1[:, :], io["norm1_g"]).then_inc(small_in, 16)
            for s in range(3):
                sp.dma_start(w[:, s, :, :], io["w_in"][s]).then_inc(w_in[s], 16)
            with sp.Fori(1, RCT + QKT) as i:
                for s in range(3):
                    sp.wait_ge(tile_done, 3 * (i - 1) + s + 1)
                    sp.dma_start(w[:, s, :, :], io["w_in"][bass.ds(3 * i + s, 1)].rearrange("o p c n -> p (o c) n"))\
                        .then_inc(w_in[s], 16)
            sp.dma_start(wv[:, :, :], io["w_v"]).then_inc(wv_in, 16)
            sp.wait_ge(act_free, 3 + NT + 2 * PA)
            sp.wait_ge(dve_free, 3 + NT + 2 * PA)
            sp.dma_start(io["k_new"], sb.qk[:, PA:2 * PA, :]).then_inc(kv_out, 16)
            sp.wait_ge(v_kept, NBLK)
            for b in range(NBLK):
                n = min(P, T - b * P)
                sp.dma_start(io["v_new"][b * P:b * P + n, :], sb.vtok[0:n, b, :]).then_inc(kv_out, 16)
            sp.wait_ge(kv_out, 16 * (1 + NBLK))

        @block.scalar
        def _(act):
            act.wait_ge(x_in, 16 * DC)
            for c in range(DC):
                nc.scalar.activation(sq[:, c, :], h[:, c, :], ACT.Square).then_inc(squared, 1)
            act.wait_ge(mean_ready, 1)
            act.wait_ge(ones_set, 2)
            for n, (lo, size) in enumerate(NCHUNKS):
                src = banks[n][:, 0:size]
                nc.scalar.activation(rstd[:, lo:lo + size], src, ACT.Sqrt, bias=sb.eps[:, 0:1]).then_inc(root_ready, 1)
            act.sem_inc(act_free, 3)
            act.wait_ge(h_ready, DC)

            def keep(i, dest, off, turn):
                for s in range(3):
                    act.wait_ge(tile_done, 3 * turn + s + 1)
                    nc.scalar.activation(dest[:, bass.ds(3 * i + s, 1), off:off + 512], banks[2 * s][:, :],
                                         ACT.Copy).then_inc(act_free, 1)

            with act.Fori(0, RCT) as i:
                keep(i, sb.prc, 1, i)
            with act.Fori(0, QKT) as i:
                keep(i, sb.qk, 0, i + RCT)
            for b in range(NBLK):
                n = min(P, T - b * P)
                act.wait_ge(v_done, b + 1)
                nc.scalar.activation(sb.vtok[0:n, b, :], banks[b % 6][0:n, 0:ATT], ACT.Copy).then_inc(v_kept, 1)

        @block.vector
        def _(dve):
            link = Chain(dve, dve_chain)
            nc.vector.memset(mean_of[:, :], 1.0 / D).then_inc(ones_set, 1)
            nc.vector.memset(sb.eps[:, 0:1], RMS_EPS).then_inc(ones_set, 1)
            dve.wait_ge(root_ready, len(NCHUNKS))
            link(nc.vector.reciprocal(rstd[:, :], rstd[:, :]))
            dve.wait_ge(small_in, 16)
            for c in range(DC):
                nc.vector.scalar_tensor_tensor(h[:, c, :], h[:, c, :], g1[:, c:c + 1], rstd[:, :],
                                               ALU.mult, ALU.mult).then_inc(h_ready, 1)
            dve.wait_ge(mean_ready, 1)
            nc.vector.memset(sb.prc[:, :, 0:1], 0.0).then_inc(pads_set, 1)
            nc.vector.memset(sb.prc[:, :, 1 + SEQ:PW], 0.0).then_inc(pads_set, 1)
            dve.wait_ge(pads_set, 2)
            nc.vector.sem_inc(dve_free, 3)

            def keep(i, dest, off, turn, spread):
                for s in range(3):
                    dve.wait_ge(tile_done, 3 * turn + s + 1)
                    nc.vector.tensor_copy(dest[:, bass.ds(3 * i + s, 1), off + 512:off + SEQ],
                                          banks[2 * s + 1][:, :])
                    if spread:
                        to = dest[:, bass.ds(3 * i + s, 1), 1 + SEQ:1 + SEQ + DB * SW]\
                            .rearrange("p o (b s) -> p (o b) s", s=SW)[:, :, 1:SW]
                        last = nc.vector.tensor_copy(to, tails[:, :].rearrange("p (b s) -> p b s", s=DS))
                    else:
                        last = nc.vector.tensor_copy(dest[:, bass.ds(3 * i + s, 1), SEQ:T], tails[:, :])
                    last.then_inc(dve_free, 1)

            with dve.Fori(0, RCT) as i:
                keep(i, sb.prc, 1, i, True)
            with dve.Fori(0, QKT) as i:
                keep(i, sb.qk, 0, i + RCT, False)

        @block.tensor
        def _(pe):
            pe.wait_ge(ones_set, 1)
            for n, (lo, size) in enumerate(NCHUNKS):
                for c in range(DC):
                    pe.wait_ge(squared, c + 1)
                    last = nc.tensor.matmul(banks[n][:, 0:size], mean_of[:, :], sq[:, c, lo:lo + size],
                                            start=c == 0, stop=c == DC - 1)
            last.then_inc(mean_ready, 1)
            pe.wait_ge(h_ready, DC)
            with pe.Fori(0, RCT + QKT) as i:
                for s in range(3):
                    pe.wait_ge(w_in[s], 16 * (i + 1))
                    pe.wait_ge(act_free, 3 * i + s + 1)
                    pe.wait_ge(dve_free, 3 * i + s + 1)
                    for n, (lo, size) in enumerate(NCHUNKS):
                        out = tails[:, :] if n == 2 else banks[2 * s + n][:, :]
                        if n == 2:
                            pe.wait_ge(dve_free, 3 * i + s + 3)
                        for c in range(DC):
                            last = nc.tensor.matmul(out, w[:, s, c, :], h[:, c, lo:lo + size],
                                                    start=c == 0, stop=c == DC - 1)
                    last.then_inc(tile_done, 1)
            pe.wait_ge(wv_in, 16)
            pe.wait_ge(act_free, 3 + NT + 2 * PA)
            pe.wait_ge(dve_free, 3 + NT + 2 * PA)
            for b in range(NBLK):
                n = min(P, T - b * P)
                if b >= 6:
                    pe.wait_ge(v_kept, b - 5)
                for c in range(DC):
                    last = nc.tensor.matmul(banks[b % 6][0:n, 0:ATT], h[:, c, b * P:b * P + n], wv[:, c, :],
                                            start=c == 0, stop=c == DC - 1)
                last.then_inc(v_done, 1)


def attend_prompt(nc, io, sb):
    QW = 512
    units = [(qc, kt, h) for qc in range(SEQ // QW) for kt in reversed(range((qc + 1) * QW // P)) for h in range(2)]
    U = len(units)
    R = 4
    with ExitStack() as ctx:
        t = lambda name, shape: ctx.enter_context(nc.sbuf_tensor(name, shape, F32))
        sem = lambda name: ctx.enter_context(nc.semaphore(name))
        HIST = KW - 1
        xp, xs = t("conv_rows", [P, CT, HIST + SEQ]), t("conv_rows_sample", [P, CT, DB, HIST + DS])
        gate, scaled = t("conv_gate", [P, SC]), t("conv_scaled", [P, 2, T])
        cw, aff = t("conv_w", [P, CT, KW]), t("conv_affine", [P, CT, 3])
        cy = sb.mix
        params_in, state_in, padded, sig_done, glu_done = sem("conv_params"), sem("conv_state"), sem("conv_set"), sem("conv_sig"), sem("conv_glu")
        scaled_done, taps, taps_dve, conv_out = sem("conv_scaled"), sem("conv_taps"), sem("conv_taps_dve"), sem("conv_out")
        q, k, v = t("q_pair", [P, SEQ]), t("k_pair", [P, SEQ]), t("v_pair", [P, SEQ // P, P])
        bias, bias2 = t("att_bias", [P, AH]), t("bias_pair", [P, 2])
        tri, rest = t("tri", [P, P]), t("rest", [P, P])
        seen, cap = t("seen", [P, P]), t("cap", [P, P])
        zb, w, a = t("logit", [P, R, QW]), t("soft", [P, R, QW]), t("weight", [P, R, QW])
        ps = lambda name: ctx.enter_context(nc.psum_tensor(name, [P, QW], F32))
        Z = [[ps(f"z{h}{n}") for n in range(2)] for h in range(2)]
        A = [ps(f"later{h}") for h in range(2)]
        O = ps("att_out")
        const_in = sem("att_const_in")
        q_staged, v_staged = sem("q_staged"), sem("v_staged")
        z_done, logit_done, min_done, exp_done, ln_done = sem("z_done"), sem("logit_done"), sem("min_done"), sem("exp_done"), sem("ln_done")
        soft_done, sum_done, diff_done, weight_done = sem("soft_done"), sem("sum_done"), sem("diff_done"), sem("weight_done")
        rest_done, pv_done, out_kept, masked = sem("rest_done"), sem("pv_done"), sem("out_kept"), sem("masked")
        block = ctx.enter_context(nc.Block())

        def tap(c, j):
            by_seq = lambda ap: ap.rearrange("p (b s) -> p b s", s=DS)
            product = scaled[:, j % 2, :] if isinstance(j, int) else None
            return ((cy[:, c, 0:SEQ], xp[:, c, bass.ds(j, SEQ)], product[:, 0:SEQ] if product is not None else None),
                    (by_seq(cy[:, c, SEQ:T]), xs[:, c, :, bass.ds(j, DS)], by_seq(product[:, SEQ:T]) if product is not None else None))
        QCS = SEQ // QW
        last_of = {qc: max(n for n, x in enumerate(units) if x[0] == qc) for qc in range(QCS)}
        first = {(qc, h): min(n for n, x in enumerate(units) if x[0] == qc and x[2] == h) for qc in range(QCS) for h in range(2)}
        rests = [n for n, x in enumerate(units) if x[1] > 0]
        NM = 2 * sum(x[1] * P // QW == x[0] for x in units)

        def cols(n):
            qc, kt, h = units[n]
            lo = max(0, kt * P - qc * QW)
            return slice(lo, QW), slice(lo, lo + P)

        def parts(n):
            qc, kt, h = units[n]
            new, all_ = cols(n)[1], cols(n)[0]
            if kt * P < qc * QW:
                return [(all_, False)]
            return [(new, True)] + ([(slice(new.stop, QW), False)] if new.stop < QW else [])

        @block.sync
        def _(sp):
            for dst, src in ((bias, "att_bias"), (tri, "tri"), (rest, "tri_rest")):
                sp.dma_start(dst[:, :], io[src]).then_inc(const_in, 16)
            for dst, src in ((seen, "att_seen"), (cap, "att_cap")):
                sp.dma_start(dst[:, :], io[src]).then_inc(const_in, 16)
            sp.dma_start(cw[:, :, :], io["conv_w"]).then_inc(params_in, 16)
            sp.dma_start(aff[:, :, :], io["conv_affine"]).then_inc(params_in, 16)
            for c in range(CT):
                sp.dma_start(xs[:, c, :, 0:HIST], io["state_conv"][c]).then_inc(state_in, 16)
            sp.wait_ge(const_in, 80)
            sp.wait_ge(glu_done, 2 * CT)
            sp.wait_ge(state_in, 16 * CT)
            sp.dma_start(io["conv_new_prompt"], xp[:, :, SEQ:]).then_inc(conv_out, 16)
            for c in range(CT):
                sp.dma_start(io["conv_new_sample"][c], xs[:, c, :, DS:]).then_inc(conv_out, 16)
            sp.wait_ge(conv_out, 16 + 16 * CT)

        @block.gpsimd
        def _(pool):
            nc.gpsimd.memset(xp[:, :, 0:HIST], 0.0).then_inc(padded, 1)
            sample = lambda tile: tile[:, SEQ:SEQ + DB * SW].rearrange("p (b s) -> p b s", s=SW)[:, :, 1:SW]
            for c in range(CT):
                pool.wait_ge(sig_done, c + 1)
                nc.gpsimd.tensor_tensor(xp[:, c, HIST:], sb.prc[:, c, 1:1 + SEQ], gate[:, 0:SEQ], ALU.mult).then_inc(glu_done, 1)
                nc.gpsimd.tensor_tensor(xs[:, c, :, HIST:], sample(sb.prc[:, c, 1:PW]), sample(gate), ALU.mult).then_inc(glu_done, 1)
            pool.wait_ge(params_in, 32)
            pool.wait_ge(state_in, 16 * CT)
            pool.wait_ge(padded, 1)
            pool.wait_ge(glu_done, 2 * CT)
            c = CT - 1
            for to, rows, _ in tap(c, 0):
                nc.gpsimd.tensor_scalar(to, rows, cw[:, c, 0:1], aff[:, c, 0:1], ALU.mult, ALU.add).then_inc(taps, 1)
            for j in range(1, KW):
                for _, rows, product in tap(c, j):
                    if j > 2:
                        pool.wait_ge(taps, 2 * (j - 1))
                    nc.gpsimd.tensor_scalar(product, rows, cw[:, c, j:j + 1], None, ALU.mult).then_inc(scaled_done, 1)
                pool.wait_ge(taps, 2 * j)
                pool.wait_ge(scaled_done, 2 * j)
                for to, _, product in tap(c, j):
                    nc.gpsimd.tensor_tensor(to, to, product, ALU.add).then_inc(taps, 1)

        @block.vector
        def _(dve):
            def logit(i, n):
                qc, kt, h = units[n]
                dve.wait_ge(z_done, i * U + n + 1)
                if n >= R:
                    dve.wait_ge(diff_done, i * U + n - R + 1)
                nc.vector.tensor_scalar(zb[:, n % R, cols(n)[0]], Z[h][n // 2 % 2][:, cols(n)[0]], HD ** -0.5, bias2[:, h:h + 1],
                                        ALU.mult, ALU.add).then_inc(logit_done, 1)
                if n >= R:
                    if n - R in rests:
                        dve.wait_ge(rest_done, i * len(rests) + rests.index(n - R) + 1)
                    else:
                        dve.wait_ge(sum_done, i * U + n - R + 1)
                dve.wait_ge(logit_done, i * U + n + 1)
                nc.vector.tensor_scalar(w[:, n % R, cols(n)[0]], zb[:, n % R, cols(n)[0]], 40.0, None, ALU.min).then_inc(min_done, 1)

            masks = [0]

            def soft(i, n):
                qc, kt, h = units[n]
                on, part = cols(n)
                dve.wait_ge(ln_done, i * U + n + 1)
                ins = nc.vector.tensor_tensor(w[:, n % R, on], w[:, n % R, on], zb[:, n % R, on], ALU.max)
                if kt * P // QW == qc:
                    masks[0] += 1
                    ins.then_inc(masked, 1)
                    dve.wait_ge(masked, i * NM + masks[0])
                    ins = nc.vector.tensor_tensor(w[:, n % R, part], w[:, n % R, part], seen[:, :], ALU.mult)
                ins.then_inc(soft_done, 1)

            def diff(i, n):
                qc, kt, h = units[n]
                dve.wait_ge(sum_done, i * U + n + 1)
                if n >= R:
                    dve.wait_ge(pv_done, i * U + n - R + 1)
                on, part = cols(n)
                ins = nc.vector.tensor_tensor(a[:, n % R, on], zb[:, n % R, on], A[h][:, on], ALU.subtract)
                if kt * P // QW == qc:
                    masks[0] += 1
                    ins.then_inc(masked, 1)
                    dve.wait_ge(masked, i * NM + masks[0])
                    ins = nc.vector.tensor_tensor(a[:, n % R, part], a[:, n % R, part], cap[:, :], ALU.min)
                ins.then_inc(diff_done, 1)

            PAIR_TAPS = (KW - 1) // PA

            def convolve(i, m):
                j = i * PAIR_TAPS + (m + 1)
                dve.wait_ge(taps_dve, 2 * j)
                for to, rows, _ in tap(0, j):
                    nc.vector.scalar_tensor_tensor(to, rows, cw[:, 0, bass.ds(j, 1)], to, ALU.mult, ALU.add).then_inc(taps_dve, 1)

            dve.wait_ge(const_in, 80)
            dve.wait_ge(params_in, 32)
            dve.wait_ge(state_in, 16 * CT)
            dve.wait_ge(padded, 1)
            dve.wait_ge(glu_done, 2 * CT)
            for to, rows, _ in tap(0, 0):
                nc.vector.tensor_scalar(to, rows, cw[:, 0, 0:1], aff[:, 0, 0:1], ALU.mult, ALU.add).then_inc(taps_dve, 1)
            with dve.Fori(0, PA) as i:
                nc.vector.tensor_copy(q[:, :], sb.qk[:, bass.ds(i, 1), 0:SEQ]).then_inc(q_staged, 1)
                nc.vector.tensor_copy(k[:, :], sb.qk[:, bass.ds(i + PA, 1), 0:SEQ]).then_inc(q_staged, 1)
                nc.vector.tensor_copy(bias2[:, :], bias[:, bass.ds(2 * i, 2)]).then_inc(q_staged, 1)
                dve.wait_ge(q_staged, 3 * i + 3)
                masks[0] = 0
                for n in range(-3, U):
                    if n + 3 < U:
                        logit(i, n + 3)
                    if 0 <= n + 2 < U:
                        soft(i, n + 2)
                    if n >= 0:
                        diff(i, n)
                    if n % 2 == 0 and n // 2 in range(PAIR_TAPS):
                        convolve(i, n // 2)
                dve.wait_ge(pv_done, U * i + U)
                dve.wait_ge(weight_done, U * i + U)

        @block.scalar
        def _(act):
            for c in range(CT):
                if c:
                    act.wait_ge(glu_done, 2 * c)
                nc.scalar.activation(gate[:, :], sb.prc[:, CT + c, 1:PW], ACT.Sigmoid).then_inc(sig_done, 1)
            nc.scalar.preload_act_table_set("natural_log_exp_and_others")
            with act.Fori(0, PA) as i:
                nc.scalar.activation(v[:, :, :], sb.vtok[:, 0:SEQ // P, bass.ds(i * P, P)], ACT.Copy).then_inc(v_staged, 1)
                for n in range(-2, U):
                    if n + 2 < U:
                        m = n + 2
                        act.wait_ge(min_done, i * U + m + 1)
                        nc.scalar.activation(w[:, m % R, cols(m)[0]], w[:, m % R, cols(m)[0]], ACT.Exp).then_inc(exp_done, 1)
                        act.wait_ge(exp_done, i * U + m + 1)
                        nc.scalar.activation(w[:, m % R, cols(m)[0]], w[:, m % R, cols(m)[0]], ACT.Ln, bias=1.0).then_inc(ln_done, 1)
                    if n >= 0:
                        act.wait_ge(diff_done, i * U + n + 1)
                        nc.scalar.activation(a[:, n % R, cols(n)[0]], a[:, n % R, cols(n)[0]], ACT.Exp).then_inc(weight_done, 1)
                    for qc in range(QCS):
                        if n == min(last_of[qc] + 2, U - 1):
                            act.wait_ge(pv_done, i * U + last_of[qc] + 1)
                            nc.scalar.activation(sb.mix[:, bass.ds(i + DC - PA, 1), qc * QW:(qc + 1) * QW], O[:, :],
                                                 ACT.Copy).then_inc(out_kept, 1)

        @block.tensor
        def _(pe):
            def score(i, n):
                qc, kt, h = units[n]
                if n >= 4:
                    pe.wait_ge(logit_done, i * U + n - 4 + 1)
                on = cols(n)[0]
                nc.tensor.matmul(Z[h][n // 2 % 2][:, on], k[h * HD:(h + 1) * HD, kt * P:(kt + 1) * P],
                                 q[h * HD:(h + 1) * HD, qc * QW + on.start:(qc + 1) * QW], start=True, stop=True).then_inc(z_done, 1)

            def later(i, n):
                qc, kt, h = units[n]
                pe.wait_ge(soft_done, i * U + n + 1)
                if n == first[qc, h] and qc:
                    pe.wait_ge(diff_done, i * U + last_of[qc - 1] + 1)
                for on, new in parts(n):
                    ins = nc.tensor.matmul(A[h][:, on], tri[:, :], w[:, n % R, on], start=new, stop=True, skip_group_check=True)
                ins.then_inc(sum_done, 1)

            def value(i, n):
                qc, kt, h = units[n]
                if n in rests:
                    pe.wait_ge(diff_done, i * U + n + 1)
                    nc.tensor.matmul(A[h][:, cols(n)[0]], rest[:, :], w[:, n % R, cols(n)[0]], start=False, stop=True,
                                     skip_group_check=True).then_inc(rest_done, 1)
                pe.wait_ge(weight_done, i * U + n + 1)
                if n == first[qc, 0] and qc:
                    pe.wait_ge(out_kept, i * QCS + qc)
                for on, new in parts(n):
                    ins = nc.tensor.matmul(O[h * HD:(h + 1) * HD, on], v[:, kt, h * HD:(h + 1) * HD], a[:, n % R, on],
                                           start=new, stop=kt == 0, skip_group_check=True)
                ins.then_inc(pv_done, 1)

            with pe.Fori(0, PA) as i:
                pe.wait_ge(q_staged, 3 * i + 3)
                pe.wait_ge(v_staged, i + 1)
                for n in range(-3, U + 1):
                    if n + 3 < U:
                        score(i, n + 3)
                    if 0 <= n < U:
                        later(i, n)
                    if n >= 1:
                        value(i, n - 1)
                pe.wait_ge(out_kept, i * QCS + QCS)


def norm_convolution(nc, io, sb):
    with ExitStack() as ctx:
        t = lambda name, shape: ctx.enter_context(nc.sbuf_tensor(name, shape, F32))
        sem = lambda name: ctx.enter_context(nc.semaphore(name))
        y = sb.mix
        sq, rs = t("conv_sq", [P, CT, T]), t("conv_rstd", [P, T])
        aff = t("conv_norm_affine", [P, CT, 3])
        mean_of = t("conv_mean_of", [P, P])
        mean = [ctx.enter_context(nc.psum_tensor(f"conv_mean{n}", [P, 512], F32)) for n in range(3)]
        var = [ctx.enter_context(nc.psum_tensor(f"conv_var{n}", [P, 512], F32)) for n in range(3)]
        params_in, set_, mean_done, centred = sem("conv_norm_params"), sem("conv_norm_set"), sem("conv_mean_done"), sem("conv_centred")
        squared, var_done, root_done, rstd_done = sem("conv_squared"), sem("conv_var_done"), sem("conv_root"), sem("conv_rstd_done")
        normed, silu_done, mixed = sem("conv_normed"), sem("conv_silu"), sem("conv_mixed")
        block = ctx.enter_context(nc.Block())

        @block.sync
        def _(sp):
            sp.dma_start(aff[:, :, :], io["conv_affine"]).then_inc(params_in, 16)
            sp.wait_ge(params_in, 16)

        @block.scalar
        def _(act):
            for c in range(CT):
                act.wait_ge(centred, (c + 1) * len(NCHUNKS))
                nc.scalar.activation(sq[:, c, :], y[:, c, 0:T], ACT.Square).then_inc(squared, 1)
            act.wait_ge(var_done, 1)
            act.wait_ge(set_, 3)
            for n, (lo, size) in enumerate(NCHUNKS):
                nc.scalar.activation(rs[:, lo:lo + size], var[n][:, 0:size], ACT.Sqrt, bias=sb.eps[:, 1:2]).then_inc(root_done, 1)
            act.wait_ge(params_in, 16)
            for c in range(CT):
                act.wait_ge(normed, c + 1)
                nc.scalar.activation(sq[:, c, :], y[:, c, 0:T], ACT.Sigmoid, bias=aff[:, c, 2:3],
                                     scale=aff[:, c, 1:2]).then_inc(silu_done, 1)

        @block.vector
        def _(dve):
            nc.vector.memset(mean_of[:, :], 1.0 / CC).then_inc(set_, 1)
            nc.vector.memset(sb.eps[:, 1:2], LN_EPS).then_inc(set_, 1)
            nc.vector.memset(sb.eps[:, 2:3], GN_EPS).then_inc(set_, 1)
            dve.wait_ge(params_in, 16)
            dve.wait_ge(mean_done, 1)
            for c in range(CT):
                for n, (lo, size) in enumerate(NCHUNKS):
                    nc.vector.tensor_tensor(y[:, c, lo:lo + size], y[:, c, lo:lo + size], mean[n][:, 0:size],
                                            ALU.subtract).then_inc(centred, 1)
            dve.wait_ge(root_done, len(NCHUNKS))
            nc.vector.reciprocal(rs[:, :], rs[:, :]).then_inc(rstd_done, 1)
            dve.wait_ge(rstd_done, 1)
            dve.wait_ge(centred, CT * len(NCHUNKS))
            for c in range(CT):
                nc.vector.tensor_tensor(y[:, c, 0:T], y[:, c, 0:T], rs[:, :], ALU.mult).then_inc(normed, 1)
            for c in range(CT):
                dve.wait_ge(silu_done, c + 1)
                nc.vector.tensor_scalar(y[:, c, 0:T], y[:, c, 0:T], aff[:, c, 1:2], aff[:, c, 2:3],
                                        ALU.mult, ALU.add).then_inc(mixed, 1)
                dve.wait_ge(mixed, 2 * c + 1)
                nc.vector.tensor_tensor(y[:, c, 0:T], y[:, c, 0:T], sq[:, c, :], ALU.mult).then_inc(mixed, 1)

        @block.tensor
        def _(pe):
            pe.wait_ge(set_, 1)
            for n, (lo, size) in enumerate(NCHUNKS):
                for c in range(CT):
                    last = nc.tensor.matmul(mean[n][:, 0:size], mean_of[:, :], y[:, c, lo:lo + size],
                                            start=c == 0, stop=c == CT - 1)
            last.then_inc(mean_done, 1)
            pe.wait_ge(squared, CT)
            for n, (lo, size) in enumerate(NCHUNKS):
                for c in range(CT):
                    last = nc.tensor.matmul(var[n][:, 0:size], mean_of[:, :], sq[:, c, lo:lo + size],
                                            start=c == 0, stop=c == CT - 1)
            last.then_inc(var_done, 1)


def prepare_rwkv(nc, io, sb):
    with ExitStack() as ctx:
        t = lambda name, shape: ctx.enter_context(nc.sbuf_tensor(name, shape, F32))
        sem = lambda name: ctx.enter_context(nc.semaphore(name))
        R0, K0, V0, LO, GA = 2 * CT, 2 * CT + PR, 2 * CT + 2 * PR, NT - 2, NT - 1
        tile = lambda j: sb.prc[:, j, 1:PW]
        mu, par = sb.mu, sb.rwkv_par
        wa_up, blk, fresh = t("wa_up", [P, RH * HD]), sb.head_sum, t("scan_keep", [P, SC])
        carried, shift = t("carried", [P, RT, DB]), t("shift_new", [P, RT, 1 + DB])
        step = t("shift_diff", [P, 2, SC])
        lw, aa, cs, before, sq, pw = (t(n, [P, SC]) for n in ("log_decay", "aaa", "log_product", "log_before", "k_sq", "product"))
        pieces = [(0, 512), (512, 512), (1024, SC - 1024)]
        bw = [ctx.enter_context(nc.psum_tensor(f"rw_w{n}", [P, 512], F32)) for n in range(3)]
        ba = [ctx.enter_context(nc.psum_tensor(f"rw_a{n}", [P, 512], F32)) for n in range(3)]
        const_in, carried_in, carried_set, shift_out = sem("rw_const"), sem("rw_carried"), sem("rw_carried_set"), sem("rw_shift_out")
        shifted, tanh_done = sem("rw_shifted"), sem("rw_tanh")
        V = Steps(sem("rw_dve"), ["scale", "scan", "before", "kraw", "root", "recip", "kk", "am", "knew", "b", "bon", "bonv",
                                  "rq", "kq", "kh", "bh", "ends", "ends_sample"])
        A = Steps(sem("rw_act"), ["decay", "aaa", "sq", "norm", "prod", "prod_before", "prod_inv"])
        E = Steps(sem("rw_pe"), ["up", "norm", "bonus"])
        block = ctx.enter_context(nc.Block())

        @block.sync
        def _(sp):
            sp.dma_start(carried[:, :, :], io["state_shift"]).then_inc(carried_in, 16)
            for dst, src in ((mu, "rwkv_mu"), (wa_up, "wa_up"), (blk, "head_sum"), (fresh, "scan_keep")):
                sp.dma_start(dst[:, :], io[src]).then_inc(const_in, 16)
            sp.dma_start(par[:, :, :], io["rwkv_par"]).then_inc(const_in, 16)
            sp.wait_ge(carried_set, 3)
            sp.dma_start(io["shift_new"], shift[:, :, :]).then_inc(shift_out, 16)
            sp.wait_ge(shift_out, 16)

        @block.vector
        def _(dve):
            rows = sb.prc[:, R0:NT, :]
            dve.wait_ge(carried_in, 16)
            nc.vector.tensor_copy(rows[:, :, 1 + SEQ:1 + SEQ + DB * SW].rearrange("p j (b s) -> p j b s", s=SW)[:, :, :, 0],
                                  carried[:, :, :]).then_inc(carried_set, 1)
            nc.vector.tensor_copy(shift[:, :, 0:1], rows[:, :, SEQ:SEQ + 1]).then_inc(carried_set, 1)
            nc.vector.tensor_copy(shift[:, :, 1:], rows[:, :, 1 + SEQ:1 + SEQ + DB * SW].rearrange("p j (b s) -> p j b s", s=SW)[:, :, :, SW - 1])\
                .then_inc(carried_set, 1)
            dve.wait_ge(carried_set, 3)
            dve.wait_ge(const_in, 80)
            for j in range(RT):
                j_ = R0 + j
                if j >= 2:
                    dve.wait_ge(shifted, 2 * (j - 1))
                nc.vector.tensor_tensor(step[:, j % 2, :], sb.prc[:, j_, 0:SC], tile(j_), ALU.subtract).then_inc(shifted, 1)
                dve.wait_ge(shifted, 2 * j + 1)
                nc.vector.scalar_tensor_tensor(tile(j_), step[:, j % 2, :], mu[:, j:j + 1], tile(j_), ALU.mult, ALU.add)\
                    .then_inc(shifted, 1)
            dve.wait_ge(shifted, 2 * RT)
            for i in range(PR):
                r, k, v = tile(R0 + i), tile(K0 + i), tile(V0 + i)
                kq, bh, bv = sb.kq[:, i, :], sb.bh[:, i, :], tile(i)
                p = lambda n: par[:, i, n:n + 1]
                own = lambda name: dve.wait_ge(V.sem, V.at(name, i))
                dve.wait_ge(A.sem, A.at("aaa", i))
                V.did(nc.vector.tensor_scalar(lw[:, :], lw[:, :], -math.exp(-0.5), None, ALU.mult), "scale")
                own("scale")
                V.did(nc.vector.tensor_tensor_scan(cs[:, :], fresh[:, :], lw[:, :], 0.0, ALU.mult, ALU.add), "scan")
                own("scan")
                V.did(nc.vector.tensor_tensor(before[:, :], cs[:, :], lw[:, :], ALU.subtract), "before")
                V.did(nc.vector.tensor_scalar(kq, k, p(2), None, ALU.mult), "kraw")
                dve.wait_ge(A.sem, A.at("norm", i))
                V.did(nc.vector.tensor_scalar(sq[:, :], sq[:, :], 1e-12, None, ALU.max), "root")
                own("root")
                V.did(nc.vector.reciprocal(sq[:, :], sq[:, :]), "recip")
                own("recip")
                V.did(nc.vector.tensor_tensor(kq, kq, sq[:, :], ALU.mult), "kk")
                own("kk")
                V.did(nc.vector.tensor_scalar(sq[:, :], aa[:, :], 1.0, p(3), ALU.subtract, ALU.mult), "am")
                own("am")
                V.did(nc.vector.scalar_tensor_tensor(k, sq[:, :], 1.0, k, ALU.add, ALU.mult), "knew")
                V.did(nc.vector.tensor_tensor(bh, kq, aa[:, :], ALU.mult), "b")
                own("knew")
                V.did(nc.vector.scalar_tensor_tensor(sq[:, :], r, p(4), k, ALU.mult, ALU.mult), "bon")
                dve.wait_ge(E.sem, E.at("bonus", i))
                for n, (lo, size) in enumerate(pieces):
                    last = nc.vector.tensor_tensor(bv[:, lo:lo + size], v[:, lo:lo + size], ba[n][:, 0:size], ALU.mult)
                V.did(last, "bonv")
                dve.wait_ge(A.sem, A.at("prod_inv", i))
                own("bonv")
                V.did(nc.vector.tensor_tensor(r, r, pw[:, :], ALU.mult), "rq")
                V.did(nc.vector.tensor_tensor(kq, kq, before[:, :], ALU.mult), "kq")
                V.did(nc.vector.tensor_tensor(k, k, cs[:, :], ALU.mult), "kh")
                V.did(nc.vector.tensor_tensor(bh, bh, cs[:, :], ALU.mult), "bh")
                V.did(nc.vector.tensor_copy(sb.ends[:, 0:NCH, i], pw[:, 0:SEQ].rearrange("p (n c) -> p n c", c=CH)[:, :, CH - 1]), "ends")
                V.did(nc.vector.tensor_copy(sb.ends[:, NCH:NCH + DB, i], pw[:, SEQ:SEQ + DB * SW].rearrange("p (n c) -> p n c", c=SW)[:, :, SW - 1]),
                      "ends_sample")

        @block.scalar
        def _(act):
            act.wait_ge(shifted, 2 * (LO - R0) + 2)
            nc.scalar.activation(sb.prc[0:HD, LO, 1:PW], sb.prc[0:HD, LO, 1:PW], ACT.Tanh).then_inc(tanh_done, 1)
            act.wait_ge(const_in, 80)
            for i in range(PR):
                p = lambda n: par[:, i, n:n + 1]
                if i:
                    act.wait_ge(V.sem, V.at("ends_sample", i - 1))
                act.wait_ge(E.sem, E.at("up", i))
                for what, bank, dst, n_ in (("decay", bw, lw, 0), ("aaa", ba, aa, 1)):
                    for n, (lo, size) in enumerate(pieces):
                        last = nc.scalar.activation(dst[:, lo:lo + size], bank[n][:, 0:size], ACT.Sigmoid, bias=p(n_))
                    A.did(last, what)
                act.wait_ge(V.sem, V.at("kraw", i))
                A.did(nc.scalar.activation(sq[:, :], sb.kq[:, i, :], ACT.Square), "sq")
                act.wait_ge(E.sem, E.at("norm", i))
                for n, (lo, size) in enumerate(pieces):
                    last = nc.scalar.activation(sq[:, lo:lo + size], bw[n][:, 0:size], ACT.Sqrt)
                A.did(last, "norm")
                A.did(nc.scalar.activation(pw[:, :], cs[:, :], ACT.Exp), "prod")
                A.did(nc.scalar.activation(before[:, :], before[:, :], ACT.Exp), "prod_before")
                A.did(nc.scalar.activation(cs[:, :], cs[:, :], ACT.Exp, scale=-1.0), "prod_inv")

        @block.tensor
        def _(pe):
            pe.wait_ge(tanh_done, 1)
            pe.wait_ge(shifted, 2 * RT)
            pe.wait_ge(const_in, 80)
            for i in range(PR):
                cols = slice(i * P, (i + 1) * P)
                if i:
                    pe.wait_ge(V.sem, V.at("bonv", i - 1))
                for bank, lo_p in ((bw, 0), (ba, HD)):
                    for n, (lo, size) in enumerate(pieces):
                        last = nc.tensor.matmul(bank[n][:, 0:size], wa_up[lo_p:lo_p + HD, cols],
                                                sb.prc[lo_p:lo_p + HD, LO, 1 + lo:1 + lo + size], start=True, stop=True)
                E.did(last, "up")
                pe.wait_ge(A.sem, A.at("sq", i))
                for n, (lo, size) in enumerate(pieces):
                    last = nc.tensor.matmul(bw[n][:, 0:size], blk[:, :], sq[:, lo:lo + size], start=True, stop=True)
                E.did(last, "norm")
                pe.wait_ge(V.sem, V.at("bon", i))
                for n, (lo, size) in enumerate(pieces):
                    last = nc.tensor.matmul(ba[n][:, 0:size], blk[:, :], sq[:, lo:lo + size], start=True, stop=True)
                E.did(last, "bonus")


def scan_rwkv(nc, io, sb):
    with ExitStack() as ctx:
        t = lambda name, shape: ctx.enter_context(nc.sbuf_tensor(name, shape, F32))
        sem = lambda name: ctx.enter_context(nc.semaphore(name))
        R0, K0, V0 = 2 * CT, 2 * CT + PR, 2 * CT + 2 * PR
        two = lambda name, shape: [t(f"{name}{n}", shape) for n in range(2)]
        kr, kh, bh, vs = two("kq_rq", [P, PR, 2, CH]), two("kh_c", [P, PR, CH]), two("bh_c", [P, PR, CH]), two("v_c", [P, PR, CH])
        end, state, state2 = two("end_c", [P, PR]), t("state", [P, PR, HD]), t("state_kept", [P, PR, HD])
        eye = t("eye", [P, HD])
        masks = t("masks", [P, 2, 5, PR, CH])
        na, arb = two("na", [P, PR, 2, CH]), two("arb", [P, PR, CH])
        xd, xl, md = two("xd", [P, PR, CH]), two("xl", [P, PR, CH]), two("md", [P, PR, CH])
        vk, bt = two("v_kh_tok", [P, 2, PR, CH]), two("bh_tok", [P, PR, CH])
        p2, p4 = two("pow2_", [P, 2, PR, CH]), two("pow4_", [P, 2, PR, CH])
        ra, rb, td, tdt, zt = (two(n, [P, PR, CH]) for n in ("ra", "rb", "td", "tdt", "zt"))
        w, nu = t("w_rhs", [P, PR, CH]), t("neg_u", [P, PR, CH])
        s0, tmask = t("state_sample", [P, PR, DB, HD]), t("seq_mask", [P, DB, HD])
        spread, w0, values_by_seq = t("spread", [P, DB, HD]), t("w_state", [P, PR, HD]), t("values_spread", [P, DB, HD])
        B = [ctx.enter_context(nc.psum_tensor(f"chunk{n}", [P, 512], F32)) for n in range(8)]
        pv = lambda b: B[b][:, 0:PR * CH].rearrange("p (i c) -> p i c", c=CH)
        pv2 = lambda b: B[b][:, PR * CH:2 * PR * CH].rearrange("p (i c) -> p i c", c=CH)
        ping = lambda s: 4 + 2 * s
        pong = lambda s: 5 + 2 * s
        const_in, state_set = sem("ch_const"), sem("ch_state_set")
        TURNS = NCH // 2

        def steps(tag, names, slots):
            out = []
            for group in names.split("|"):
                out += [n + str(s) for s in slots for n in group.split()]
            return Steps(sem(tag), out)

        def sets(slots, tag):
            return (steps("ch_dve" + tag, "stage_k stage_b | na xd md xl arb | r1 | r2 | r3 | td | q1 | q2 | tt | keep_state state", slots),
                    steps("ch_act" + tag, "stage_kq stage_rq | vk bt p2 | p4 | tdt | zt | w nu y", slots),
                    steps("ch_pool" + tag, "stage_v stage_end", slots),
                    steps("ch_pe" + tag, "kk bb tok p2 | p4 | p8 | r2 | r3 | td | tdt | zt | q1 | q2 | tt | w u y state", slots))
        prompt_sets, sample_sets = sets((0, 1), ""), sets((0,), "_sample")
        AA, AB, S2, SO = sem("ch_sample_pe"), sem("ch_sample_dve"), sem("ch_sample_state"), sem("ch_out")
        block = ctx.enter_context(nc.Block())
        heads = [(i, slice(h * HD, (h + 1) * HD)) for i in range(PR) for h in range(2)]

        def turns(eng, turn):
            turn(0, *prompt_sets, (0, 1), True, False)
            with eng.Fori(1, TURNS) as c:
                turn(c, *prompt_sets, (0, 1), False, False)
            turn(0, *sample_sets, (0,), False, True)

        def last_turn(eng, sets_, name, c, sample):
            s = prompt_sets[sets_]
            eng.wait_ge(s.sem, s.at(name, TURNS - 1 if sample else c - 1))

        chunk_of = lambda c, s, sample: NCH if sample else 2 * c + s

        @block.sync
        def _(sp):
            sp.dma_start(eye[:, :], io["eye2"]).then_inc(const_in, 16)
            sp.dma_start(masks[:, :, :, :, :], io["chunk_masks"]).then_inc(const_in, 16)
            sp.dma_start(s0[:, :, :, :], io["state_wkv"]).then_inc(const_in, 16)
            sp.dma_start(tmask[:, :, :], io["seq_mask"]).then_inc(const_in, 16)
            V = prompt_sets[0]
            sp.wait_ge(V.sem, V.at("state1", TURNS - 1))
            sp.dma_start(io["wkv_new_prompt"], state[:, :, :]).then_inc(SO, 16)
            sp.wait_ge(S2, 2 * PR)
            sp.dma_start(io["wkv_new_sample"], s0[:, :, :, :]).then_inc(SO, 16)
            sp.wait_ge(SO, 32)

        @block.gpsimd
        def _(pool):
            def turn(c, V, A, G, E, slots, first, sample):
                for s in slots:
                    n = chunk_of(c, s, sample)
                    if not first:
                        last_turn(pool, 3, f"tok{s}", c, sample)
                        last_turn(pool, 0, f"state{s}", c, sample)
                    G.did(nc.gpsimd.tensor_copy(vs[s][:, :, :], sb.prc[:, V0:V0 + PR, bass.ds(1 + n * CH, CH)]), f"stage_v{s}")
                    G.did(nc.gpsimd.tensor_copy(end[s][:, :], sb.ends[:, bass.ds(n, 1), :].rearrange("p o i -> p (o i)")), f"stage_end{s}")
            turns(pool, turn)

        @block.scalar
        def _(act):
            def turn(c, V, A, G, E, slots, first, sample):
                at = lambda st, name: act.wait_ge(st.sem, st.at(name, c))
                for s in slots:
                    n = chunk_of(c, s, sample)
                    if not first:
                        last_turn(act, 3, f"state{s}", c, sample)
                        act.sem_inc(sb.passed, 1)
                    A.did(nc.scalar.activation(kr[s][:, :, 0, :], sb.kq[:, :, bass.ds(n * CH, CH)], ACT.Copy), f"stage_kq{s}")
                    A.did(nc.scalar.activation(kr[s][:, :, 1, :], sb.prc[:, R0:R0 + PR, bass.ds(1 + n * CH, CH)], ACT.Copy), f"stage_rq{s}")
                for s in slots:
                    at(E, f"tok{s}")
                    A.did(nc.scalar.activation(vk[s][:, :, :, :], B[2][:, 0:2 * PR * CH], ACT.Copy), f"vk{s}")
                    at(V, f"md{s}")
                    A.did(nc.scalar.activation(bt[s][:, :, :], pv(3), ACT.Copy), f"bt{s}")
                    at(E, f"p2{s}")
                    A.did(nc.scalar.activation(p2[s][:, :, :, :], B[ping(s)][:, 0:2 * PR * CH], ACT.Copy), f"p2{s}")
                for s in slots:
                    at(E, f"p4{s}")
                    A.did(nc.scalar.activation(p4[s][:, :, :, :], B[pong(s)][:, 0:2 * PR * CH], ACT.Copy), f"p4{s}")
                for s in slots:
                    at(E, f"tdt{s}")
                    A.did(nc.scalar.activation(tdt[s][:, :, :], pv(ping(s)), ACT.Copy), f"tdt{s}")
                for s in slots:
                    at(E, f"zt{s}")
                    A.did(nc.scalar.activation(zt[s][:, :, :], pv(pong(s)), ACT.Copy), f"zt{s}")
                for s in slots:
                    n = chunk_of(c, s, sample)
                    at(E, f"w{s}")
                    if sample:
                        act.wait_ge(AB, 2 * PR + 1)
                        A.did(nc.scalar.activation(w[:, :, :], w0[:, :, :], ACT.Copy), f"w{s}")
                    else:
                        A.did(nc.scalar.activation(w[:, :, :], pv(0), ACT.Copy), f"w{s}")
                    at(E, f"u{s}")
                    A.did(nc.scalar.activation(nu[:, :, :], pv(1), ACT.Copy, scale=-1.0), f"nu{s}")
                    at(E, f"y{s}")
                    act.sem_inc(sb.passed, 1)
                    A.did(nc.scalar.activation(sb.prc[:, R0:R0 + PR, bass.ds(1 + n * CH, CH)], pv(2), ACT.Copy), f"y{s}")
            turns(act, turn)

        @block.vector
        def _(dve):
            def turn(c, V, A, G, E, slots, first, sample):
                at = lambda st, name: dve.wait_ge(st.sem, st.at(name, c))
                m = masks[:, int(sample), :, :, :]
                for s in slots:
                    n = chunk_of(c, s, sample)
                    if not first:
                        last_turn(dve, 3, f"tok{s}", c, sample)
                    V.did(nc.vector.tensor_copy(kh[s][:, :, :], sb.prc[:, K0:K0 + PR, bass.ds(1 + n * CH, CH)]), f"stage_k{s}")
                    V.did(nc.vector.tensor_copy(bh[s][:, :, :], sb.bh[:, :, bass.ds(n * CH, CH)]), f"stage_b{s}")
                for s in slots:
                    quad = lambda b: B[b][:, 0:2 * PR * CH].rearrange("p (i a c) -> p i a c", a=2, c=CH)
                    at(E, f"kk{s}")
                    nc.vector.tensor_tensor(na[s][:, :, 0, :], quad(0)[:, :, 0, :], m[:, 0, :, :], ALU.mult)
                    V.did(nc.vector.tensor_tensor(na[s][:, :, 1, :], quad(0)[:, :, 1, :], m[:, 1, :, :], ALU.mult), f"na{s}")
                    at(E, f"tok{s}")
                    V.did(nc.vector.tensor_tensor(xd[s][:, :, :], quad(1)[:, :, 0, :], m[:, 2, :, :], ALU.mult), f"xd{s}")
                    V.did(nc.vector.tensor_tensor(md[s][:, :, :], pv2(3), m[:, 4, :, :], ALU.mult), f"md{s}")
                    V.did(nc.vector.tensor_tensor(xl[s][:, :, :], quad(1)[:, :, 0, :], m[:, 3, :, :], ALU.mult), f"xl{s}")
                    V.did(nc.vector.tensor_tensor(arb[s][:, :, :], quad(1)[:, :, 1, :], m[:, 1, :, :], ALU.mult), f"arb{s}")
                for s in slots:
                    at(E, f"p8{s}")
                    for i in range(PR):
                        last = nc.vector.tensor_tensor(ra[s][:, i, :], pv(ping(s))[:, i, :], eye[:, :], ALU.add)
                    V.did(last, f"r1{s}")
                for name, bank, dst, base, needs, op in (
                        ("r2", pong, rb, ra, "r1", ALU.add), ("r3", ping, ra, rb, "r2", ALU.add), ("td", pong, td, ra, "r3", ALU.subtract),
                        ("q1", ping, rb, td, "td", ALU.subtract), ("q2", pong, ra, td, "q1", ALU.subtract), ("tt", ping, rb, td, "q2", ALU.subtract)):
                    for s in slots:
                        at(E, f"{name}{s}")
                        at(V, f"{needs}{s}")
                        V.did(nc.vector.tensor_tensor(dst[s][:, :, :], base[s][:, :, :], pv(bank(s)), op), f"{name}{s}")
                if sample:
                    for i in range(PR):
                        dve.wait_ge(AA, i + 1)
                        nc.vector.tensor_tensor(spread[:, :, :], B[(6, 7, 5)[i]][:, :].rearrange("p (b v) -> p b v", v=HD), tmask[:, :, :],
                                                ALU.mult).then_inc(AB, 1)
                        dve.wait_ge(AB, 2 * i + 1)
                        nc.vector.tensor_reduce(w0[:, i, :], spread[:, :, :].rearrange("p b v -> p v b"), AX.X, ALU.add).then_inc(AB, 1)
                        dve.wait_ge(AB, 2 * i + 2)
                    at(E, "w0")
                    nc.vector.tensor_tensor(w0[:, :, :], w0[:, :, :], pv(0), ALU.add).then_inc(AB, 1)
                    at(A, "nu0")
                    at(A, "vk0")
                    for i in range(PR):
                        if i:
                            dve.wait_ge(AA, PR + i)
                        for src, dst in ((vk[0][:, 0, i, :], values_by_seq), (nu[:, i, :], spread)):
                            nc.vector.tensor_tensor(dst[:, :, :], src.unsqueeze(1).to_broadcast([P, DB, HD]), tmask[:, :, :],
                                                    ALU.mult).then_inc(AB, 1)
                        dve.wait_ge(AA, PR + i + 1)
                        nc.vector.tensor_tensor(s0[:, i, :, :], s0[:, i, :, :], B[(6, 7, 5)[i]][:, :].rearrange("p (b v) -> p b v", v=HD),
                                                ALU.add).then_inc(S2, 1)
                        dve.wait_ge(S2, 2 * i + 1)
                        nc.vector.tensor_tensor(s0[:, i, :, :], s0[:, i, :, :],
                                                sb.ends[:, NCH:NCH + DB, i].unsqueeze(2).to_broadcast([P, DB, HD]), ALU.mult).then_inc(S2, 1)
                    return
                for s in slots:
                    at(G, f"stage_end{s}")
                    if s:
                        at(V, f"state{s - 1}")
                    elif not first:
                        last_turn(dve, 0, "state1", c, sample)
                    for i in range(PR):
                        last = nc.vector.tensor_scalar(state2[:, i, :], state[:, i, :], end[s][:, i:i + 1], None, ALU.mult)
                    V.did(last, f"keep_state{s}")
                    at(E, f"state{s}")
                    at(V, f"keep_state{s}")
                    for i in range(PR):
                        last = nc.vector.scalar_tensor_tensor(state[:, i, :], pv(3)[:, i, :], end[s][:, i:i + 1], state2[:, i, :], ALU.mult, ALU.add)
                    V.did(last, f"state{s}")
            nc.vector.memset(state[:, :, :], 0.0).then_inc(state_set, 1)
            dve.wait_ge(const_in, 64)
            dve.wait_ge(state_set, 1)
            turns(dve, turn)

        @block.tensor
        def _(pe):
            def mm(out, lhs, rhs, **kw):
                kw = dict(start=True, stop=True) | kw
                return nc.tensor.matmul(out, lhs, rhs, **kw)

            def turn(c, V, A, G, E, slots, first, sample):
                def at(st, name):
                    pe.wait_ge(st.sem, st.at(name, c))
                    pe.sem_inc(sb.passed, 1)

                def before(sets_, name):
                    last_turn(pe, sets_, name, c, sample)
                    pe.sem_inc(sb.passed, 1)

                def each(name, f):
                    for i, r in heads:
                        last = f(i, r)
                    E.did(last, name)
                b2 = lambda b, i, r: B[b][r, i * 2 * CH:(i + 1) * 2 * CH]
                for s in slots:
                    at(A, f"stage_rq{s}")
                    at(V, f"stage_b{s}")
                    if s:
                        at(V, "arb0")
                        at(A, "bt0")
                    elif not first:
                        before(0, "state1")
                        before(1, "y1")
                    each(f"kk{s}", lambda i, r: mm(b2(0, i, r), kh[s][r, i, :], kr[s][r, i, :, :]))
                    each(f"bb{s}", lambda i, r: mm(b2(1, i, r), bh[s][r, i, :], kr[s][r, i, :, :]))
                    at(G, f"stage_v{s}")
                    for i, r in heads:
                        mm(pv(2)[r, i, :], vs[s][r, i, :], eye[r, :])
                        mm(pv2(2)[r, i, :], kh[s][r, i, :], eye[r, :])
                        mm(pv(3)[r, i, :], bh[s][r, i, :], eye[r, :])
                        last = mm(pv2(3)[r, i, :], kr[s][r, i, 0, :], bh[s][r, i, :])
                    E.did(last, f"tok{s}")
                    at(V, f"md{s}")
                    for i, r in heads:
                        mm(pv(ping(s))[r, i, :], md[s][r, i, :], xd[s][r, i, :])
                        last = mm(pv2(ping(s))[r, i, :], xd[s][r, i, :], md[s][r, i, :])
                    E.did(last, f"p2{s}")
                for s in slots:
                    at(A, f"p2{s}")
                    for i, r in heads:
                        mm(pv(pong(s))[r, i, :], p2[s][r, 1, i, :], p2[s][r, 0, i, :])
                        last = mm(pv2(pong(s))[r, i, :], p2[s][r, 0, i, :], p2[s][r, 1, i, :])
                    E.did(last, f"p4{s}")
                side = lambda buf: lambda s, r, i: buf[s][r, i, :]
                half = lambda buf: lambda s, r, i: buf[s][r, 1, i, :]
                eyes = lambda s, r, i: eye[r, :]
                for name, bank, lhs, rhs, eng, needs in (
                        ("p8", ping, half(p4), lambda s, r, i: p4[s][r, 0, i, :], A, "p4"),
                        ("r2", pong, half(p4), side(ra), V, "r1"), ("r3", ping, half(p2), side(rb), V, "r2"),
                        ("td", pong, side(md), side(ra), V, "r3"), ("tdt", ping, side(td), eyes, V, "td"),
                        ("zt", pong, side(xl), side(tdt), A, "tdt"), ("q1", ping, side(zt), side(td), A, "zt"),
                        ("q2", pong, side(zt), side(rb), V, "q1"), ("tt", ping, side(zt), side(ra), V, "q2")):
                    for s in slots:
                        at(eng, f"{needs}{s}")
                        each(f"{name}{s}", lambda i, r: mm(pv(bank(s))[r, i, :], lhs(s, r, i), rhs(s, r, i)))
                if sample:
                    for i in range(PR):
                        if i == 2:
                            at(V, "q20")
                        for h in range(2):
                            r = slice(h * HD, (h + 1) * HD)
                            last = mm(B[(6, 7, 5)[i]][r, :], kr[0][r, i, 0, :], s0[r, i, :, :])
                        last.then_inc(AA, 1)
                for s in slots:
                    if sample:
                        each("w0", lambda i, r: mm(pv(0)[r, i, :], na[0][r, i, 0, :], vk[0][r, 0, i, :]))
                    else:
                        if s:
                            at(V, "state0")
                        else:
                            at(V, "arb1")
                            at(A, "bt1")
                        for i, r in heads:
                            mm(pv(0)[r, i, :], kr[s][r, i, 0, :], state[r, i, :], stop=False)
                            last = mm(pv(0)[r, i, :], na[s][r, i, 0, :], vk[s][r, 0, i, :], start=False)
                        E.did(last, f"w{s}")
                    at(V, f"tt{s}")
                    at(A, f"w{s}")
                    each(f"u{s}", lambda i, r: mm(pv(1)[r, i, :], rb[s][r, i, :], w[r, i, :]))
                    at(A, f"nu{s}")
                    if sample:
                        pe.wait_ge(AB, 2 * PR)
                    elif s:
                        at(A, "y0")
                    for i, r in heads:
                        mm(pv(2)[r, i, :], vk[s][r, 0, i, :], na[s][r, i, 1, :], stop=False, skip_group_check=sample)
                        last = mm(pv(2)[r, i, :], nu[r, i, :], arb[s][r, i, :], start=False, stop=sample, skip_group_check=sample)
                        if sample:
                            for b in range(DB):
                                q = slice(b * SW + 1, (b + 1) * SW)
                                last = mm(pv(2)[r, i, q], s0[r, i, b, :], kr[s][r, i, 1, q], start=False, skip_group_check=True)
                        else:
                            last = mm(pv(2)[r, i, :], state[r, i, :], kr[s][r, i, 1, :], start=False)
                    E.did(last, f"y{s}")
                    if sample:
                        for i in range(PR):
                            pe.wait_ge(AB, 2 * PR + 1 + 2 * (i + 1))
                            for h in range(2):
                                r = slice(h * HD, (h + 1) * HD)
                                mm(B[(6, 7, 5)[i]][r, :], vk[0][r, 1, i, :], values_by_seq[r, :, :], stop=False)
                                last = mm(B[(6, 7, 5)[i]][r, :], bt[0][r, i, :], spread[r, :, :], start=False)
                            last.then_inc(AA, 1)
                        return
                    for i, r in heads:
                        mm(pv(3)[r, i, :], vk[s][r, 1, i, :], vk[s][r, 0, i, :], stop=False)
                        last = mm(pv(3)[r, i, :], bt[s][r, i, :], nu[r, i, :], start=False)
                    E.did(last, f"state{s}")
            pe.wait_ge(const_in, 64)
            turns(pe, turn)


def finish_rwkv(nc, io, sb):
    with ExitStack() as ctx:
        t = lambda name, shape: ctx.enter_context(nc.sbuf_tensor(name, shape, F32))
        sem = lambda name: ctx.enter_context(nc.semaphore(name))
        R0, GA = 2 * CT, NT - 1
        pieces = [(0, 512), (512, 512), (1024, SC - 1024)]
        par = sb.rwkv_par
        g_up, rs, sq = t("g_up", [P, RH * HD]), t("gn_rstd", [P, SC]), t("gn_sq", [P, SC])
        m, g = t("head_mean", [P, P]), t("gate", [P, SC])
        b1 = [ctx.enter_context(nc.psum_tensor(f"gn_a{n}", [P, 512], F32)) for n in range(3)]
        b2 = [ctx.enter_context(nc.psum_tensor(f"gn_b{n}", [P, 512], F32)) for n in range(3)]
        const_in, sig, mset = sem("gn_const"), sem("gn_sig"), sem("gn_mset")
        V = Steps(sem("gn_dve"), ["centre", "recip", "norm", "affine", "bonus", "gated"])
        A = Steps(sem("gn_act"), ["gate", "sq", "root"])
        E = Steps(sem("gn_pe"), ["mean", "gate", "var"])
        block = ctx.enter_context(nc.Block())

        @block.sync
        def _(sp):
            sp.dma_start(g_up[:, :], io["g_up"]).then_inc(const_in, 16)
            sp.wait_ge(const_in, 16)

        @block.vector
        def _(dve):
            nc.vector.tensor_scalar(m[:, :], sb.head_sum[:, :], 1.0 / HD, None, ALU.mult).then_inc(mset, 1)
            for i in range(PR):
                y, bv = sb.prc[:, R0 + i, 1:PW], sb.prc[:, i, 1:PW]
                own = lambda name: dve.wait_ge(V.sem, V.at(name, i))
                dve.wait_ge(E.sem, E.at("mean", i))
                for n, (lo, size) in enumerate(pieces):
                    last = nc.vector.tensor_tensor(y[:, lo:lo + size], y[:, lo:lo + size], b1[n][:, 0:size], ALU.subtract)
                V.did(last, "centre")
                dve.wait_ge(A.sem, A.at("root", i))
                V.did(nc.vector.reciprocal(rs[:, :], rs[:, :]), "recip")
                own("recip")
                V.did(nc.vector.tensor_tensor(y, y, rs[:, :], ALU.mult), "norm")
                own("norm")
                V.did(nc.vector.tensor_scalar(y, y, par[:, i, 5:6], par[:, i, 6:7], ALU.mult, ALU.add), "affine")
                own("affine")
                V.did(nc.vector.tensor_tensor(y, y, bv, ALU.add), "bonus")
                own("bonus")
                nc.vector.tensor_tensor(sb.mix[:, CT + i, 0:SEQ], y[:, 0:SEQ], g[:, 0:SEQ], ALU.mult)
                seq = lambda x: x[:, SEQ:SEQ + DB * SW].rearrange("p (b s) -> p b s", s=SW)[:, :, 1:SW]
                V.did(nc.vector.tensor_tensor(sb.mix[:, CT + i, SEQ:T].rearrange("p (b s) -> p b s", s=DS), seq(y), seq(g),
                                              ALU.mult), "gated")

        @block.scalar
        def _(act):
            nc.scalar.activation(sb.prc[:, GA, 1:PW], sb.prc[:, GA, 1:PW], ACT.Sigmoid).then_inc(sig, 1)
            for i in range(PR):
                if i:
                    act.wait_ge(V.sem, V.at("gated", i - 1))
                act.wait_ge(E.sem, E.at("gate", i))
                for n, (lo, size) in enumerate(pieces):
                    last = nc.scalar.activation(g[:, lo:lo + size], b2[n][:, 0:size], ACT.Copy)
                A.did(last, "gate")
                act.wait_ge(V.sem, V.at("centre", i))
                A.did(nc.scalar.activation(sq[:, :], sb.prc[:, R0 + i, 1:PW], ACT.Square), "sq")
                act.wait_ge(E.sem, E.at("var", i))
                for n, (lo, size) in enumerate(pieces):
                    last = nc.scalar.activation(rs[:, lo:lo + size], b1[n][:, 0:size], ACT.Sqrt, bias=sb.eps[:, 2:3])
                A.did(last, "root")

        @block.tensor
        def _(pe):
            pe.wait_ge(mset, 1)
            for i in range(PR):
                y = sb.prc[:, R0 + i, 1:PW]
                if i:
                    pe.wait_ge(A.sem, A.at("root", i - 1))
                for n, (lo, size) in enumerate(pieces):
                    last = nc.tensor.matmul(b1[n][:, 0:size], m[:, :], y[:, lo:lo + size], start=True, stop=True)
                E.did(last, "mean")
                pe.wait_ge(const_in, 16)
                pe.wait_ge(sig, 1)
                for n, (lo, size) in enumerate(pieces):
                    last = nc.tensor.matmul(b2[n][:, 0:size], g_up[:, i * P:(i + 1) * P], sb.prc[:, GA, 1 + lo:1 + lo + size],
                                            start=True, stop=True)
                E.did(last, "gate")
                pe.wait_ge(A.sem, A.at("sq", i))
                for n, (lo, size) in enumerate(pieces):
                    last = nc.tensor.matmul(b1[n][:, 0:size], m[:, :], sq[:, lo:lo + size], start=True, stop=True)
                E.did(last, "var")


def attend_sample(nc, io, sb):
    NK = NPG + 1
    HQ = AH * DS
    with ExitStack() as ctx:
        t = lambda name, shape, dt=F32: ctx.enter_context(nc.sbuf_tensor(name, shape, dt))
        sem = lambda name: ctx.enter_context(nc.semaphore(name))
        kp, vp = t("k_pages", [P, 2, NPG, ATT]), t("v_pages", [P, 2, NPG, ATT])
        pages, row, k_rows, v_rows = t("pages", [P, DB * NPG], mybir.dt.int32), t("row", [P, 1]), t("s_k_rows", [P, 2, NPG], U32), t("s_v_rows", [P, 2, NPG], U32)
        kn, vn = t("k_own", [P, PA, P]), t("v_own", [P, ATT])
        kt, qd = t("k_turned", [P, 3, ATT]), t("q_diag", [P, 2, PA, 2, DS])
        bias, seen, cap = t("s_bias", [P, NK * HQ]), t("s_seen", [P, DB, HQ]), t("s_cap", [P, DB, HQ])
        tri, ones, ident = t("s_tri", [P, P]), t("s_ones", [P, P]), t("s_ident", [P, P])
        zb, w, suf, a = t("s_logit", [P, NK * HQ]), t("s_soft", [P, NK * HQ]), t("s_suffix", [P, NPG * HQ]), t("s_weight", [P, NK * HQ])
        turn = [ctx.enter_context(nc.psum_tensor(f"s_turn{n}", [P, 512], F32)) for n in range(3)]
        zp = [ctx.enter_context(nc.psum_tensor(f"s_z{n}", [P, 512], F32)) for n in range(2)]
        rp, op = (ctx.enter_context(nc.psum_tensor(n, [P, 512], F32)) for n in ("s_later", "s_out"))
        const_in, own_set = sem("s_const"), sem("s_own")
        k_in, v_in = [sem(f"s_k_in{n}") for n in range(2)], [sem(f"s_v_in{n}") for n in range(2)]
        k_rows_set, v_rows_set, q_set = sem("s_k_rows"), sem("s_v_rows"), sem("s_q")
        turned, z_done = sem("s_turned"), sem("s_z_done")
        kept = [sem("s_kept_dve"), sem("s_kept_act")]
        V = Steps(sem("s_dve"), ["logit", "min", "soft", "seen", "suf"] + [f"suf{n}" for n in range(NPG - 1)] + ["diff", "cap"])
        A = Steps(sem("s_act"), ["exp", "ln", "weight", "out"])
        E = Steps(sem("s_pe"), ["later", "out"])

        def sequences(eng, body):
            for s in range(2):
                body(s, 0, s)
            with eng.Fori(1, DB // 2 - 1) as i:
                for s in range(2):
                    body(2 * i + s, i, s)
            for s in range(2):
                body(DB - 2 + s, DB // 2 - 1, s)

        known = lambda b: isinstance(b, int)
        first = lambda b: known(b) and b == 0
        has_next = lambda b, n: not (known(b) and b + n >= DB)
        block = ctx.enter_context(nc.Block())

        @block.sync
        def _(sp):
            for dst, src in ((pages, "pages"), (row, "row"), (bias, "sample_bias"), (tri, "tri"), (ones, "ones"), (ident, "ident")):
                sp.dma_start(dst[:, :], io[src]).then_inc(const_in, 16)
            for dst, src in ((seen, "sample_seen"), (cap, "sample_cap")):
                sp.dma_start(dst[:, :, :], io[src]).then_inc(const_in, 16)
            sp.wait_ge(const_in, 128)

        @block.gpsimd
        def _(pool):
            def gather(dst, table, rows, s, arrive):
                pool.sem_inc(sb.passed, 1)
                for g in range(NPG):
                    pool.indirect_dma_start(out=dst[:, s, g, :], out_offset=None, in_=io[table],
                                            in_offset=bass.IndirectOffsetOnAxis(ap=rows[:, s, g:g + 1], axis=0)).then_inc(arrive[s], 16)
            for b in range(2):
                pool.wait_ge(k_rows_set, b + 1)
                gather(kp, "cache_k", k_rows, b, k_in)
            pool.wait_ge(v_rows_set, 1)
            gather(vp, "cache_v", v_rows, 0, v_in)

            def body(b, half, s):
                if has_next(b, 2):
                    pool.wait_ge(k_rows_set, b + 3)
                    pool.wait_ge(z_done, b + 1)
                    gather(kp, "cache_k", k_rows, s, k_in)
                if has_next(b, 1):
                    pool.wait_ge(v_rows_set, b + 2)
                    if not first(b):
                        pool.wait_ge(E.sem, E.at("out", b - 1))
                    gather(vp, "cache_v", v_rows, 1 - s, v_in)
            sequences(pool, body)

        @block.vector
        def _(dve):
            nc.vector.memset(kn[:, :, :], 0.0).then_inc(own_set, 1)
            nc.vector.memset(vn[:, :], 0.0).then_inc(own_set, 1)
            nc.vector.memset(qd[:, :, :, :, :], 0.0).then_inc(own_set, 1)
            dve.wait_ge(const_in, 128)

            def page_rows(rows, b, s, done):
                nc.vector.tensor_scalar(rows[:, s, :], pages[:, bass.ds(b * NPG, NPG)], float(PAGE), row[:, 0:1],
                                        ALU.mult, ALU.add).then_inc(done, 1)

            def queries(b, s):
                for h in range(2):
                    r = slice(h * HD, (h + 1) * HD)
                    last = nc.vector.tensor_copy(qd[r, s, :, h, :], sb.qk[r, 0:PA, bass.ds(SEQ + b * DS, DS)])
                last.then_inc(q_set, 1)

            def keep(b, gs):
                for g in gs:
                    dve.wait_ge(turned, b * NPG + g + 1)
                    nc.vector.tensor_copy(kt[:, g % 3, :], turn[g % 3][:, 0:ATT]).then_inc(kept[0], 1)

            page_rows(k_rows, 0, 0, k_rows_set)
            page_rows(k_rows, 1, 1, k_rows_set)
            page_rows(v_rows, 0, 0, v_rows_set)
            dve.wait_ge(own_set, 3)
            nc.vector.tensor_copy(kn[:, :, 0:NS], sb.qk[:, PA:2 * PA, SEQ:T]).then_inc(own_set, 1)
            nc.vector.tensor_copy(vn[0:NS, :], sb.vtok[0:NS, NBLK - 1, :]).then_inc(own_set, 1)
            queries(0, 0)
            keep(0, range(0, NPG, 2))

            def body(b, half, s):
                own = lambda name: dve.wait_ge(V.sem, V.at(name, b))
                if has_next(b, 2):
                    dve.wait_ge(k_in[s], 16 * NPG * (half + 1))
                    page_rows(k_rows, b + 2, s, k_rows_set)
                if has_next(b, 1):
                    if not first(b):
                        dve.wait_ge(v_in[1 - s], 16 * NPG * (half + s))
                    page_rows(v_rows, b + 1, 1 - s, v_rows_set)
                    if not first(b):
                        dve.wait_ge(z_done, b)
                    queries(b + 1, 1 - s)
                dve.wait_ge(z_done, b + 1)
                V.did(nc.vector.scalar_tensor_tensor(zb[:, :], zp[s][:, 0:NK * HQ], HD ** -0.5, bias[:, :], ALU.mult, ALU.add), "logit")
                own("logit")
                V.did(nc.vector.tensor_scalar(w[:, :], zb[:, :], 40.0, None, ALU.min), "min")
                if has_next(b, 1):
                    keep(b + 1, range(0, NPG // 2, 2))
                dve.wait_ge(A.sem, A.at("ln", b))
                V.did(nc.vector.tensor_tensor(w[:, :], w[:, :], zb[:, :], ALU.max), "soft")
                own("soft")
                last_page = slice(NPG * HQ, NK * HQ)
                V.did(nc.vector.tensor_tensor(w[:, last_page], w[:, last_page], seen[:, bass.ds(b, 1), :].rearrange("p o q -> p (o q)"),
                                              ALU.mult), "seen")
                own("seen")
                V.did(nc.vector.tensor_copy(suf[:, (NPG - 1) * HQ:], w[:, last_page]), "suf")
                own("suf")
                for n in range(NPG - 1):
                    g = NPG - 2 - n
                    V.did(nc.vector.tensor_tensor(suf[:, g * HQ:(g + 1) * HQ], suf[:, (g + 1) * HQ:(g + 2) * HQ],
                                                  w[:, (g + 1) * HQ:(g + 2) * HQ], ALU.add), f"suf{n}")
                    own(f"suf{n}")
                if has_next(b, 1):
                    keep(b + 1, range(NPG // 2, NPG, 2))
                dve.wait_ge(E.sem, E.at("later", b))
                if not first(b):
                    dve.wait_ge(E.sem, E.at("out", b - 1))
                V.did(nc.vector.tensor_tensor(a[:, :], zb[:, :], rp[:, 0:NK * HQ], ALU.subtract), "diff")
                own("diff")
                V.did(nc.vector.tensor_tensor(a[:, last_page], a[:, last_page], cap[:, bass.ds(b, 1), :].rearrange("p o q -> p (o q)"),
                                              ALU.min), "cap")
            sequences(dve, body)

        @block.scalar
        def _(act):
            nc.scalar.preload_act_table_set("natural_log_exp_and_others")

            def keep(b):
                for g in range(1, NPG, 2):
                    act.wait_ge(turned, b * NPG + g + 1)
                    nc.scalar.activation(kt[:, g % 3, :], turn[g % 3][:, 0:ATT], ACT.Copy).then_inc(kept[1], 1)
            keep(0)

            def body(b, half, s):
                act.wait_ge(V.sem, V.at("min", b))
                A.did(nc.scalar.activation(w[:, :], w[:, :], ACT.Exp), "exp")
                act.wait_ge(A.sem, A.at("exp", b))
                A.did(nc.scalar.activation(w[:, :], w[:, :], ACT.Ln, bias=1.0), "ln")
                if has_next(b, 1):
                    keep(b + 1)
                act.wait_ge(V.sem, V.at("cap", b))
                A.did(nc.scalar.activation(a[:, :], a[:, :], ACT.Exp), "weight")
                act.wait_ge(E.sem, E.at("out", b))
                act.sem_inc(sb.passed, 1)
                for h in range(2):
                    r = slice(h * HD, (h + 1) * HD)
                    last = nc.scalar.activation(sb.mix[r, DC - PA:DC, bass.ds(SEQ + b * DS, DS)],
                                                op[r, 0:HQ].rearrange("p (i h q) -> p i h q", h=2, q=DS)[:, :, h, :], ACT.Copy)
                A.did(last, "out")
            sequences(act, body)

        @block.tensor
        def _(pe):
            def scores(b, half, s):
                pe.wait_ge(k_in[s], 16 * NPG * (half + 1))
                pe.wait_ge(q_set, b + 1)
                for g in range(NK):
                    if g < NPG:
                        if g >= 3:
                            pe.wait_ge(kept[(g - 3) % 2], b * (NPG // 2) + (g - 3) // 2 + 1)
                        for j in range(PA):
                            last = nc.tensor.transpose(turn[g % 3][:, j * P:(j + 1) * P], kp[:, s, g, j * P:(j + 1) * P], ident[:, :])
                        last.then_inc(turned, 1)
                    if g:
                        pe.wait_ge(kept[(g - 1) % 2], b * (NPG // 2) + (g - 1) // 2 + 1)
                        for j in range(PA):
                            nc.tensor.matmul(zp[s][:, (g - 1) * HQ + j * 2 * DS:(g - 1) * HQ + (j + 1) * 2 * DS],
                                             kt[:, (g - 1) % 3, j * P:(j + 1) * P], qd[:, s, j, :, :], start=True, stop=True)
                for j in range(PA):
                    last = nc.tensor.matmul(zp[s][:, NPG * HQ + j * 2 * DS:NPG * HQ + (j + 1) * 2 * DS],
                                            kn[:, j, :], qd[:, s, j, :, :], start=True, stop=True)
                last.then_inc(z_done, 1)

            pe.wait_ge(const_in, 128)
            pe.wait_ge(own_set, 5)
            scores(0, 0, 0)

            def body(b, half, s):
                if has_next(b, 1):
                    scores(b + 1, half + s, 1 - s)
                pe.wait_ge(V.sem, V.at(f"suf{NPG - 2}", b))
                nc.tensor.matmul(rp[:, 0:NK * HQ], tri[:, :], w[:, :], start=True, stop=False, skip_group_check=True)
                E.did(nc.tensor.matmul(rp[:, 0:NPG * HQ], ones[:, :], suf[:, :], start=False, stop=True, skip_group_check=True), "later")
                pe.wait_ge(A.sem, A.at("weight", b))
                pe.wait_ge(v_in[s], 16 * NPG * (half + 1))
                if not first(b):
                    pe.wait_ge(A.sem, A.at("out", b - 1))
                for j in range(PA):
                    for g in range(NK):
                        lhs = vn[:, j * P:(j + 1) * P] if g == NPG else vp[:, s, g, j * P:(j + 1) * P]
                        last = nc.tensor.matmul(op[:, j * 2 * DS:(j + 1) * 2 * DS], lhs,
                                                a[:, g * HQ + j * 2 * DS:g * HQ + (j + 1) * 2 * DS], start=g == 0, stop=g == NK - 1)
                E.did(last, "out")
            sequences(pe, body)


def close_mixer(nc, io, sb):
    with ExitStack() as ctx:
        t = lambda name, shape: ctx.enter_context(nc.sbuf_tensor(name, shape, F32))
        sem = lambda name: ctx.enter_context(nc.semaphore(name))
        wo, x, h2, h2t = t("w_out", [P, DC, D]), t("x_rows", [P, 2, D]), t("h2_rows", [P, 2, D]), t("h2_turned", [P, 2, DC, P])
        g2, junk, ident = t("g2", [P, D]), t("close_junk", [P, D]), t("close_ident", [P, P])
        ssq, rstd = t("ssq", [P, 2]), t("close_rstd", [P, 2])
        Y = [[ctx.enter_context(nc.psum_tensor(f"close_y{s}{n}", [P, 512], F32)) for n in range(2)] for s in range(2)]
        TR = [[ctx.enter_context(nc.psum_tensor(f"close_t{s}{n}", [P, 512], F32)) for n in range(2)] for s in range(2)]
        const_in, pad_set = sem("cl_const"), sem("cl_pad")
        x_in = [sem(f"cl_x_in{s}") for s in range(2)]
        x_out = [sem(f"cl_out{s}") for s in range(2)]
        V = Steps(sem("cl_dve"), ["x0", "x1", "recip", "h2"])
        A = Steps(sem("cl_act"), ["ssq", "root", "t0", "t1"])
        E, ET = Steps(sem("cl_pe"), ["y"]), Steps(sem("cl_turned"), ["turn"])
        block = ctx.enter_context(nc.Block())

        @block.sync
        def _(sp):
            for c in range(DC):
                sp.dma_start(wo[:, c, :], io["w_out"][:, c, :]).then_inc(const_in, 16)
            sp.dma_start(g2[:, :], io["norm2_g"]).then_inc(const_in, 16)
            sp.dma_start(ident[:, :], io["ident"]).then_inc(const_in, 16)
            for b in range(NBLK + 1):
                if b < NBLK:
                    s = b % 2
                    if b >= 2:
                        sp.wait_ge(x_out[s], 48 * (b // 2))
                    sp.dma_start(x[:, s, :], io["x_rows"][b]).then_inc(x_in[s], 16)
                if b:
                    s = (b - 1) % 2
                    sp.wait_ge(V.sem, V.at("h2", b - 1))
                    sp.dma_start(io["x1"][b - 1], x[:, s, :]).then_inc(x_out[s], 16)
                    sp.dma_start(io["h2"][b - 1], h2[:, s, :]).then_inc(x_out[s], 16)
                    sp.wait_ge(A.sem, A.at("t1", b - 1))
                    sp.dma_start(io["h2t"][b - 1], h2t[:, s, :, :]).then_inc(x_out[s], 16)
            sp.wait_ge(x_out[0], 48 * ((NBLK + 1) // 2))
            sp.wait_ge(x_out[1], 48 * (NBLK // 2))

        @block.vector
        def _(dve):
            for g in range(1, P // NS):
                nc.vector.tensor_copy(sb.mix[:, :, SEQ + g * NS:SEQ + (g + 1) * NS], sb.mix[:, :, SEQ:T]).then_inc(pad_set, 1)
            dve.wait_ge(const_in, 16 * (DC + 2))
            for b in range(NBLK):
                s = b % 2
                dve.wait_ge(x_in[s], 16 * (b // 2 + 1))
                dve.wait_ge(E.sem, E.at("y", b))
                for n in range(2):
                    V.did(nc.vector.tensor_tensor(x[:, s, n * 512:(n + 1) * 512], x[:, s, n * 512:(n + 1) * 512], Y[s][n][:, :], ALU.add), f"x{n}")
                dve.wait_ge(A.sem, A.at("root", b))
                V.did(nc.vector.reciprocal(rstd[:, s:s + 1], rstd[:, s:s + 1]), "recip")
                dve.wait_ge(V.sem, V.at("recip", b))
                if b >= 2:
                    dve.wait_ge(x_out[s], 48 * (b // 2))
                V.did(nc.vector.scalar_tensor_tensor(h2[:, s, :], x[:, s, :], rstd[:, s:s + 1], g2[:, :], ALU.mult, ALU.mult), "h2")

        @block.scalar
        def _(act):
            for b in range(NBLK):
                s = b % 2
                act.wait_ge(V.sem, V.at("x1", b))
                A.did(nc.scalar.activation(junk[:, :], x[:, s, :], ACT.Square, accum_out=ssq[:, s:s + 1]), "ssq")
                act.wait_ge(A.sem, A.at("ssq", b))
                A.did(nc.scalar.activation(rstd[:, s:s + 1], ssq[:, s:s + 1], ACT.Sqrt, bias=sb.eps[:, 0:1], scale=1.0 / D), "root")
                act.wait_ge(ET.sem, ET.at("turn", b))
                for n in range(2):
                    A.did(nc.scalar.activation(h2t[:, s, 4 * n:4 * n + 4, :], TR[s][n][:, :], ACT.Copy), f"t{n}")

        @block.tensor
        def _(pe):
            pe.wait_ge(const_in, 16 * (DC + 2))
            pe.wait_ge(pad_set, P // NS - 1)

            def turn(b):
                s = b % 2
                pe.wait_ge(V.sem, V.at("h2", b))
                if b >= 2:
                    pe.wait_ge(A.sem, A.at("t1", b - 2))
                    pe.wait_ge(x_out[s], 48 * (b // 2))
                for c in range(DC):
                    last = nc.tensor.transpose(TR[s][c // 4][:, c % 4 * P:(c % 4 + 1) * P], h2[:, s, c * P:(c + 1) * P], ident[:, :])
                ET.did(last, "turn")

            for b in range(NBLK):
                s = b % 2
                if b >= 2:
                    pe.wait_ge(V.sem, V.at("x1", b - 2))
                for n in range(2):
                    for c in range(DC):
                        last = nc.tensor.matmul(Y[s][n][:, :], sb.mix[:, c, b * P:(b + 1) * P], wo[:, c, n * 512:(n + 1) * 512],
                                                start=c == 0, stop=c == DC - 1)
                E.did(last, "y")
                if b:
                    turn(b - 1)
            turn(NBLK - 1)


def peer(nc, io, sb):
    RING = 8
    BH = PH * TOPK
    HN = 2 * KEYS
    LOW = -3.0e38
    LEAD = 2
    with ExitStack() as ctx:
        t = lambda name, shape, dt=F32: ctx.enter_context(nc.sbuf_tensor(name, shape, dt))
        sem = lambda name: ctx.enter_context(nc.semaphore(name))
        wk = t("wk", [P, DC, PH * HN])
        u, v = t("u_rows", [P, RING, D]), t("v_rows", [P, RING, D])
        h2, h2t, x1 = t("p_h2", [P, 2, D]), t("p_h2t", [P, 2, DC, P]), t("p_x1", [P, 2, D])
        gf, ident, iota = t("final_g", [P, D]), t("p_ident", [P, P]), t("iota", [P, TOPK])
        ident4 = t("ident_groups", [P, NS])
        sc, work = t("scores", [P, 2, 2, KEYS]), t("scores_left", [P, KEYS])
        best, where, wheref = t("best", [P, 2, TOPK]), t("where", [P, 2, TOPK], U32), t("where_f", [P, 2, TOPK])
        cand, left = t("cand", [P, TOPK, TOPK]), t("cand_left", [P, TOPK * TOPK])
        top, pos = t("top", [P, TOPK]), t("pos", [P, TOPK], U32)
        part, partf = t("pos_part", [P, 2, TOPK], U32), t("pos_part_f", [P, 2, TOPK])
        same, pick = t("same", [P, TOPK, TOPK]), t("pick", [P, 2, TOPK])
        expert, gate = t("expert", [P, 2, PH, TOPK], U32), t("p_gate", [P, 2, PH, TOPK])
        neg, expo, esum = t("neg_max", [P, 1]), t("exp_top", [P, TOPK]), t("exp_sum", [P, 1])
        hid, gel, wgt = t("hidden", [P, 2, TOPK]), t("gelu", [P, 2, TOPK]), t("weights", [P, 2, TOPK])
        diag = t("diag", [P, RING, P])
        eps_set = sem("p_eps_set")
        act_junk = t("p_act_junk", [P, D])
        ssq, rstd = t("p_ssq", [P, 1]), t("p_rstd", [P, 1])
        ps = lambda name: ctx.enter_context(nc.psum_tensor(name, [P, 512], F32))
        Y = [[ps(f"peer_y{s}{n}") for n in range(2)] for s in range(2)]
        S = [ps(f"peer_s{n}") for n in range(2)]
        WK = [ps(f"peer_k{n}") for n in range(2)] + Y[1]
        const_in, key_in, wq_in = sem("p_const"), sem("p_key_in"), [sem(f"p_wq_in{n}") for n in range(2)]
        wk_done, wk_kept = sem("wk_done"), sem("wk_kept")
        u_in, v_in = [sem(f"u_in{n}") for n in range(RING)], [sem(f"v_in{n}") for n in range(RING)]
        u_free, v_free = sem("u_free"), sem("v_free")
        h2_in, h2t_in, x1_in = ([sem(f"{n}_{s}") for s in range(2)] for n in ("p_h2_in", "p_h2t_in", "p_x1_in"))
        gelu_done, weights_done, diag_done = sem("gelu_done"), sem("weights_done"), sem("diag_done")
        score_done, score_kept, exps_done = sem("score_done"), sem("score_kept"), sem("exps_done")
        values_done, summed, y_ready, y_out = sem("values_done"), sem("p_summed"), sem("y_ready"), sem("y_out")
        C = Steps(sem("choice"), [n + str(side) for side in range(2) for n in ("max_a", "at_a", "left", "max_b", "at_b")]
                  + ["where_f", "cand", "top_a", "neg", "pos_a", "cand_left", "top_b", "pos_b", "first", "second", "parts_f"]
                  + [n + str(side) for side in range(2) for n in ("same", "marked", "pick")] + ["expert"])
        G = Steps(sem("gates"), ["recip", "gate"])
        F = Steps(sem("final_act"), ["ssq", "root"])
        R = Steps(sem("final_dve"), ["recip"])

        GR = P // NS

        def blocks(eng, body):
            body(0, 0, 0, P, TOPK)
            with eng.Fori(0, (NBLK - 3) // 2) as i:
                body(2 * i + 1, i, 1, P, TOPK)
                body(2 * i + 2, i + 1, 0, P, TOPK)
            body(NBLK - 2, (NBLK - 2) // 2, 1, P, TOPK)
            body(NBLK - 1, (NBLK - 1) // 2, 0, NS, TOPK // GR)

        def ahead(b, s, h, by):
            if h + by < PH:
                return b, s, h + by
            return (None, None, None) if last(b) else (b + 1, 1 - s, h + by - PH)

        def groups(b):
            if last(b):
                return [(slice(g * NS, (g + 1) * NS), slice(g, TOPK, GR), slice(0, TOPK // GR)) for g in range(GR)]
            return [(slice(0, P), slice(0, TOPK), slice(0, TOPK))]

        first = lambda b: isinstance(b, int) and b == 0
        last = lambda b: isinstance(b, int) and b == NBLK - 1
        pair = lambda ap: ap.rearrange("p a n -> p (a n)")
        block = ctx.enter_context(nc.Block())
        WQ = 4
        wq = [u[:, n * WQ:(n + 1) * WQ, :] for n in range(2)]
        keys = pair(v[:, 0:2, :]).rearrange("p (h n) -> p h n", n=KEYS)

        @block.sync
        def _(sp):
            sp.dma_start(keys, io["sub_keys"]).then_inc(key_in, 16)
            for g in range(2 * PH // WQ):
                if g >= 2:
                    sp.wait_ge(wk_done, 2 * WQ * (g - 1))
                sp.dma_start(wq[g % 2], io["w_query"][g * WQ:(g + 1) * WQ].rearrange("h p n -> p h n")).then_inc(wq_in[g % 2], 16)
            sp.dma_start(gf[:, :], io["final_g"]).then_inc(const_in, 16)
            sp.dma_start(ident[:, :], io["ident"]).then_inc(const_in, 16)
            sp.dma_start(iota[:, :], io["iota"]).then_inc(const_in, 16)
            sp.dma_start(ident4[:, :], io["ident_groups"]).then_inc(const_in, 16)
            sp.dma_start(h2t[:, 0, :, :], io["h2t"][0]).then_inc(h2t_in[0], 16)
            sp.dma_start(h2[:, 0, :], io["h2"][0]).then_inc(h2_in[0], 16)
            sp.dma_start(x1[:, 0, :], io["x1"][0]).then_inc(x1_in[0], 16)

            def body(b, half, s, n, K):
                o = 1 - s
                row = lambda name, x: io[name][bass.ds(x, 1)]
                if not last(b):
                    if not first(b):
                        sp.wait_ge(score_done, PH * b)
                    sp.dma_start(h2t[:, o, :, :], row("h2t", b + 1).rearrange("o p c n -> p (o c) n")).then_inc(h2t_in[o], 16)
                    if not first(b):
                        sp.wait_ge(u_free, RING + BH * b)
                    sp.dma_start(h2[:, o, :], row("h2", b + 1).rearrange("o p n -> p (o n)")).then_inc(h2_in[o], 16)
                if not first(b):
                    sp.wait_ge(y_ready, b)
                    sp.dma_start(row("y", b - 1).rearrange("o p n -> p (o n)"), x1[:, o, :]).then_inc(y_out, 16)
                    sp.wait_ge(y_out, 16 * b)
                if not last(b):
                    sp.dma_start(x1[:, o, :], row("x1", b + 1).rearrange("o p n -> p (o n)")).then_inc(x1_in[o], 16)
            blocks(sp, body)
            sp.wait_ge(y_ready, NBLK)
            sp.dma_start(io["y"][NBLK - 1, 0:NS, :], x1[0:NS, 0, :]).then_inc(y_out, 16)
            sp.wait_ge(y_out, 16 * NBLK)

        @block.gpsimd
        def _(pool):
            def body(b, half, s, n, K):
                for h in range(PH):
                    pool.wait_ge(C.sem, C.at("expert", b * PH + h))
                    for rows, table, free, arrived in ((u, "peer_u", u_free, u_in), (v, "peer_v", v_free, v_in)):
                        for m in range(h * K, (h + 1) * K):
                            pool.wait_ge(free, b * BH + m + 1)
                            pool.sem_inc(sb.passed, 1)
                            pool.indirect_dma_start(out=rows[:, m % RING, :], out_offset=None, in_=io[table],
                                                    in_offset=bass.IndirectOffsetOnAxis(ap=expert[:, s, h, m % K:m % K + 1], axis=0))\
                                .then_inc(arrived[m % RING], 16)
            blocks(pool, body)

        @block.vector
        def _(dve):
            def choose(b, s, h):
                turn = b * PH + h

                def step(name, ins):
                    C.did(ins, name)
                    dve.wait_ge(C.sem, C.at(name, turn))
                    dve.sem_inc(sb.passed, 1)
                dve.wait_ge(score_kept, turn + 1)
                dve.sem_inc(sb.passed, 1)
                lo, hi = slice(0, 8), slice(8, TOPK)
                for side in range(2):
                    x, n = sc[:, h % 2, side, :], str(side)
                    step("max_a" + n, nc.vector.max(best[:, side, lo], x))
                    step("at_a" + n, nc.vector.max_index(where[:, side, lo], best[:, side, lo], x))
                    step("left" + n, nc.vector.match_replace(work[:, :], best[:, side, lo], x, LOW))
                    step("max_b" + n, nc.vector.max(best[:, side, hi], work[:, :]))
                    step("at_b" + n, nc.vector.max_index(where[:, side, hi], best[:, side, hi], work[:, :]))
                step("where_f", nc.vector.tensor_copy(wheref[:, :, :], where[:, :, :]))
                grid = [P, TOPK, TOPK]
                step("cand", nc.vector.tensor_tensor(cand[:, :, :], best[:, 0, :].unsqueeze(2).to_broadcast(grid),
                                                     best[:, 1, :].unsqueeze(1).to_broadcast(grid), ALU.add))
                flat = pair(cand[:, :, :])
                step("top_a", nc.vector.max(top[:, lo], flat))
                step("neg", nc.vector.tensor_scalar(neg[:, :], top[:, 0:1], -1.0, None, ALU.mult))
                step("pos_a", nc.vector.max_index(pos[:, lo], top[:, lo], flat))
                step("cand_left", nc.vector.match_replace(left[:, :], top[:, lo], flat, LOW))
                step("top_b", nc.vector.max(top[:, hi], left[:, :]))
                step("pos_b", nc.vector.max_index(pos[:, hi], top[:, hi], left[:, :]))
                step("first", nc.vector.tensor_scalar(part[:, 0, :], pos[:, :], int(math.log2(TOPK)), None, ALU.logical_shift_right))
                step("second", nc.vector.tensor_scalar(part[:, 1, :], pos[:, :], TOPK - 1, None, ALU.bitwise_and))
                step("parts_f", nc.vector.tensor_copy(partf[:, :, :], part[:, :, :]))
                for side in range(2):
                    n = str(side)
                    step("same" + n, nc.vector.tensor_tensor(same[:, :, :], partf[:, side, :].unsqueeze(2).to_broadcast(grid),
                                                             iota[:, :].unsqueeze(1).to_broadcast(grid), ALU.is_equal))
                    step("marked" + n, nc.vector.tensor_tensor(same[:, :, :], same[:, :, :],
                                                               wheref[:, side, :].unsqueeze(1).to_broadcast(grid), ALU.mult))
                    step("pick" + n, nc.vector.tensor_reduce(pick[:, side, :], same[:, :, :], AX.X, ALU.add))
                for r, mine, kept in groups(b):
                    ins = nc.vector.scalar_tensor_tensor(expert[r, s, h, kept], pick[r, 0, mine], float(KEYS), pick[r, 1, mine],
                                                         ALU.mult, ALU.add)
                step("expert", ins)

            def gates(b, s, h):
                turn = b * PH + h
                dve.wait_ge(exps_done, turn + 1)
                G.did(nc.vector.reciprocal(esum[:, :], esum[:, :]), "recip")
                dve.wait_ge(G.sem, G.at("recip", turn))
                for r, mine, kept in groups(b):
                    ins = nc.vector.tensor_scalar(gate[r, s, h, kept], expo[r, mine], esum[r, 0:1], None, ALU.mult)
                G.did(ins, "gate")

            def finish(b, half, s, n):
                dve.wait_ge(values_done, b + 1)
                dve.wait_ge(x1_in[s], 16 * (half + 1))
                for k in range(2):
                    ins = nc.vector.tensor_tensor(x1[0:n, s, k * 512:(k + 1) * 512], x1[0:n, s, k * 512:(k + 1) * 512],
                                                  Y[s][k][0:n, :], ALU.add)
                ins.then_inc(summed, 1)
                dve.wait_ge(F.sem, F.at("root", b))
                R.did(nc.vector.reciprocal(rstd[0:n, :], rstd[0:n, :]), "recip")
                dve.wait_ge(R.sem, R.at("recip", b))
                nc.vector.scalar_tensor_tensor(x1[0:n, s, :], x1[0:n, s, :], rstd[0:n, 0:1], gf[0:n, :], ALU.mult, ALU.mult)\
                    .then_inc(y_ready, 1)

            def body(b, half, s, n, K):
                o = 1 - s
                dve.wait_ge(h2_in[s], 16 * (half + 1))
                for h in range(PH):
                    turn = b * PH + h
                    if h >= 2 or not first(b):
                        dve.wait_ge(gelu_done, turn - 1)
                    for k in range(K):
                        m = h * K + k
                        dve.wait_ge(u_in[m % RING], 16 * (b * (BH // RING) + m // RING + 1))
                        nc.vector.tensor_tensor_reduce(out=u[:, m % RING, :], in0=u[:, m % RING, :], in1=h2[:, s, :], scale=1.0, scalar=0.0,
                                                       op0=ALU.mult, op1=ALU.add, accum_out=hid[:, h % 2, k:k + 1]).then_inc(u_free, 1)
                    near, far = ahead(b, s, h, 1), ahead(b, s, h, LEAD)
                    if near[2] is not None:
                        gates(*near)
                    dve.wait_ge(gelu_done, turn + 1)
                    if h >= 2 or not first(b):
                        dve.wait_ge(diag_done, b * BH + K * (h - 1) if h else b * BH - TOPK)
                    dve.wait_ge(G.sem, G.at("gate", b * PH + h))
                    nc.vector.tensor_tensor(wgt[:, h % 2, 0:K], gel[:, h % 2, 0:K], gate[:, s, h, 0:K], ALU.mult).then_inc(weights_done, 1)
                    if far[2] is not None:
                        if far[2] == 0 and not first(b):
                            dve.wait_ge(v_free, RING + BH * b)
                        choose(*far)
                    if h == 1 and not first(b):
                        finish(b - 1, half - 1 + s, o, P)

            nc.vector.memset(sb.eps[:, 0:1], RMS_EPS).then_inc(eps_set, 1)
            nc.vector.sem_inc(u_free, RING)
            nc.vector.sem_inc(summed, 2)
            dve.wait_ge(const_in, 64)
            choose(0, 0, 0)
            gates(0, 0, 0)
            choose(0, 0, 1)
            blocks(dve, body)
            finish(NBLK - 1, (NBLK - 1) // 2, 0, NS)

        @block.scalar
        def _(act):
            def keep(b, h):
                turn = b * PH + h
                act.wait_ge(score_done, turn + 1)
                if not (first(b) and h < 2):
                    act.wait_ge(C.sem, C.at("at_b1", turn - 2))
                nc.scalar.activation(sc[:, h % 2, :, :], S[h % 2][:, 0:HN], ACT.Copy).then_inc(score_kept, 1)

            def exps(b, h):
                turn = b * PH + h
                act.wait_ge(C.sem, C.at("top_b", turn))
                nc.scalar.activation(expo[:, :], top[:, :], ACT.Exp, bias=neg[:, 0:1], accum_out=esum[:, 0:1]).then_inc(exps_done, 1)

            def norm(b, s, n):
                act.wait_ge(summed, b + 3)
                F.did(nc.scalar.activation(act_junk[0:n, :], x1[0:n, s, :], ACT.Square, accum_out=ssq[0:n, 0:1]), "ssq")
                act.wait_ge(F.sem, F.at("ssq", b))
                F.did(nc.scalar.activation(rstd[0:n, :], ssq[0:n, :], ACT.Sqrt, bias=sb.eps[0:n, 0:1], scale=1.0 / D), "root")

            def body(b, half, s, n, K):
                for h in range(PH):
                    turn = b * PH + h
                    far = ahead(b, s, h, LEAD)
                    if far[2] is not None:
                        keep(far[0], far[2])
                    act.wait_ge(u_free, RING + b * BH + (h + 1) * K)
                    if h >= 2 or not first(b):
                        act.wait_ge(weights_done, turn - 1)
                    nc.scalar.activation(gel[:, h % 2, 0:K], hid[:, h % 2, 0:K], ACT.Gelu_apprx_tanh).then_inc(gelu_done, 1)
                    act.wait_ge(weights_done, turn + 1)
                    eye = ident4 if last(b) else ident
                    for k in range(K):
                        m = h * K + k
                        act.wait_ge(v_free, b * BH + m + 1)
                        nc.scalar.activation(diag[:, m % RING, 0:n], eye[:, 0:n], ACT.Copy, scale=wgt[:, h % 2, k:k + 1])\
                            .then_inc(diag_done, 1)
                    if far[2] is not None:
                        exps(far[0], far[2])
                    if h == 1 and not first(b):
                        norm(b - 1, 1 - s, P)

            for hc in range(2 * PH):
                for j in range(2):
                    act.wait_ge(wk_done, 2 * hc + j + 1)
                    nc.scalar.activation(wk[:, 4 * j:4 * j + 4, hc * P:(hc + 1) * P], WK[(2 * hc + j) % 4][:, :], ACT.Copy).then_inc(wk_kept, 1)
            act.wait_ge(const_in, 64)
            act.wait_ge(eps_set, 1)
            for h in range(LEAD):
                keep(0, h)
                exps(0, h)
            blocks(act, body)
            norm(NBLK - 1, 0, NS)

        @block.tensor
        def _(pe):
            def score(b, s, h):
                turn = b * PH + h
                if not (first(b) and h < 2):
                    pe.wait_ge(score_kept, turn - 1)
                for c in range(DC):
                    ins = nc.tensor.matmul(S[h % 2][:, 0:HN], h2t[:, s, c, :], wk[:, c, h * HN:(h + 1) * HN], start=c == 0, stop=c == DC - 1)
                ins.then_inc(score_done, 1)

            def body(b, half, s, n, K):
                o = 1 - s
                pe.wait_ge(summed, b + 1)
                for h in range(PH):
                    far = ahead(b, s, h, LEAD)
                    if far[2] is not None:
                        if far[2] == 0:
                            pe.wait_ge(h2t_in[o], 16 * (half + 1 + s))
                        score(*far)
                    for k in range(K):
                        m = h * K + k
                        pe.wait_ge(diag_done, b * BH + m + 1)
                        pe.wait_ge(v_in[m % RING], 16 * (b * (BH // RING) + m // RING + 1))
                        if n < P:
                            pe.sem_inc(sb.passed, 1)
                        for j in range(2):
                            ins = nc.tensor.matmul(Y[s][j][0:n, :], diag[:, m % RING, 0:n], v[:, m % RING, j * 512:(j + 1) * 512],
                                                   start=m == 0, stop=m == PH * K - 1)
                        ins.then_inc(v_free, 1)
                pe.wait_ge(v_free, RING + BH * b + PH * K)
                pe.sem_inc(values_done, 1)

            pe.wait_ge(key_in, 16)
            for hc in range(2 * PH):
                g = hc // WQ
                pe.wait_ge(wq_in[g % 2], 16 * (g // 2 + 1))
                for j in range(2):
                    if hc >= 2:
                        pe.wait_ge(wk_kept, 2 * hc + j - 3)
                    for c in range(4):
                        ins = nc.tensor.matmul(WK[(2 * hc + j) % 4][:, c * P:(c + 1) * P], wq[g % 2][:, hc % WQ, (4 * j + c) * P:(4 * j + c + 1) * P],
                                               keys[:, hc, :], start=True, stop=True)
                    ins.then_inc(wk_done, 1)
            pe.wait_ge(wk_kept, 4 * PH)
            pe.sem_inc(v_free, RING)
            pe.wait_ge(h2t_in[0], 16)
            for h in range(LEAD):
                score(0, 0, h)
            blocks(pe, body)


class Resident:
    pass


def build(nc, io):
    with ExitStack() as ctx:
        sb = Resident()
        sb.passed = ctx.enter_context(nc.semaphore("passed"))
        sb.mix = ctx.enter_context(nc.sbuf_tensor("mix", [P, DC, TP], F32))
        sb.eps = ctx.enter_context(nc.sbuf_tensor("eps", [P, 4], F32))
        with ExitStack() as mixer:
            sb.prc = mixer.enter_context(nc.sbuf_tensor("prc", [P, NT, PW], F32))
            with ExitStack() as att:
                sb.qk = att.enter_context(nc.sbuf_tensor("qk", [P, 2 * PA, T], F32))
                sb.vtok = att.enter_context(nc.sbuf_tensor("vtok", [P, NBLK, ATT], F32))
                project(nc, io, sb)
                attend_prompt(nc, io, sb)
                attend_sample(nc, io, sb)
            norm_convolution(nc, io, sb)
            with ExitStack() as rwkv:
                t = lambda name, shape: rwkv.enter_context(nc.sbuf_tensor(name, shape, F32))
                sb.kq, sb.bh = t("kq", [P, PR, SC]), t("bh", [P, PR, SC])
                sb.ends, sb.rwkv_par, sb.mu = t("ends", [P, NCH + DB, PR]), t("rwkv_par", [P, PR, 7]), t("mu", [P, RT])
                sb.head_sum = t("head_sum", [P, P])
                prepare_rwkv(nc, io, sb)
                scan_rwkv(nc, io, sb)
                finish_rwkv(nc, io, sb)
        close_mixer(nc, io, sb)
    with ExitStack() as ctx:
        sb.eps = ctx.enter_context(nc.sbuf_tensor("eps_peer", [P, 4], F32))
        peer(nc, io, sb)


def layout(given):
    dense = np.ascontiguousarray
    f4 = np.float32
    a = lambda name: np.asarray(given[name])
    chans = lambda arr, n: arr.reshape(n, P)
    everywhere = lambda arr: dense(np.broadcast_to(arr, (P,) + arr.shape))
    x = np.concatenate([a("x_prompt").reshape(SEQ, D), a("x_sample").reshape(NS, D)], 0)
    w_in = a("w_in")[0].reshape(DC, P, NT + 3 * PA, P)
    VT = NT + 2 * PA
    part = np.arange(P)
    out = {
        "xT": dense(x.T.reshape(DC, P, T).transpose(1, 0, 2)),
        "x_rows": np.concatenate([x[:SEQ]] + [x[SEQ:]] * (P // NS)).reshape(NBLK, P, D),
        "w_in": dense(w_in[:, :, :VT].transpose(2, 1, 0, 3)),
        "w_v": dense(a("w_in")[0][:, VT * P:].reshape(DC, P, ATT).transpose(1, 0, 2)),
        "norm1_g": dense(chans(a("norm1_g")[0], DC).T),
        "norm2_g": everywhere(a("norm2_g")[0]),
        "final_g": everywhere(a("final_g")),
        "w_out": dense(a("w_out")[0].reshape(DC, P, D).transpose(1, 0, 2)),
        "ones": np.ones((P, P), f4),
        "ident": np.eye(P, dtype=f4), "ident_groups": np.tile(np.eye(NS, dtype=f4), (P // NS, 1)),
    }

    bias = a("att_bias")[0]
    later = part[:, None] >= part[None, :]
    seen = part[:, None] < part[None, :]
    key_seq, key_at = part // DS, part % DS
    seen_new = (key_seq[:, None, None] == np.arange(DB)[None, :, None]) & \
        (key_at[:, None, None] < np.tile(np.arange(DS), AH)[None, None, :])
    out.update({
        "att_bias": everywhere(bias),
        "tri": later.astype(f4), "tri_rest": (~later).astype(f4),
        "att_seen": seen.astype(f4), "att_cap": np.where(seen, 0, -1e30).astype(f4),
        "sample_bias": everywhere(np.tile(np.repeat(bias, DS), NPG + 1)),
        "sample_seen": seen_new.astype(f4), "sample_cap": np.where(seen_new, 0, -1e30).astype(f4),
        "pages": everywhere(a("page_table").reshape(DB * NPG)),
        "row": np.arange(P, dtype=f4)[:, None].copy(),
        "cache_k": a("cache_k")[0].reshape(-1, ATT), "cache_v": a("cache_v")[0].reshape(-1, ATT),
    })

    conv = lambda name: chans(a(name)[0], CT)
    out.update({
        "conv_w": dense(a("conv_w")[0].T.reshape(CT, P, KW).transpose(1, 0, 2)),
        "conv_affine": dense(np.stack([conv("conv_b"), conv("conv_ln_g"), conv("conv_ln_b")], -1).transpose(1, 0, 2)),
        "state_conv": dense(a("state_conv")[0].transpose(2, 0, 1).reshape(CT, P, DB, KW - 1)),
    })

    par = [a("rwkv_" + name)[0].reshape(PR, P) for name in ("w0", "a0", "k_k", "k_a", "r_k", "ln_g", "ln_b")]
    keep = np.ones(SC, f4)
    keep[0:SEQ:CH] = 0
    keep[SEQ:SEQ + DB * SW:SW] = 0
    keep[SEQ + 1:SEQ + DB * SW:SW] = 0
    keep[SEQ + DB * SW] = 0
    s, t = np.arange(CH)[:, None], np.arange(CH)[None, :]
    near = s // 16 == t // 16
    real = lambda col: (col < DB * SW) & (col % SW != 0)
    same = (s // SW == t // SW) & real(s) & real(t)
    prompt = [s < t, s <= t, (s < t) & near, (s < t) & ~near, (s > t) & near]
    sample = [(s < t) & same, (s <= t) & same, (s < t) & same, np.zeros_like(same), (s > t) & same]
    masks = np.stack([np.stack(prompt), np.stack(sample)]).astype(f4)
    masks = np.tile(masks.transpose(2, 0, 1, 3), (2, 1, 1, 1))
    step = np.arange(CH)
    of_seq = ((step[:, None] // SW == np.arange(DB)[None, :]) & real(step)[:, None]).astype(f4)
    out.update({
        "rwkv_mu": dense(chans(a("rwkv_mu")[0], RT).T),
        "wa_up": dense(np.concatenate([a("rwkv_w_up")[0], a("rwkv_a_up")[0]], 0)),
        "g_up": dense(a("rwkv_g_up")[0]),
        "rwkv_par": dense(np.stack(par, -1).transpose(1, 0, 2)),
        "head_sum": (part[:, None] // HD == part[None, :] // HD).astype(f4),
        "scan_keep": everywhere(keep),
        "eye2": np.tile(np.eye(CH, dtype=f4), (2, 1)),
        "chunk_masks": dense(np.repeat(masks[:, :, :, None, :], PR, axis=3)),
        "seq_mask": dense(np.repeat(np.tile(of_seq, (2, 1))[:, :, None], HD, axis=2)),
        "state_shift": dense(a("state_shift")[0].T.reshape(RT, P, DB).transpose(1, 0, 2)),
        "state_wkv": dense(a("state_wkv")[0].transpose(1, 3, 0, 2).reshape(PR, P, DB, HD).transpose(1, 0, 2, 3)),
    })

    out.update({
        "sub_keys": dense(a("peer_sub_keys")[0].transpose(3, 0, 1, 2).reshape(P, 2 * PH, KEYS)),
        "w_query": dense(a("peer_w_query")[0].T.reshape(2 * PH, P, D)),
        "iota": everywhere(np.arange(TOPK, dtype=f4)),
        "peer_u": a("peer_u")[0], "peer_v": a("peer_v")[0],
    })
    return out


OUTPUTS = {
    "y": (NBLK, P, D), "k_new": (P, PA, T), "v_new": (T, ATT),
    "conv_new_prompt": (P, CT, KW - 1), "conv_new_sample": (CT, P, DB, KW - 1), "shift_new": (P, RT, 1 + DB),
    "wkv_new_prompt": (P, PR, HD), "wkv_new_sample": (P, PR, DB, HD),
}
SCRATCH = {"x1": (NBLK, P, D), "h2": (NBLK, P, D), "h2t": (NBLK, P, DC, P)}


def kernel(**inputs):
    import concourse.bacc as bacc
    from concourse.bass_utils import run_bass_kernel_spmd

    nc = bacc.Bacc("TRN2", target_bir_lowering=False, num_devices=1)
    arrays, io = {}, {}
    for name, arr in layout(inputs).items():
        arrays["in_" + name] = np.ascontiguousarray(arr)
        io[name] = nc.dram_tensor("in_" + name, arr.shape, mybir.dt.from_np(arr.dtype), kind="ExternalInput").ap()
    for name, shape in OUTPUTS.items():
        io[name] = nc.dram_tensor("out_" + name, shape, F32, kind="ExternalOutput").ap()
    for name, shape in SCRATCH.items():
        io[name] = nc.dram_tensor("scratch_" + name, shape, F32).ap()
    build(nc, io)
    got = run_bass_kernel_spmd(nc, [arrays], core_ids=[0]).results[0]

    out = lambda name: np.asarray(got["out_" + name])
    y = out("y").reshape(TP, D)
    k = out("k_new").transpose(1, 0, 2).reshape(ATT, T).T
    v = out("v_new")
    conv_p = out("conv_new_prompt").transpose(2, 1, 0).reshape(1, 1, KW - 1, CC)
    conv_s = out("conv_new_sample").transpose(2, 3, 0, 1).reshape(1, DB, KW - 1, CC)
    shift = out("shift_new").transpose(2, 1, 0).reshape(1, 1 + DB, RC)
    wkv_p = out("wkv_new_prompt").reshape(2, HD, PR, HD).transpose(2, 0, 3, 1).reshape(1, 1, RH, HD, HD)
    wkv_s = out("wkv_new_sample").reshape(2, HD, PR, DB, HD).transpose(3, 2, 0, 4, 1).reshape(1, DB, RH, HD, HD)
    prompt = lambda arr: arr[:SEQ].reshape(1, 1, SEQ, AH, HD)
    sample = lambda arr: arr[SEQ:T].reshape(1, DB, DS, AH, HD)
    return (y[:SEQ].reshape(1, SEQ, D), y[SEQ:T].reshape(DB, DS, D),
            prompt(k), prompt(v), conv_p, shift[:, :1], wkv_p,
            sample(k), sample(v), conv_s, shift[:, 1:], wkv_s)
```
